# Optimizing a Trainium2 kernel written in Bass

```python
import jax, jax.numpy as jnp
from jax import lax
import numpy as np

D_MODEL = 1024
BATCH = 1
SEQ = 128
DEPTH = 2
DEC_BATCH = 1
DEC_SEQ = 256
PAST_LEN = 128

GRID_W = 64
BLOCK_Q = 128
N_HEADS = 8
N_KV_HEADS = 2
HEAD_DIM = 64
Q_PER_KV = N_HEADS // N_KV_HEADS
ATTN_W = N_HEADS * HEAD_DIM
KV_W = N_KV_HEADS * HEAD_DIM
N_FREQ = HEAD_DIM // 4
ROPE_THETA = 10000.0
CHUNK = 128
SGU_GROUPS = 4
SGU_W = 512
SGU_GW = SGU_W // SGU_GROUPS
R_HEADS = 8
R_HEAD = 64
RW = R_HEADS * R_HEAD
LORA_W = 64
LORA_A = 64
LORA_G = 128
CONV_W = 3
DECAY_SCALE = 0.606531
GN_EPS = 64e-5
N_BRANCH = 3
N_EXPERTS = 64
TOP_K = 6
D_EXPERT = 128
D_SHARED = 256
ROUTED_SCALE = 2.5
EPS = 1e-6
IN_SIZES = (ATTN_W, KV_W, KV_W, SGU_W, SGU_W, 3 * RW, 2 * LORA_W, 2 * LORA_A, LORA_G, N_BRANCH * D_MODEL)
N_IN = ATTN_W + 2 * KV_W + 2 * SGU_W + 3 * RW + 2 * LORA_W + 2 * LORA_A + LORA_G + N_BRANCH * D_MODEL

kernel_name = 'hybrid_dit_prefix_ctx_step'

def rms_norm(x, g):
    xf = x.astype(jnp.float32)
    y = xf * lax.rsqrt(jnp.mean(xf * xf, axis=-1, keepdims=True) + EPS)
    return (y * g.astype(jnp.float32)).astype(x.dtype)

def split_cols(z, sizes):
    parts, off = [], 0
    for s in sizes:
        parts.append(z[..., off:off + s])
        off += s
    return parts

def axial_rope(n_tok):
    rows = n_tok // GRID_W
    t = jnp.arange(rows * GRID_W)
    row = (t // GRID_W).astype(jnp.float32)
    col = (t % GRID_W).astype(jnp.float32)
    inv = ROPE_THETA ** (-jnp.arange(N_FREQ, dtype=jnp.float32) / N_FREQ)
    ang = jnp.stack([row[:, None] * inv[None, :], col[:, None] * inv[None, :]], axis=1)
    return jnp.cos(ang), jnp.sin(ang)

def apply_rope(x, cos, sin):
    b, t, h, _ = x.shape
    xs = x.astype(jnp.float32).reshape(b, t, h, 2, 2, N_FREQ)
    x1, x2 = xs[..., 0, :], xs[..., 1, :]
    c, s = cos[None, :, None], sin[None, :, None]
    out = jnp.stack([x1 * c - x2 * s, x2 * c + x1 * s], axis=-2)
    return out.reshape(b, t, h, HEAD_DIM).astype(x.dtype)

def block_attention(q, k, v):
    b, t = q.shape[:2]
    nb = t // BLOCK_Q
    qb = jnp.moveaxis(q.reshape(b, nb, BLOCK_Q, N_KV_HEADS, Q_PER_KV, HEAD_DIM), 1, 0)
    scale = HEAD_DIM ** -0.5

    def one_block(qblk):
        s = jnp.einsum('bqkgd,bskd->bkgqs', qblk, k).astype(jnp.float32) * scale
        p = jax.nn.softmax(s, axis=-1).astype(v.dtype)
        return jnp.einsum('bkgqs,bskd->bqkgd', p, v)

    o = lax.map(one_block, qb)
    return jnp.moveaxis(o, 0, 1).reshape(b, t, ATTN_W)

def chunk_sgu(u, v, g, ws, bs):
    b, t, _ = v.shape
    vc = rms_norm(v, g).reshape(b, t // CHUNK, CHUNK, SGU_GROUPS, SGU_GW)
    mixed = jnp.einsum('gij,bnjgc->bnigc', ws, vc) + bs.T[None, None, :, :, None]
    return u * mixed.reshape(b, t, SGU_W)

def centred_conv(x, w):
    t = x.shape[1]
    pad = CONV_W // 2
    xp = jnp.pad(x, ((0, 0), (pad, pad), (0, 0)))
    return sum(xp[:, j:j + t] * w[j] for j in range(CONV_W))

def wkv_scan(s0, r, w, k, v, kk, a, reverse):
    def step(s, inp):
        r_t, w_t, k_t, v_t, kk_t, a_t = inp
        sa = jnp.einsum('bhij,bhj->bhi', s, -kk_t)
        s = s * w_t[:, :, None, :] + sa[..., None] * (kk_t * a_t)[:, :, None, :] + v_t[..., None] * k_t[:, :, None, :]
        return s, jnp.einsum('bhij,bhj->bhi', s, r_t)

    xs = tuple(jnp.moveaxis(z.astype(jnp.float32), 1, 0) for z in (r, w, k, v, kk, a))
    s_fin, o = lax.scan(step, s0.astype(jnp.float32), xs, reverse=reverse)
    return s_fin, jnp.moveaxis(o, 0, 1)

def moe(h, P, l):
    b, t, d = h.shape
    hf = h.reshape(b * t, d)
    scores = jax.nn.sigmoid(jnp.dot(hf, P['router_w'][l]).astype(jnp.float32))
    _, idx = lax.top_k(scores + P['router_bias'][l].astype(jnp.float32), TOP_K)
    sel = jnp.take_along_axis(scores, idx, axis=-1)
    wts = sel / jnp.sum(sel, axis=-1, keepdims=True) * ROUTED_SCALE
    combine = jnp.sum(jax.nn.one_hot(idx, N_EXPERTS, dtype=jnp.float32) * wts[..., None], axis=1).astype(h.dtype)
    hid = jax.nn.silu(jnp.einsum('nd,edf->nef', hf, P['exp_gate'][l])) * jnp.einsum('nd,edf->nef', hf, P['exp_up'][l])
    routed = jnp.einsum('nef,efd->nd', hid * combine[..., None], P['exp_down'][l])
    shared = jnp.dot(jax.nn.silu(jnp.dot(hf, P['sh_gate'][l])) * jnp.dot(hf, P['sh_up'][l]), P['sh_down'][l])
    return (routed + shared).reshape(b, t, d)

def trunk_layer(x, cvec, P, l, ctx=None, rope=None):
    b, t, _ = x.shape
    dt = x.dtype
    mod = jnp.dot(jax.nn.silu(cvec), P['mod_w'][l]) + P['mod_b'][l]
    sh1, sc1, gt1, sh2, sc2, gt2 = jnp.split(mod[:, None, :], 6, axis=-1)
    h = rms_norm(x, P['norm1_g'][l]) * (1 + sc1) + sh1
    z = jnp.dot(h, P['w_in'][l])
    q, k, v, su, sv, rkv, xw, xa, xg, gates = split_cols(z, IN_SIZES)

    q = rms_norm(q.reshape(b, t, N_HEADS, HEAD_DIM), P['q_norm'][l])
    k = rms_norm(k.reshape(b, t, N_KV_HEADS, HEAD_DIM), P['k_norm'][l])
    v = v.reshape(b, t, N_KV_HEADS, HEAD_DIM)
    if ctx is None:
        k_all, v_all = k, v
        s_init = (jnp.zeros((b, R_HEADS, R_HEAD, R_HEAD), jnp.float32),) * 2
    else:
        cos, sin = rope
        q = apply_rope(q, cos, sin)
        k_lat = apply_rope(k, cos, sin)
        k_all = jnp.concatenate([ctx[0].astype(dt), k_lat], axis=1)
        v_all = jnp.concatenate([ctx[1].astype(dt), v], axis=1)
        s_init = (ctx[2], ctx[3])
    o_attn = block_attention(q, k_all, v_all)

    o_sgu = chunk_sgu(su, sv, P['sgu_norm_g'][l], P['sgu_ws'][l], P['sgu_bs'][l])

    def heads(a_):
        return a_.reshape(b, t, R_HEADS, R_HEAD)

    rkv = centred_conv(rkv, P['rwkv_conv'][l])
    r, kr, vr = jnp.split(rkv, 3, axis=-1)
    r_h, v_h = heads(r), heads(vr)
    kk = heads(kr * P['rwkv_k_k'][l]).astype(jnp.float32)
    kk = kk * lax.rsqrt(jnp.sum(kk * kk, axis=-1, keepdims=True) + 1e-12)
    xw = xw.reshape(b, t, 2, LORA_W)
    xa = xa.reshape(b, t, 2, LORA_A)
    outs, bonuses, finals = [], [], []
    for d in range(2):
        w_d = jnp.exp(-DECAY_SCALE * jax.nn.sigmoid(P['rwkv_w0'][l, d] + jnp.dot(jnp.tanh(xw[:, :, d]), P['rwkv_w2'][l, d])))
        a_d = jax.nn.sigmoid(P['rwkv_a0'][l, d] + jnp.dot(xa[:, :, d], P['rwkv_a2'][l, d]))
        k_d = heads(kr * (1 + (a_d - 1) * P['rwkv_k_a'][l]))
        s_fin, o_d = wkv_scan(s_init[d], r_h, heads(w_d), k_d, v_h, kk, heads(a_d), reverse=(d == 1))
        outs.append(o_d)
        bonuses.append(jnp.sum(r_h * k_d * P['rwkv_r_k'][l], axis=-1, keepdims=True) * v_h)
        finals.append(s_fin)
    of = outs[0] + outs[1]
    mu = jnp.mean(of, axis=-1, keepdims=True)
    var = jnp.mean(jnp.square(of - mu), axis=-1, keepdims=True)
    on = ((of - mu) * lax.rsqrt(var + GN_EPS)).reshape(b, t, RW).astype(dt) * P['rwkv_ln_g'][l] + P['rwkv_ln_b'][l]
    g_out = jnp.dot(jax.nn.sigmoid(xg), P['rwkv_g2'][l])
    o_rwkv = (on + (bonuses[0] + bonuses[1]).reshape(b, t, RW)) * g_out

    g_a, g_s, g_r = jnp.split(jax.nn.sigmoid(gates), N_BRANCH, axis=-1)
    merged = (g_a * jnp.dot(o_attn, P['proj_attn'][l])
              + g_s * jnp.dot(o_sgu, P['proj_sgu'][l])
              + g_r * jnp.dot(o_rwkv, P['proj_rwkv'][l]))
    x = x + gt1 * jnp.dot(merged, P['w_out'][l])

    h2 = rms_norm(x, P['norm2_g'][l]) * (1 + sc2) + sh2
    x = x + gt2 * moe(h2, P, l)
    return x, (k, v, finals[0], finals[1])

def setup_inputs(seed: int = 0) -> dict:
    key = jax.random.key(seed)
    keys = iter(jax.random.split(key, 64))

    def nrm(shape, scale):
        return jax.random.normal(next(keys), shape, jnp.float32) * scale

    L, D = DEPTH, D_MODEL
    conv_base = jnp.array([0.25, 0.5, 0.25], jnp.float32)[None, :, None]
    return {
        'x_prompt': nrm((BATCH, SEQ, D), 1.0),
        'x_sample': nrm((DEC_BATCH, DEC_SEQ, D), 1.0),
        'cache_k': nrm((DEC_BATCH, L, PAST_LEN, N_KV_HEADS, HEAD_DIM), 1.0),
        'cache_v': nrm((DEC_BATCH, L, PAST_LEN, N_KV_HEADS, HEAD_DIM), 1.0),
        'state_wkv': nrm((DEC_BATCH, L, 2, R_HEADS, R_HEAD, R_HEAD), 0.3),
        'c': nrm((DEC_BATCH, D), 1.0),
        'c_ctx': nrm((D,), 1.0),
        'mod_w': nrm((L, D, 6 * D), 0.5 * D ** -0.5),
        'mod_b': nrm((L, 6 * D), 0.02),
        'norm1_g': 1.0 + nrm((L, D), 0.05),
        'norm2_g': 1.0 + nrm((L, D), 0.05),
        'w_in': nrm((L, D, N_IN), D ** -0.5),
        'q_norm': 1.0 + nrm((L, HEAD_DIM), 0.05),
        'k_norm': 1.0 + nrm((L, HEAD_DIM), 0.05),
        'sgu_norm_g': 1.0 + nrm((L, SGU_W), 0.05),
        'sgu_ws': nrm((L, SGU_GROUPS, CHUNK, CHUNK), CHUNK ** -0.5),
        'sgu_bs': 1.0 + nrm((L, SGU_GROUPS, CHUNK), 0.1),
        'rwkv_conv': conv_base + nrm((L, CONV_W, 3 * RW), 0.05),
        'rwkv_w0': nrm((L, 2, RW), 1.0),
        'rwkv_w2': nrm((L, 2, LORA_W, RW), LORA_W ** -0.5),
        'rwkv_a0': nrm((L, 2, RW), 0.5),
        'rwkv_a2': nrm((L, 2, LORA_A, RW), LORA_A ** -0.5),
        'rwkv_g2': nrm((L, LORA_G, RW), LORA_G ** -0.5),
        'rwkv_k_k': 0.85 + nrm((L, RW), 0.05),
        'rwkv_k_a': 1.0 + nrm((L, RW), 0.05),
        'rwkv_r_k': nrm((L, R_HEADS, R_HEAD), 0.1),
        'rwkv_ln_g': 1.0 + nrm((L, RW), 0.05),
        'rwkv_ln_b': nrm((L, RW), 0.02),
        'proj_attn': nrm((L, ATTN_W, D), ATTN_W ** -0.5),
        'proj_sgu': nrm((L, SGU_W, D), SGU_W ** -0.5),
        'proj_rwkv': nrm((L, RW, D), RW ** -0.5),
        'w_out': nrm((L, D, D), D ** -0.5),
        'router_w': nrm((L, D, N_EXPERTS), D ** -0.5),
        'router_bias': nrm((L, N_EXPERTS), 0.01),
        'exp_gate': nrm((L, N_EXPERTS, D, D_EXPERT), D ** -0.5),
        'exp_up': nrm((L, N_EXPERTS, D, D_EXPERT), D ** -0.5),
        'exp_down': nrm((L, N_EXPERTS, D_EXPERT, D), D_EXPERT ** -0.5),
        'sh_gate': nrm((L, D, D_SHARED), D ** -0.5),
        'sh_up': nrm((L, D, D_SHARED), D ** -0.5),
        'sh_down': nrm((L, D_SHARED, D), D_SHARED ** -0.5),
    }

def reference(x_prompt, x_sample, cache_k, cache_v, state_wkv, c, c_ctx, mod_w, mod_b, norm1_g, norm2_g,
              w_in, q_norm, k_norm, sgu_norm_g, sgu_ws, sgu_bs, rwkv_conv, rwkv_w0, rwkv_w2, rwkv_a0,
              rwkv_a2, rwkv_g2, rwkv_k_k, rwkv_k_a, rwkv_r_k, rwkv_ln_g, rwkv_ln_b, proj_attn, proj_sgu,
              proj_rwkv, w_out, router_w, router_bias, exp_gate, exp_up, exp_down, sh_gate, sh_up, sh_down):
    P = {
        'mod_w': mod_w, 'mod_b': mod_b, 'norm1_g': norm1_g, 'norm2_g': norm2_g, 'w_in': w_in,
        'q_norm': q_norm, 'k_norm': k_norm, 'sgu_norm_g': sgu_norm_g, 'sgu_ws': sgu_ws, 'sgu_bs': sgu_bs,
        'rwkv_conv': rwkv_conv, 'rwkv_w0': rwkv_w0, 'rwkv_w2': rwkv_w2, 'rwkv_a0': rwkv_a0,
        'rwkv_a2': rwkv_a2, 'rwkv_g2': rwkv_g2, 'rwkv_k_k': rwkv_k_k, 'rwkv_k_a': rwkv_k_a,
        'rwkv_r_k': rwkv_r_k, 'rwkv_ln_g': rwkv_ln_g, 'rwkv_ln_b': rwkv_ln_b, 'proj_attn': proj_attn,
        'proj_sgu': proj_sgu, 'proj_rwkv': proj_rwkv, 'w_out': w_out, 'router_w': router_w,
        'router_bias': router_bias, 'exp_gate': exp_gate, 'exp_up': exp_up, 'exp_down': exp_down,
        'sh_gate': sh_gate, 'sh_up': sh_up, 'sh_down': sh_down,
    }

    xp = x_prompt
    c_p = jnp.broadcast_to(c_ctx, (x_prompt.shape[0], D_MODEL))
    ks, vs, ss = [], [], []
    for l in range(DEPTH):
        xp, (k_l, v_l, s_f, s_b) = trunk_layer(xp, c_p, P, l)
        ks.append(k_l)
        vs.append(v_l)
        ss.append(jnp.stack([s_f, s_b], axis=1))
    new_cache_k = jnp.stack(ks, axis=1)
    new_cache_v = jnp.stack(vs, axis=1)
    new_state_wkv = jnp.stack(ss, axis=1).astype(x_prompt.dtype)

    rope = axial_rope(x_sample.shape[1])
    xs = x_sample
    for l in range(DEPTH):
        ctx = (cache_k[:, l], cache_v[:, l], state_wkv[:, l, 0], state_wkv[:, l, 1])
        xs, _ = trunk_layer(xs, c, P, l, ctx=ctx, rope=rope)

    return (xp, xs, new_cache_k, new_cache_v, new_state_wkv)


_drawn_inputs = setup_inputs


def setup_inputs(seed=0):
    import zlib

    import numpy as np

    out = dict(_drawn_inputs(seed))
    spreads = {}
    factors = {'q_norm': 3.526, 'rwkv_ln_b': 2.694, 'state_wkv': 3.885}
    for name, (base, spread) in spreads.items():
        noise = np.random.default_rng([zlib.crc32(name.encode()), seed]).standard_normal(out[name].shape)
        drawn = base * np.exp(spread * noise) if base else spread * noise
        out[name] = __import__('jax').numpy.asarray(drawn.astype(out[name].dtype))
    for name, factor in factors.items():
        out[name] = (out[name] * factor).astype(out[name].dtype)
    return out
```

```python
from contextlib import ExitStack

import numpy as np

import concourse.bass as bass
from concourse import mybir

F32 = mybir.dt.float32
U32 = mybir.dt.uint32
ALU = mybir.AluOpType
ACT = mybir.ActivationFunctionType
AX = mybir.AxisListType.X

P = 128
D = 1024
KD = D // P
DEPTH = 2
CTX, LAT = 128, 256
T = CTX + LAT
NT = T // P
GROUPS = [(0, CTX), (CTX, T)]
HD = 64
QT = 4
DECAY = 0.606531
GN_EPS = 64e-5
EPS = 1e-6
N_EXP, TOP_K, SHARED = 64, 6, 2
ROUTED_SCALE = 2.5
SLOTS = 3
SLOT_W = KD * 3 * P

C_MOD = 0
C_IN = C_MOD + 16
C_MERGE = C_IN + 10
C_OUT = C_MERGE + 12
C_EXP = C_OUT + 4
N_CHUNKS = C_EXP + N_EXP + SHARED
ROUNDS = (N_EXP + SHARED) // SLOTS
assert C_EXP % SLOTS == 0 and N_CHUNKS % SLOTS == 0


def offsets(sizes):
    at, out = 0, {}
    for name, n in sizes:
        out[name] = at
        at += n
    return out, at


MAT, N_MAT = offsets([("sgu_ws", 512), ("w2", 512), ("a2", 512), ("g2", 512), ("router", KD * N_EXP),
                      ("ctx_kT", P), ("ctx_v", P), ("state0", 512)])
VEC, N_VEC = offsets([("g1", KD), ("g2n", KD), ("mod_b", 48), ("qn", 1), ("kn", 1), ("sgu_g", 4),
                      ("conv", 36), ("w0", 8), ("a0", 8), ("k_k", 4), ("k_a", 4), ("r_k", 4),
                      ("ln_g", 4), ("ln_b", 4)])
ROW, N_ROW = offsets([("sgu_b", 512), ("router_b", N_EXP)])
CON, N_CON = offsets([("ident", P), ("heads", P), ("ones", P), ("rot", P), ("cos", LAT), ("sin", LAT),
                      ("causal", 4 * P), ("level", 14 * P), ("iota", N_EXP), ("cvec", KD * 2)])

PAD = 388
CVW = 386
CV_AT = [0, 129, 257]
LEVELS = 7
Z_ACT = (16, 29, 30)
SCANS = [(0, 0), (1, 0), (0, 1), (1, 2), (0, 2), (1, 1)]


def program(nc, xT, weights, params, rows, consts, yT, new_k, new_v, new_s, depth=DEPTH):
    combine_dram = nc.dram_tensor("combine", (N_EXP + SHARED, T), F32).ap()
    with ExitStack() as ctx:
        def sb(name, shape, dt=F32):
            return ctx.enter_context(nc.sbuf_tensor(name, shape, dt))

        def sem(name):
            return ctx.enter_context(nc.semaphore(name))

        X = sb("X", [P, KD, T])
        H = sb("H", [P, KD, T])
        o_attn = sb("o_attn", [P, QT, T])
        o_sgu = sb("o_sgu", [P, QT, T])
        o_rwkv = sb("o_rwkv", [P, QT, T])
        slot = [sb(f"slot{s}", [P, SLOT_W]) for s in range(SLOTS)]
        con = sb("con", [P, N_CON])
        mat = sb("mat", [P, N_MAT])
        vec = sb("vec", [P, N_VEC])
        row = sb("row", [P, N_ROW])
        mod = sb("mod", [P, 48, 2])
        amp = sb("amp", [P, 2, KD, 2])
        csil = sb("csil", [P, KD, 2])
        small = sb("small", [P, 64])
        epscol = sb("epscol", [P, 4])
        ps = ctx.enter_context(nc.psum_tensor("ps", [P, 8, 512], F32))

        def c_(name, n=P):
            return con[:, CON[name]:CON[name] + n]

        ident, heads, ones, rot = (c_(n) for n in ("ident", "heads", "ones", "rot"))
        cos, sin = c_("cos", LAT), c_("sin", LAT)

        def v_(name, i=0, n=1):
            return vec[:, VEC[name] + i:VEC[name] + i + n]

        def m_(name, n=512):
            return mat[:, MAT[name]:MAT[name] + n]

        ARENA = 24512
        arena = sb("arena", [P, ARENA])

        def at(off, *shape):
            n = int(np.prod(shape))
            assert off + n <= ARENA, (off, shape)
            a = arena[:, off:off + n]
            if len(shape) == 2:
                a = a.rearrange("p (a b) -> p a b", a=shape[0])
            if len(shape) == 3:
                a = a.rearrange("p (a b c) -> p a b c", a=shape[0], b=shape[1])
            return a

        XW, XA, XG = (at(i * T, T) for i in range(3))
        A0 = 3 * T
        QK = at(A0, 5, T)
        VT = at(A0 + 5 * T, NT, P)
        SU = at(A0 + 6 * T, QT, T)
        SV = at(A0 + 10 * T, NT, 512)
        RAW = at(A0 + 14 * T, 12, PAD)
        A1 = A0 + 14 * T + 12 * PAD
        SQ5 = at(A1, 5, T)
        RS5 = at(A1 + 5 * T, 5, T)
        PM = at(A1, 3, T)
        PTS = at(A1 + 3 * T, 2, T)
        KOUT = at(A1 + 10 * T, P)
        att_small = at(A1 + 10 * T + P, 4, 24)
        SGT = at(A1, NT, P)
        SSQ = at(A1 + T, 512)
        SQ8 = at(A0, KD, T)
        RS1 = at(A0 + 8 * T, T)
        CV = at(ARENA - 12 * CVW, 12, CVW)
        B1 = A0
        KK = at(B1, QT, CVW); B1 += QT * CVW
        VTM = at(B1, NT, 512); B1 += NT * 512
        KS = at(B1, QT, CVW); B1 += QT * CVW
        SG = at(B1, QT, P); B1 += 512
        SA = at(B1, QT, P); B1 += 512
        CUM = at(B1, QT, P); B1 += 512
        CX = at(B1, QT, P); B1 += 512
        EP = at(B1, QT, P); B1 += 512
        BE = at(B1, QT, P); B1 += 512
        AR = at(B1, QT, 2 * P); B1 += 1024
        KTM = at(B1, 512); B1 += 512
        KA, BTM = SG, EP.rearrange("p j t -> p (j t)")
        G = at(B1, 8, 512); B1 += 4096
        XX = at(B1, 8, 2, P); B1 += 2048
        BL = at(B1, 2, 512); B1 += 1024
        YS = at(B1, 2, 512); B1 += 1024
        SH = at(B1, QT, HD); B1 += 256
        SL = at(B1, 2, QT * HD); B1 += 512
        SOUT = at(B1, 2, QT * HD); B1 += 512
        HALF = at(B1, QT); B1 += 4
        EH = at(B1, QT); B1 += 4
        assert B1 <= ARENA - 12 * CVW, (B1, ARENA - 12 * CVW)
        RSB, USB = YS[:, 0, :], YS[:, 1, :]
        E0 = A0 + 2 * QT * CVW + NT * 512
        E_SQ = at(E0, QT, T)
        E_RS = at(E0 + 4 * T, QT, T)
        E_B = at(E0 + 8 * T, QT, T)
        MG = at(0, KD, T)
        GT = at(8 * T, 2, 3, T)
        MT = at(14 * T, 3, T)
        SC = at(0, NT, N_EXP)
        BI = at(192, NT, N_EXP)
        CB = at(384, NT, N_EXP)
        TOPV = at(576, NT, 8)
        TOPF = at(600, NT, 8)
        EQ = at(640, TOP_K, N_EXP)
        topi = sb("topi", [P, NT, 8], U32)
        CT = at(1024, T)
        R_SQ8 = at(2048, KD, T)
        R_RS1 = at(2048 + 8 * T, T)
        SGS = at(2048, SLOTS, T)
        TS = at(2048 + 3 * T, SLOTS, T)
        HID = at(2048 + 6 * T, SLOTS, T)
        CBC = at(2048 + 9 * T, SLOTS, T)
        RO = at(2048 + 12 * T, NT, D)

        const_landed = sem("const_landed")
        pool_ready = sem("pool_ready")
        eps_ready = sem("eps_ready")
        csil_ready = sem("csil_ready")
        line_written = sem("line_written")
        y_written = sem("y_written")
        row_landed = [sem(f"row{s}_landed") for s in range(SLOTS)]
        arrived = sem("arrived")
        released = sem("released")
        seen = {n: sem(f"seen_{n}") for n in ("pe", "act", "dve", "pool", "sp")}

        layer_sems = []

        def lsem(name):
            s = sem(name)
            layer_sems.append(s)
            return s

        slot_filled = [lsem(f"slot{s}_filled") for s in range(SLOTS)]
        slot_free = [lsem(f"slot{s}_free") for s in range(SLOTS)]
        par_landed = lsem("par_landed")
        act_step, dve_step, pool_step = lsem("act_step"), lsem("dve_step"), lsem("pool_step")
        mod_filled, mod_ready, amp_ready = lsem("mod_filled"), lsem("mod_ready"), lsem("amp_ready")
        sq_ready, sq_summed, root_ready, h_ready = (lsem(n) for n in ("sq_ready", "sq_summed", "root_ready", "h_ready"))
        z_filled, z_dve, z_act = lsem("z_filled"), lsem("z_dve"), lsem("z_act")
        raw_zeroed = lsem("raw_zeroed")
        qsq_ready, qsq_summed, qroot_ready, qk_normed = (lsem(n) for n in ("qsq_ready", "qsq_summed", "qroot_ready", "qk_normed"))
        rot_filled, qk_ready = lsem("rot_filled"), lsem("qk_ready")
        kout_filled, kout_ready, kv_written = lsem("kout_filled"), lsem("kout_ready"), lsem("kv_written")
        s_filled, s_max, p_exp, p_ready = (lsem(n) for n in ("s_filled", "s_max", "p_exp", "p_ready"))
        pt_filled, pt_ready, pv_filled, oattn_ready = (lsem(n) for n in ("pt_filled", "pt_ready", "pv_filled", "oattn_ready"))
        sv_summed, sv_root, sv_normed, sgu_filled, sgu_drained = (lsem(n) for n in ("sv_summed", "sv_root", "sv_normed", "sgu_filled", "sgu_drained"))
        cv_ready, kksq_ready, kk_summed, kk_root, kk_ready = (lsem(n) for n in ("cv_ready", "kksq_ready", "kk_summed", "kk_root", "kk_ready"))
        vtm_filled, vtm_ready = lsem("vtm_filled"), lsem("vtm_ready")
        wa_filled, gate_ready, cum_ready, exp_ready, px_ready = (lsem(n) for n in ("wa_filled", "gate_ready", "cum_ready", "exp_ready", "px_ready"))
        keys_ready = lsem("keys_ready")
        tm_filled, tm_ready = lsem("tm_filled"), lsem("tm_ready")
        gram_filled, gram_ready = lsem("gram_filled"), lsem("gram_ready")
        block_ready = lsem("block_ready")
        y_filled, y_ready, xy_filled, inv_ready = (lsem(n) for n in ("y_filled", "y_ready", "xy_filled", "inv_ready"))
        sh_ready, r_filled, r_ready, u_filled, u_ready = (lsem(n) for n in ("sh_ready", "r_filled", "r_ready", "u_filled", "u_ready"))
        os_filled, os_ready = lsem("os_filled"), lsem("os_ready")
        state_written = lsem("state_written")
        state_ready = lsem("state_ready")
        gn_ready, gn_summed, gn_root = lsem("gn_ready"), lsem("gn_summed"), lsem("gn_root")
        gn_done = lsem("gn_done")
        bonus_ready = lsem("bonus_ready")
        orwkv_ready = lsem("orwkv_ready")
        g_filled, g_ready, pr_filled, mg_ready = (lsem(n) for n in ("g_filled", "g_ready", "pr_filled", "mg_ready"))
        wo_filled, wo_drained = lsem("wo_filled"), lsem("wo_drained")
        sq2_ready, sq2_summed, root2_ready, h2_ready = (lsem(n) for n in ("sq2_ready", "sq2_summed", "root2_ready", "h2_ready"))
        lg_filled, score_ready, comb_ready, ct_filled, ct_ready, ct_written = (
            lsem(n) for n in ("lg_filled", "score_ready", "comb_ready", "ct_filled", "ct_ready", "ct_written"))
        e_gate, e_silu, e_up, e_scaled, e_hid = (lsem(n) for n in ("e_gate", "e_silu", "e_up", "e_scaled", "e_hid"))
        acc_filled, ro_ready = lsem("acc_filled"), lsem("ro_ready")
        back_filled, x_ready = lsem("back_filled"), lsem("x_ready")

        block = ctx.enter_context(nc.Block())

        class InOrder:

            def __init__(self, eng, step):
                self.eng, self.step, self.count = eng, step, {}

            def __call__(self, instruction, s=None):
                s = self.step if s is None else s
                n = self.count[id(s)] = self.count.get(id(s), 0) + 1
                instruction.then_inc(s, 1)
                self.eng.wait_ge(s, n)

        def layer_end(eng, name, layer):
            eng.drain().then_inc(arrived, 1)
            eng.wait_ge(released, layer + 1)
            eng.sem_inc(seen[name], 1)

        def chunk(n):
            return n % SLOTS, 16 * (n // SLOTS + 1)

        @block.sync
        def _(eng):
            eng.dma_start(con[:, :], consts).then_inc(const_landed, 16)
            eng.dma_start(X[:, :, :], xT.rearrange("(k p) t -> p k t", p=P)).then_inc(const_landed, 16)
            with eng.Fori(0, depth) as layer:
                def fill(s, n):
                    eng.dma_start(slot[s][:, :], weights[bass.ds(layer * N_CHUNKS + n, 1), :, :]
                                  .rearrange("l p n -> (l p) n")).then_inc(slot_filled[s], 16)

                for s in range(SLOTS):
                    fill(s, s)
                eng.dma_start(mat[:, :], params[bass.ds(layer, 1), :, 0:N_MAT]
                              .rearrange("l p n -> (l p) n")).then_inc(par_landed, 16)
                eng.dma_start(vec[:, :], params[bass.ds(layer, 1), :, N_MAT:N_MAT + N_VEC]
                              .rearrange("l p n -> (l p) n")).then_inc(par_landed, 16)
                eng.dma_start(row[:, :], rows[bass.ds(layer, 1), :].to_broadcast([P, N_ROW])).then_inc(par_landed, 16)
                with eng.Fori(1, N_CHUNKS // SLOTS) as i:
                    for s in range(SLOTS):
                        eng.wait_ge(slot_free[s], i)
                        fill(s, i * SLOTS + s)
                eng.wait_ge(arrived, 4 * layer + 4)
                eng.sem_inc(seen["sp"], 1)
                for s in layer_sems:
                    eng.sem_clear(s)
                eng.sem_inc(released, 1)
            eng.dma_start(yT.rearrange("(k p) t -> p k t", p=P), X[:, :, :]).then_inc(y_written, 16)
            eng.wait_ge(y_written, 16)

        @block.gpsimd
        def _(eng):
            do0 = InOrder(eng, pool_ready)
            for i, v in enumerate((EPS, 1e-12, GN_EPS, 0.0)):
                do0(eng.memset(epscol[:, i:i + 1], v))
            eng.wait_ge(const_landed, 32)
            for t in range(NT):
                eng.dma_start(combine_dram[N_EXP:N_EXP + SHARED, t * P:(t + 1) * P],
                              ones[0:SHARED, :]).then_inc(line_written, 16)
            eng.wait_ge(line_written, 16 * NT)
            with eng.Fori(0, depth) as layer:
                do = InOrder(eng, pool_step)
                eng.wait_ge(h_ready, 2)
                for col in (0, 1 + CTX, 2 + T):
                    do(eng.memset(RAW[:, :, col:col + 1], 0.0), raw_zeroed)
                for n, (d, c) in enumerate(SCANS):
                    for lv in range(LEVELS):
                        for g in range(2):
                            eng.wait_ge(gram_ready, 8 * n + 4 * g + 4)
                            if n or lv:
                                eng.wait_ge(y_filled, 2 * LEVELS * n + 2 * lv + g - 1)
                            if lv == 1:
                                eng.wait_ge(inv_ready, 2 * LEVELS * n + g + 1)
                            m = CON["level"] + (d * LEVELS + lv) * P
                            do(eng.tensor_tensor(BL[:, g, :].rearrange("p (u t) -> p u t", u=4),
                                                 G[:, 4 * g:4 * g + 4, 0:P],
                                                 con[:, None, m:m + P].to_broadcast([P, 4, P]), ALU.mult), block_ready)
                eng.wait_ge(ct_written, 16)
                def weight_rows(i):
                    for s in range(SLOTS):
                        eng.dma_start(CBC[:, s, :], combine_dram[bass.ds(i * SLOTS + s, 1), :]
                                      .to_broadcast([P, T])).then_inc(row_landed[s], 16)

                weight_rows(0)
                with eng.Fori(1, ROUNDS) as i:
                    eng.wait_ge(e_scaled, i * SLOTS)
                    eng.sem_inc(seen["pool"], 1)
                    weight_rows(i)
                layer_end(eng, "pool", layer)

        @block.scalar
        def _(eng):
            eng.wait_ge(const_landed, 32)
            eng.wait_ge(pool_ready, 4)
            eng.activation(csil[:, :, :], c_("cvec", 2 * KD).rearrange("p (k g) -> p k g", g=2),
                           ACT.Silu).then_inc(csil_ready, 1)
            with eng.Fori(0, depth) as layer:
                do = InOrder(eng, act_step)

                def norm_input(squares, SQ, summed, root, RS):
                    do(eng.activation(SQ[:, :, :], X[:, :, :], ACT.Square), squares)
                    eng.wait_ge(summed, 1)
                    do(eng.activation(RS, ps[:, 1, 0:T], ACT.Sqrt, bias=epscol[:, 0:1], scale=1.0 / D), root)

                norm_input(sq_ready, SQ8, sq_summed, root_ready, RS1)
                for n, dst, func in zip(Z_ACT, (XG, XW, XA), (ACT.Sigmoid, ACT.Tanh, ACT.Copy)):
                    eng.wait_ge(z_filled, n + 1)
                    do(eng.activation(dst, ps[:, n % 4, 0:T], func), z_act)
                eng.wait_ge(z_dve, 5)
                do(eng.activation(SQ5, QK, ACT.Square), qsq_ready)
                for j in range(5):
                    eng.wait_ge(qsq_summed, j + 1)
                    do(eng.activation(RS5[:, j, :], ps[:, 4 + j % 4, 0:T], ACT.Sqrt, bias=epscol[:, 0:1],
                                      scale=1.0 / HD), qroot_ready)
                eng.wait_ge(kout_filled, 1)
                do(eng.activation(KOUT, ps[:, 7, 0:P], ACT.Copy), kout_ready)
                eng.dma_start(new_k[bass.ds(layer, 1), :, :].rearrange("l t n -> (l t) n"), KOUT).then_inc(kv_written, 16)
                eng.dma_start(new_v[bass.ds(layer, 1), :, :].rearrange("l t n -> (l t) n"), VT[:, 0, :]).then_inc(kv_written, 16)
                for u in range(24 + 2):
                    if u < 24:
                        n = P if u % NT == 0 else T
                        eng.wait_ge(s_max, u + 1)
                        if u >= 3:
                            eng.wait_ge(pt_filled, u - 2)
                        do(eng.activation(PM[:, u % 3, 0:n], ps[:, 4 + u % 3, 0:n], ACT.Exp,
                                          bias=att_small[:, 1, u:u + 1], scale=HD ** -0.5,
                                          accum_out=att_small[:, 2, u:u + 1]), p_exp)
                    if u >= 2:
                        w = u - 2
                        n = P if w % NT == 0 else T
                        eng.wait_ge(pt_filled, w + 1)
                        if w >= 2:
                            eng.wait_ge(pv_filled, w - 1)
                        do(eng.activation(PTS[:, w % 2, 0:n], ps[:, (7, 3)[w % 2], 0:n], ACT.Copy), pt_ready)
                eng.wait_ge(kv_written, 32)
                eng.wait_ge(pv_filled, 24)
                eng.wait_ge(oattn_ready, 4)
                for t in range(NT):
                    do(eng.activation(SSQ, SV[:, t, :], ACT.Square, accum_out=small[:, t:t + 1]))
                do(eng.activation(small[:, 4:7], small[:, 0:3], ACT.Sqrt, bias=epscol[:, 0:1], scale=1.0 / 512), sv_root)
                eng.wait_ge(kksq_ready, 1)
                for j in range(QT):
                    eng.wait_ge(kk_summed, j + 1)
                    do(eng.activation(G[:, 4 + j, 0:CVW - 1], ps[:, 4 + j, 0:CVW - 1], ACT.Sqrt, bias=epscol[:, 1:2]), kk_root)
                for c in range(NT):
                    eng.wait_ge(vtm_filled, c + 1)
                    do(eng.activation(VTM[:, c, :], ps[:, c, :], ACT.Copy), vtm_ready)
                for n, (d, c) in enumerate(SCANS):
                    eng.wait_ge(wa_filled, n + 1)
                    if n:
                        eng.wait_ge(os_filled, n)
                    for j in range(QT):
                        do(eng.activation(SG[:, j, :], ps[:, 0, j * P:(j + 1) * P], ACT.Sigmoid,
                                          bias=v_("w0", d * 4 + j)))
                    for j in range(QT):
                        do(eng.activation(SA[:, j, :], ps[:, 1, j * P:(j + 1) * P], ACT.Sigmoid,
                                          bias=v_("a0", d * 4 + j)), gate_ready)
                    eng.wait_ge(cum_ready, n + 1)
                    do(eng.activation(EP, CUM, ACT.Exp, scale=-DECAY))
                    do(eng.activation(CUM, CUM, ACT.Exp, scale=DECAY))
                    do(eng.activation(CX, CX, ACT.Exp, scale=-DECAY))
                    do(eng.activation(EH, HALF, ACT.Exp, scale=-DECAY), exp_ready)
                    eng.wait_ge(tm_filled, n + 1)
                    do(eng.activation(BTM, ps[:, 2, :], ACT.Copy), tm_ready)
                    do(eng.activation(KTM, ps[:, 3, :], ACT.Copy), tm_ready)
                    for lv in range(1, LEVELS):
                        for g in range(2):
                            eng.wait_ge(y_filled, 2 * LEVELS * n + 2 * lv + g + 1)
                            do(eng.activation(YS[:, g, :], ps[:, g, :], ACT.Copy), y_ready)
                    eng.wait_ge(r_filled, n + 1)
                    for hh, b in enumerate((2, 0)):
                        do(eng.activation(RSB.rearrange("p (j h i) -> p j h i", j=QT, h=2)[:, :, hh, :],
                                          ps[:, b, 0:QT * HD].rearrange("p (j i) -> p j i", j=QT), ACT.Copy), r_ready)
                    eng.wait_ge(u_filled, n + 1)
                    do(eng.activation(USB, ps[:, 3, :], ACT.Copy, scale=-1.0), u_ready)
                eng.dma_start(new_s[bass.ds(layer, 1), :, :].rearrange("l p n -> (l p) n"),
                              SOUT.rearrange("p d n -> p (d n)")).then_inc(state_written, 16)
                for j in range(QT):
                    eng.wait_ge(gn_summed, QT + j + 1)
                    do(eng.activation(E_RS[:, j, :], ps[:, 4 + j, 0:T], ACT.Sqrt, bias=epscol[:, 2:3], scale=1.0 / HD), gn_root)
                for n in range(KD):
                    for b in range(3):
                        eng.wait_ge(g_filled, 3 * n + b + 1)
                        if n >= 2:
                            eng.wait_ge(mg_ready, n - 1)
                        do(eng.activation(GT[:, n % 2, b, :], ps[:, b, 0:T], ACT.Sigmoid), g_ready)
                eng.wait_ge(wo_drained, 2 * KD)
                norm_input(sq2_ready, R_SQ8, sq2_summed, root2_ready, R_RS1)
                eng.wait_ge(lg_filled, 1)
                do(eng.activation(SC, ps[:, 0, 0:NT * N_EXP].rearrange("p (t e) -> p t e", t=NT), ACT.Sigmoid), score_ready)
                eng.wait_ge(ct_ready, 1)
                eng.wait_ge(line_written, 16 * NT)
                eng.dma_start(combine_dram[0:N_EXP, :], CT[0:N_EXP, :]).then_inc(ct_written, 16)
                def gates_of(i):
                    for s in range(SLOTS):
                        eng.wait_ge(e_gate, i * SLOTS + s + 1)
                        eng.activation(SGS[:, s, :], ps[:, 6, 0:T], ACT.Silu).then_inc(e_silu, 1)

                gates_of(0)
                with eng.Fori(1, ROUNDS) as i:
                    eng.wait_ge(e_scaled, i * SLOTS)
                    gates_of(i)
                eng.wait_ge(state_written, 16)
                layer_end(eng, "act", layer)

        @block.vector
        def _(eng):
            eng.wait_ge(const_landed, 32)
            with eng.Fori(0, depth) as layer:
                do = InOrder(eng, dve_step)

                def sum2(out, a, b, op=ALU.add, s=None):
                    do(eng.tensor_tensor(out, a, b, op), s)

                eng.wait_ge(par_landed, 48)
                eng.wait_ge(mod_filled, 1)
                do(eng.tensor_tensor(mod[:, :, :], ps[:, 0, 0:96].rearrange("p (m g) -> p m g", g=2),
                                     v_("mod_b", 0, 48)[:, :, None].to_broadcast([P, 48, 2]), ALU.add), mod_ready)
                for i, (g, m) in enumerate((("g1", 1), ("g2n", 4))):
                    do(eng.tensor_scalar(amp[:, i, :, :], mod[:, m * KD:(m + 1) * KD, :], 1.0, None, ALU.add))
                    do(eng.tensor_tensor(amp[:, i, :, :], amp[:, i, :, :],
                                         v_(g, 0, KD)[:, :, None].to_broadcast([P, KD, 2]), ALU.mult))

                def modulated(i, shift, root, RS, ready):
                    eng.wait_ge(root, 1)
                    do(eng.reciprocal(RS, RS))
                    do(eng.tensor_tensor(H[:, :, :], X[:, :, :], RS[:, None, :].to_broadcast([P, KD, T]), ALU.mult))
                    for g, (a, b) in enumerate(GROUPS):
                        for k in range(KD):
                            do(eng.tensor_scalar(H[:, k, a:b], H[:, k, a:b], amp[:, i, k, g:g + 1],
                                                 mod[:, shift * KD + k, g:g + 1], ALU.mult, ALU.add),
                               ready if k == KD - 1 else None)

                modulated(0, 0, root_ready, RS1, h_ready)
                def out_of(n, dst, src):
                    eng.wait_ge(z_filled, n + 1)
                    do(eng.tensor_copy(dst, src), z_dve)

                for n in range(5):
                    out_of(n, QK[:, n, :], ps[:, n % 4, 0:T])
                out_of(5, VT, ps[:, 5 % 4, 0:T].rearrange("p (t n) -> p t n", t=NT))
                for n in range(6, 10):
                    out_of(n, SU[:, n - 6, :], ps[:, n % 4, 0:T])
                for n in range(10, 13):
                    out_of(n, SV[:, n - 10, 0:256], ps[:, n % 4, 0:256])
                for n in range(13, 16):
                    out_of(n, SV[:, n - 13, 256:512], ps[:, n % 4, 0:256])
                eng.wait_ge(raw_zeroed, 3)
                for n in range(17, 29):
                    j = n - 17
                    eng.wait_ge(z_filled, n + 1)
                    do(eng.tensor_copy(RAW[:, j, 1:1 + CTX], ps[:, n % 4, 0:CTX]))
                    do(eng.tensor_copy(RAW[:, j, 2 + CTX:2 + T], ps[:, n % 4, CTX:T]), z_dve)
                eng.wait_ge(qroot_ready, 5)
                do(eng.reciprocal(RS5, RS5))
                do(eng.scalar_tensor_tensor(QK[:, 0:4, :], QK[:, 0:4, :], v_("qn"), RS5[:, 0:4, :], ALU.mult, ALU.mult))
                do(eng.scalar_tensor_tensor(QK[:, 4, :], QK[:, 4, :], v_("kn"), RS5[:, 4, :], ALU.mult, ALU.mult), qk_normed)
                eng.wait_ge(rot_filled, 5)
                for j in range(5):
                    b, o = 4 + j // 2, (j % 2) * LAT
                    do(eng.tensor_tensor(SQ5[:, j, CTX:T], QK[:, j, CTX:T], cos, ALU.mult))
                    do(eng.tensor_tensor(RS5[:, j, CTX:T], ps[:, b, o:o + LAT], sin, ALU.mult))
                do(eng.tensor_tensor(QK[:, :, CTX:T], SQ5[:, :, CTX:T], RS5[:, :, CTX:T], ALU.add), qk_ready)
                for u in range(24 + 9):
                    if u < 24:
                        n = P if u % NT == 0 else T
                        eng.wait_ge(s_filled, u + 1)
                        do(eng.tensor_reduce(att_small[:, 0, u:u + 1], ps[:, 4 + u % 3, 0:n], AX, ALU.max))
                        do(eng.tensor_scalar(att_small[:, 1, u:u + 1], att_small[:, 0, u:u + 1], -HD ** -0.5, None,
                                             ALU.mult), s_max)
                    if 1 <= u <= 24:
                        w = u - 1
                        n = P if w % NT == 0 else T
                        eng.wait_ge(p_exp, w + 1)
                        do(eng.reciprocal(att_small[:, 3, w:w + 1], att_small[:, 2, w:w + 1]))
                        do(eng.tensor_scalar(PM[:, w % 3, 0:n], PM[:, w % 3, 0:n], att_small[:, 3, w:w + 1], None,
                                             ALU.mult), p_ready)
                    if u >= 9 and (u - 9) % 6 == 0 and (u - 9) // 6 < 4:
                        j = (u - 9) // 6
                        eng.wait_ge(pv_filled, 6 * j + 6)
                        do(eng.tensor_copy(o_attn[:, j, :], ps[:, j % 2, 0:T]), oattn_ready)
                eng.wait_ge(sv_root, 1)
                do(eng.reciprocal(small[:, 8:11], small[:, 4:7]))
                for t in range(NT):
                    do(eng.tensor_scalar(SV[:, t, :], SV[:, t, :], small[:, 8 + t:9 + t], None, ALU.mult), sv_normed)
                for g in range(4):
                    eng.wait_ge(sgu_filled, g + 1)
                    do(eng.scalar_tensor_tensor(SGT, ps[:, g % 2, 0:T].rearrange("p (t i) -> p t i", t=NT),
                                                v_("sgu_g", g),
                                                row[:, None, ROW["sgu_b"] + g * P:ROW["sgu_b"] + (g + 1) * P]
                                                .to_broadcast([P, NT, P]), ALU.mult, ALU.add), sgu_drained)
                    do(eng.tensor_tensor(o_sgu[:, g, :], SGT.rearrange("p t i -> p (t i)"), SU[:, g, :], ALU.mult))
                for j in range(12):
                    w = [v_("conv", i * 12 + j) for i in range(3)]
                    o = CV[:, j, 0:CVW - 1]
                    do(eng.tensor_scalar(o, RAW[:, j, 0:385], w[0], None, ALU.mult))
                    do(eng.scalar_tensor_tensor(o, RAW[:, j, 1:386], w[1], o, ALU.mult, ALU.add))
                    do(eng.scalar_tensor_tensor(o, RAW[:, j, 2:387], w[2], o, ALU.mult, ALU.add), cv_ready)
                R_, K_, V_ = CV[:, 0:4, :], CV[:, 4:8, :], CV[:, 8:12, :]
                W1 = CVW - 1
                for j in range(QT):
                    do(eng.tensor_scalar(KK[:, j, 0:W1], K_[:, j, 0:W1], v_("k_k", j), None, ALU.mult))
                do(eng.tensor_tensor(G[:, 0:4, 0:W1], KK[:, :, 0:W1], KK[:, :, 0:W1], ALU.mult), kksq_ready)
                eng.wait_ge(kk_root, 4)
                do(eng.reciprocal(G[:, 4:8, 0:W1], G[:, 4:8, 0:W1]))
                do(eng.tensor_tensor(KK[:, :, 0:W1], KK[:, :, 0:W1], G[:, 4:8, 0:W1], ALU.mult), kk_ready)
                do(eng.tensor_copy(SL, m_("state0").rearrange("p (d n) -> p d n", d=2)))
                do(eng.tensor_scalar(small[:, 16:20], v_("k_a", 0, 4), -1.0, 1.0, ALU.mult, ALU.add))
                for n, (d, c) in enumerate(SCANS):
                    a, b = CV_AT[c], CV_AT[c] + P
                    first = c not in [x[1] for x in SCANS[:n]]
                    eng.wait_ge(gate_ready, 4 * n + 4)
                    for j in range(QT):
                        src, dst, one = SG[:, j, :], CUM[:, j, :], ones
                        if d:
                            src, dst, one = src[:, ::-1], dst[:, ::-1], one[:, ::-1]
                        do(eng.tensor_tensor_scan(dst, one, src, 0.0, ALU.mult, ALU.add))
                    last = CUM[:, :, 0:1] if d else CUM[:, :, P - 1:P]
                    do(eng.tensor_scalar(HALF[:, :, None], last, 0.5, None, ALU.mult))
                    do(eng.tensor_tensor(CUM, CUM, HALF[:, :, None].to_broadcast([P, QT, P]), ALU.subtract))
                    do(eng.tensor_tensor(CX, CUM, SG, ALU.subtract), cum_ready)
                    eng.wait_ge(exp_ready, n + 1)
                    do(eng.tensor_tensor(AR[:, :, 0:P], KK[:, :, a:b], CX, ALU.mult))
                    do(eng.tensor_tensor(AR[:, :, P:2 * P], R_[:, :, a:b], EP, ALU.mult))
                    do(eng.tensor_tensor(BE, SA, CUM, ALU.mult))
                    do(eng.tensor_tensor(BE, BE, KK[:, :, a:b], ALU.mult))
                    for j in range(QT):
                        do(eng.tensor_scalar(SA[:, j, :], SA[:, j, :], v_("k_a", j), small[:, 16 + j:17 + j],
                                             ALU.mult, ALU.add))
                    do(eng.tensor_tensor(SA, SA, K_[:, :, a:b], ALU.mult))
                    if first:
                        do(eng.tensor_copy(KS[:, :, a:b], SA))
                    else:
                        do(eng.tensor_tensor(KS[:, :, a:b], KS[:, :, a:b], SA, ALU.add))
                    do(eng.tensor_tensor(KA, SA, CUM, ALU.mult), keys_ready)
                    if c:
                        do(eng.tensor_tensor(SH, SL[:, d, :].rearrange("p (j i) -> p j i", j=QT),
                                             EH[:, :, None].to_broadcast([P, QT, HD]), ALU.mult), sh_ready)
                    mask = con[:, None, CON["causal"] + d * 2 * P:CON["causal"] + (d + 1) * 2 * P].to_broadcast([P, 2, 2 * P])
                    for u in range(8):
                        eng.wait_ge(gram_filled, 8 * n + u + 1)
                        do(eng.tensor_tensor(G[:, u, :].rearrange("p (a t) -> p a t", a=2),
                                             ps[:, 4 + u % 4, :].rearrange("p (a t) -> p a t", a=2), mask, ALU.mult), gram_ready)
                    for lv in range(LEVELS):
                        for g in range(2):
                            XG4 = XX[:, 4 * g:4 * g + 4, :, :]
                            k = 2 * LEVELS * n + 2 * lv + g + 1
                            if lv == 0:
                                eng.wait_ge(y_filled, k)
                                eye = ident[:, None, :].to_broadcast([P, 4, P])
                                do(eng.tensor_tensor(XG4[:, :, 0, :], eye, ps[:, g, :].rearrange("p (u t) -> p u t", u=4), ALU.subtract))
                                do(eng.tensor_tensor(XG4[:, :, 1, :], eye, BL[:, g, :].rearrange("p (u t) -> p u t", u=4),
                                                     ALU.subtract), inv_ready)
                            elif lv < LEVELS - 1:
                                eng.wait_ge(xy_filled, 2 * (LEVELS - 1) * n + 2 * (lv - 1) + g + 1)
                                do(eng.tensor_tensor(XG4, XG4, ps[:, 4 + 2 * g:6 + 2 * g, :].rearrange(
                                    "p a (u x t) -> p (a u) x t", u=2, x=2), ALU.subtract), inv_ready)
                            else:
                                eng.wait_ge(xy_filled, 2 * (LEVELS - 1) * n + 2 * (lv - 1) + g + 1)
                                do(eng.tensor_tensor(XG4[:, :, 1, :], XG4[:, :, 1, :], ps[:, 4 + 2 * g, :].rearrange(
                                    "p (u t) -> p u t", u=4), ALU.subtract), inv_ready)
                    eng.wait_ge(os_filled, n + 1)
                    O_ = o_rwkv[:, :, c * P:(c + 1) * P]
                    src = ps[:, 4, :].rearrange("p (j t) -> p j t", j=QT)
                    do(eng.tensor_copy(O_, src)) if first else do(eng.tensor_tensor(O_, O_, src, ALU.add))
                    to = (SOUT if c == 0 else SL)[:, d, :].rearrange("p (j i) -> p j i", j=QT)
                    src = ps[:, 5, 0:QT * HD].rearrange("p (j i) -> p j i", j=QT)
                    if c:
                        do(eng.tensor_tensor(SH, SH, src, ALU.add))
                        src = SH
                    do(eng.tensor_tensor(to, src, EH[:, :, None].to_broadcast([P, QT, HD]), ALU.mult), state_ready)
                do(eng.tensor_copy(E_B, o_rwkv[:, :, :]), gn_ready)
                for j in range(QT):
                    eng.wait_ge(gn_summed, j + 1)
                    do(eng.scalar_tensor_tensor(E_B[:, j, :], ps[:, j, 0:T], -1.0 / HD, E_B[:, j, :], ALU.mult, ALU.add))
                do(eng.tensor_tensor(E_SQ, E_B, E_B, ALU.mult), gn_ready)
                eng.wait_ge(gn_root, QT)
                do(eng.reciprocal(E_RS, E_RS))
                do(eng.tensor_tensor(E_B, E_B, E_RS, ALU.mult))
                for j in range(QT):
                    do(eng.tensor_scalar(E_B[:, j, :], E_B[:, j, :], v_("ln_g", j), v_("ln_b", j), ALU.mult, ALU.add), gn_done)
                for j in range(QT):
                    for (a, b), o in zip(GROUPS, (0, 129)):
                        do(eng.scalar_tensor_tensor(E_SQ[:, j, a:b], R_[:, j, o:o + b - a], v_("r_k", j),
                                                    KS[:, j, o:o + b - a], ALU.mult, ALU.mult), bonus_ready)
                for j in range(QT):
                    eng.wait_ge(gn_summed, 2 * QT + j + 1)
                    for (a, b), o in zip(GROUPS, (0, 129)):
                        do(eng.tensor_tensor(E_RS[:, j, a:b], ps[:, j, a:b], V_[:, j, o:o + b - a], ALU.mult))
                    do(eng.tensor_tensor(E_B[:, j, :], E_B[:, j, :], E_RS[:, j, :], ALU.add))
                for j in range(QT):
                    eng.wait_ge(gn_summed, 3 * QT + j + 1)
                    do(eng.tensor_tensor(o_rwkv[:, j, :], E_B[:, j, :], ps[:, 4 + j, 0:T], ALU.mult), orwkv_ready)
                for n in range(KD):
                    eng.wait_ge(g_ready, 3 * n + 3)
                    for b in range(3):
                        eng.wait_ge(pr_filled, 3 * n + b + 1)
                        do(eng.tensor_tensor(MT[:, b, :], ps[:, 3 + b, 0:T], GT[:, n % 2, b, :], ALU.mult))
                    do(eng.tensor_tensor(MT[:, 0, :], MT[:, 0, :], MT[:, 1, :], ALU.add))
                    do(eng.tensor_tensor(MG[:, n, :], MT[:, 0, :], MT[:, 2, :], ALU.add), mg_ready)

                def residual(n, gate, src, s):
                    for g, (a, b) in enumerate(GROUPS):
                        do(eng.scalar_tensor_tensor(X[:, n, a:b], src[:, a:b], mod[:, gate * KD + n, g:g + 1],
                                                    X[:, n, a:b], ALU.mult, ALU.add), s)

                for n in range(KD):
                    eng.wait_ge(wo_filled, n + 1)
                    residual(n, 2, ps[:, 6 + n % 2, :], wo_drained)
                modulated(1, 3, root2_ready, R_RS1, h2_ready)
                eng.wait_ge(score_ready, 1)
                do(eng.tensor_tensor(BI, SC, row[:, None, ROW["router_b"]:ROW["router_b"] + N_EXP]
                                     .to_broadcast([P, NT, N_EXP]), ALU.add))
                for t in range(NT):
                    do(eng.max(TOPV[:, t, :], BI[:, t, :]))
                    do(eng.max_index(topi[:, t, :], TOPV[:, t, :], BI[:, t, :]))
                do(eng.tensor_copy(TOPF, topi[:, :, :]))
                for t in range(NT):
                    do(eng.tensor_tensor(EQ, c_("iota", N_EXP)[:, None, :].to_broadcast([P, TOP_K, N_EXP]),
                                         TOPF[:, t, 0:TOP_K, None].to_broadcast([P, TOP_K, N_EXP]), ALU.is_equal))
                    do(eng.tensor_reduce(CB[:, t, :], EQ.rearrange("p k e -> p e k"), AX, ALU.add))
                do(eng.tensor_tensor(CB, CB, SC, ALU.mult))
                do(eng.tensor_reduce(small[:, 24:27], CB, AX, ALU.add))
                do(eng.reciprocal(small[:, 28:31], small[:, 24:27]))
                for t in range(NT):
                    do(eng.tensor_scalar(CB[:, t, :], CB[:, t, :], small[:, 28 + t:29 + t], ROUTED_SCALE,
                                         ALU.mult, ALU.mult), comb_ready)
                eng.wait_ge(ct_filled, 1)
                do(eng.tensor_copy(CT[0:N_EXP, :], ps[0:N_EXP, 1, 0:T]), ct_ready)
                def hidden(i):
                    for s in range(SLOTS):
                        e = i * SLOTS + s
                        eng.wait_ge(row_landed[s], layer * (16 * (N_EXP + SHARED) // SLOTS) + i * 16 + 16)
                        eng.wait_ge(e_silu, e + 1)
                        eng.tensor_tensor(TS[:, s, :], SGS[:, s, :], CBC[:, s, :], ALU.mult).then_inc(e_scaled, 1)
                        eng.wait_ge(slot_free[s], i + C_EXP // SLOTS)
                        eng.wait_ge(e_scaled, e + 1)
                        eng.wait_ge(e_up, e + 1)
                        eng.tensor_tensor(HID[:, s, :], TS[:, s, :], ps[:, 7, 0:T], ALU.mult).then_inc(e_hid, 1)

                hidden(0)
                with eng.Fori(1, ROUNDS) as i:
                    eng.wait_ge(e_hid, i * SLOTS)
                    hidden(i)
                eng.wait_ge(acc_filled, 1)
                for t in range(NT):
                    do(eng.tensor_copy(RO[:, t, :], ps[:, 2 * t:2 * t + 2, :].rearrange("p a b -> p (a b)")), ro_ready)
                for n in range(KD):
                    eng.wait_ge(back_filled, n + 1)
                    residual(n, 5, ps[:, 6 + n % 2, :], x_ready)
                layer_end(eng, "dve", layer)

        @block.tensor
        def _(eng):
            eng.wait_ge(const_landed, 32)
            eng.wait_ge(csil_ready, 1)
            with eng.Fori(0, depth) as layer:
                def landed(n):
                    s, v = chunk(n)
                    eng.wait_ge(slot_filled[s], v)
                    return slot[s][:, :].rearrange("p (k n) -> p k n", k=KD)

                owed = []

                def release(n):
                    owed.append(slot_free[n % SLOTS])

                def matmul(*args, **kw):
                    mm = eng.matmul(*args, **kw)
                    if owed:
                        mm.then_inc(owed.pop(0), 1)
                    return mm

                for n in range(16):
                    w = landed(C_MOD + n)
                    for m in range(3):
                        i = 3 * n + m
                        for k in range(KD):
                            mm = eng.matmul(ps[:, 0, 2 * i:2 * i + 2], w[:, k, m * P:(m + 1) * P], csil[:, k, :],
                                            start=(k == 0), stop=(k == KD - 1))
                    mm.then_inc(slot_free[(C_MOD + n) % SLOTS], 1)
                eng.wait_ge(sq_ready, 1)
                for k in range(KD):
                    mm = matmul(ps[:, 1, 0:T], ones, SQ8[:, k, :], start=(k == 0), stop=(k == KD - 1))
                    if k == 0:
                        mm.then_inc(mod_filled, 1)
                mm.then_inc(sq_summed, 1)
                eng.wait_ge(h_ready, 2)
                Z = {}

                def z_bank(n):
                    m = n - 4
                    if m in Z_ACT:
                        eng.wait_ge(z_act, Z_ACT.index(m) + 1)
                    elif m >= 0:
                        eng.wait_ge(z_dve, len([x for x in range(m + 1) if x not in Z_ACT]))
                    return n % 4

                def z_tile(n, w, col, free=None):
                    b = z_bank(n)
                    for k in range(KD):
                        mm = matmul(ps[:, b, 0:T], w[:, k, col:col + P], H[:, k, :], start=(k == 0), stop=(k == KD - 1))
                    mm.then_inc(z_filled, 1)

                def z_tokens(b, at_, t, w, col, width):
                    for k in range(KD):
                        mm = matmul(ps[:, b, at_:at_ + width], H[:, k, t * P:(t + 1) * P], w[:, k, col:col + width],
                                        start=(k == 0), stop=(k == KD - 1))
                    return mm

                w = landed(C_IN + 0)
                for m in range(3):
                    z_tile(m, w, m * P)
                release(C_IN + 0)
                w = landed(C_IN + 1)
                z_tile(3, w, 0)
                z_tile(4, w, P)
                b = z_bank(5)
                for t in range(NT):
                    mm = z_tokens(b, t * P, t, w, 2 * P, P)
                mm.then_inc(z_filled, 1)
                release(C_IN + 1)
                w = landed(C_IN + 2)
                for m in range(3):
                    z_tile(6 + m, w, m * P)
                release(C_IN + 2)
                w = landed(C_IN + 3)
                z_tile(9, w, 0)
                for t in range(NT):
                    z_tokens(z_bank(10 + t), 0, t, w, P, 2 * P).then_inc(z_filled, 1)
                release(C_IN + 3)
                w = landed(C_IN + 4)
                for t in range(NT):
                    z_tokens(z_bank(13 + t), 0, t, w, 0, 2 * P).then_inc(z_filled, 1)
                z_tile(16, w, 2 * P)
                release(C_IN + 4)
                for n in range(4):
                    w = landed(C_IN + 5 + n)
                    for m in range(3):
                        z_tile(17 + 3 * n + m, w, m * P)
                    release(C_IN + 5 + n)
                w = landed(C_IN + 9)
                z_tile(29, w, 0)
                z_tile(30, w, P)
                eng.drain().then_inc(slot_free[(C_IN + 9) % SLOTS], 1)
                eng.wait_ge(qsq_ready, 1)
                for j in range(5):
                    if j == 4:
                        eng.wait_ge(qroot_ready, 1)
                    matmul(ps[:, 4 + j % 4, 0:T], heads, SQ5[:, j, :], start=True, stop=True).then_inc(qsq_summed, 1)
                eng.wait_ge(qk_normed, 1)
                eng.transpose(ps[:, 7, 0:P], QK[:, 4, 0:CTX], ident).then_inc(kout_filled, 1)
                for j in range(5):
                    matmul(ps[:, 4 + j // 2, (j % 2) * LAT:(j % 2 + 1) * LAT], rot, QK[:, j, CTX:T],
                               start=True, stop=True).then_inc(rot_filled, 1)
                eng.wait_ge(qk_ready, 1)
                eng.wait_ge(kout_ready, 1)
                eng.wait_ge(z_act, 3)
                eng.wait_ge(z_dve, 28)
                units = [(j, hh, t) for j in range(QT) for hh in range(2) for t in range(NT)]

                def scores(u):
                    j, hh, t = units[u]
                    r = slice(hh * HD, (hh + 1) * HD)
                    if u >= 3:
                        eng.wait_ge(p_exp, u - 2)
                    q = QK[r, j, t * P:(t + 1) * P]
                    b = 4 + u % 3
                    if t == 0:
                        mm = matmul(ps[:, b, 0:P], q, QK[r, 4, 0:CTX], start=True, stop=True)
                    else:
                        matmul(ps[:, b, 0:P], q, m_("ctx_kT", P)[r, :], start=True, stop=True)
                        mm = matmul(ps[:, b, P:T], q, QK[r, 4, CTX:T], start=True, stop=True)
                    mm.then_inc(s_filled, 1)

                def turn(u):
                    t = units[u][2]
                    eng.wait_ge(p_ready, u + 1)
                    if u >= 2:
                        eng.wait_ge(pt_ready, u - 1)
                    for kb in range(1 if t == 0 else NT):
                        mm = eng.transpose(ps[:, (7, 3)[u % 2], kb * P:(kb + 1) * P], PM[:, u % 3, kb * P:(kb + 1) * P], ident)
                    mm.then_inc(pt_filled, 1)

                def values(u):
                    j, hh, t = units[u]
                    r = slice(hh * HD, (hh + 1) * HD)
                    eng.wait_ge(pt_ready, u + 1)
                    if j >= 2 and hh == 0 and t == 0:
                        eng.wait_ge(oattn_ready, j - 1)
                    v = [VT[:, 0, r]] if t == 0 else [m_("ctx_v", P)[:, r], VT[:, 1, r], VT[:, 2, r]]
                    for kb, vb in enumerate(v):
                        mm = matmul(ps[r, j % 2, t * P:(t + 1) * P], vb, PTS[:, u % 2, kb * P:(kb + 1) * P],
                                        start=(kb == 0), stop=(kb == len(v) - 1))
                    mm.then_inc(pv_filled, 1)

                for u in range(24 + 3):
                    if u < 24:
                        scores(u)
                    if 2 <= u < 26:
                        turn(u - 2)
                    if u >= 3:
                        values(u - 3)
                eng.wait_ge(sv_normed, NT)
                eng.wait_ge(oattn_ready, 4)
                for g in range(4):
                    if g >= 2:
                        eng.wait_ge(sgu_drained, g - 1)
                    for t in range(NT):
                        mm = matmul(ps[:, g % 2, t * P:(t + 1) * P], SV[:, t, g * P:(g + 1) * P],
                                        m_("sgu_ws")[:, g * P:(g + 1) * P], start=True, stop=True)
                    mm.then_inc(sgu_filled, 1)
                eng.wait_ge(sgu_drained, 4)
                eng.wait_ge(kksq_ready, 1)
                for j in range(QT):
                    matmul(ps[:, 4 + j, 0:CVW - 1], heads, G[:, j, 0:CVW - 1], start=True, stop=True).then_inc(kk_summed, 1)
                for c in range(NT):
                    for j in range(QT):
                        mm = eng.transpose(ps[:, c, j * P:(j + 1) * P], CV[:, 8 + j, CV_AT[c]:CV_AT[c] + P], ident)
                    mm.then_inc(vtm_filled, 1)
                eng.wait_ge(vtm_ready, NT)
                for n, (d, c) in enumerate(SCANS):
                    r = slice(d * HD, (d + 1) * HD)
                    half = [slice(0, HD), slice(HD, P)]
                    if n:
                        eng.wait_ge(state_ready, n)
                        eng.wait_ge(u_ready, n)
                    for x, b, name in ((XW, 0, "w2"), (XA, 1, "a2")):
                        for j in range(QT):
                            mm = matmul(ps[:, b, j * P:(j + 1) * P], m_(name)[r, j * P:(j + 1) * P],
                                            x[r, c * P:(c + 1) * P], start=True, stop=True)
                    mm.then_inc(wa_filled, 1)
                    eng.wait_ge(keys_ready, n + 1)
                    for b, src in ((2, BE), (3, KA)):
                        for j in range(QT):
                            mm = eng.transpose(ps[:, b, j * P:(j + 1) * P], src[:, j, :], ident)
                    mm.then_inc(tm_filled, 1)
                    for u in range(8):
                        j, hh = u // 2, half[u % 2]
                        if u == 0:
                            eng.wait_ge(kk_ready, 1)
                        if u >= 4:
                            eng.wait_ge(gram_ready, 8 * n + u - 3)
                        matmul(ps[:, 4 + u % 4, 0:2 * P], BE[hh, j, :], AR[hh, j, :], start=True, stop=True)
                        matmul(ps[:, 4 + u % 4, 2 * P:4 * P], KA[hh, j, :], AR[hh, j, :], start=True,
                                   stop=True).then_inc(gram_filled, 1)
                    for lv in range(LEVELS):
                        for g in range(2):
                            k = 2 * LEVELS * n + 2 * lv + g
                            eng.wait_ge(block_ready, k + 1)
                            if lv >= 1:
                                eng.wait_ge(inv_ready, k - 1)
                            if lv >= 2:
                                eng.wait_ge(y_ready, 2 * (LEVELS - 1) * n + 2 * (lv - 2) + g + 1)
                            for q in range(4):
                                mm = matmul(ps[:, g, q * P:(q + 1) * P], BL[:, g, q * P:(q + 1) * P],
                                                ident if lv == 0 else XX[:, 4 * g + q, 0, :], start=True, stop=True)
                            mm.then_inc(y_filled, 1)
                        for g in range(2):
                            if lv == 0:
                                continue
                            k = 2 * (LEVELS - 1) * n + 2 * (lv - 1) + g
                            eng.wait_ge(y_ready, k + 1)
                            if lv == 1:
                                eng.wait_ge(gram_ready, 8 * n + 8)
                            for q in range(4):
                                u, y = 4 * g + q, YS[:, g, q * P:(q + 1) * P]
                                if lv < LEVELS - 1:
                                    b, o = 4 + 2 * g + q // 2, (q % 2) * 2 * P
                                    matmul(ps[:, b, o:o + P], XX[:, u, 1, :], y, start=True, stop=True)
                                    mm = matmul(ps[:, b, o + P:o + 2 * P], y, XX[:, u, 1, :], start=True, stop=True)
                                else:
                                    mm = matmul(ps[:, 4 + 2 * g, q * P:(q + 1) * P], y, XX[:, u, 1, :], start=True, stop=True)
                            mm.then_inc(xy_filled, 1)
                    eng.wait_ge(tm_ready, 2 * n + 2)
                    eng.wait_ge(y_ready, 2 * (LEVELS - 1) * (n + 1))
                    if c:
                        eng.wait_ge(sh_ready, len([x for x in SCANS[:n + 1] if x[1]]))
                    for u in range(8):
                        j, hh = u // 2, half[u % 2]
                        out = ps[:, (2, 0)[u % 2], j * HD:(j + 1) * HD]
                        vt = VTM[:, c, u * HD:(u + 1) * HD]
                        if c:
                            matmul(out, AR[hh, j, 0:P], SH[hh, j, :], start=True, stop=False)
                        mm = matmul(out, G[:, u, 2 * P:3 * P], vt, start=(c == 0), stop=True)
                    mm.then_inc(r_filled, 1)
                    eng.wait_ge(r_ready, 2 * n + 2)
                    eng.wait_ge(inv_ready, 2 * LEVELS * (n + 1))
                    for u in range(8):
                        o = slice(u * HD, (u + 1) * HD)
                        mm = matmul(ps[:, 3, o], XX[:, u, 1, :], RSB[:, o], start=True, stop=True)
                    mm.then_inc(u_filled, 1)
                    eng.wait_ge(u_ready, n + 1)
                    for u in range(8):
                        j, hh = u // 2, half[u % 2]
                        o = slice(u * HD, (u + 1) * HD)
                        out = ps[hh, 4, j * P:(j + 1) * P]
                        if c:
                            matmul(out, SH[hh, j, :], AR[hh, j, P:2 * P], start=True, stop=False)
                        matmul(out, USB[:, o], G[:, u, P:2 * P], start=(c == 0), stop=False)
                        matmul(out, VTM[:, c, o], G[:, u, 3 * P:4 * P], start=False, stop=True)
                    for u in range(8):
                        j, hh = u // 2, half[u % 2]
                        o = slice(u * HD, (u + 1) * HD)
                        out = ps[hh, 5, j * HD:(j + 1) * HD]
                        matmul(out, BTM[:, o], USB[:, o], start=True, stop=False)
                        mm = matmul(out, KTM[:, o], VTM[:, c, o], start=False, stop=True)
                    mm.then_inc(os_filled, 1)
                eng.wait_ge(gn_ready, 1)
                for j in range(QT):
                    matmul(ps[:, j, 0:T], heads, o_rwkv[:, j, :], start=True, stop=True).then_inc(gn_summed, 1)
                eng.wait_ge(gn_ready, 2)
                for j in range(QT):
                    matmul(ps[:, 4 + j, 0:T], heads, E_SQ[:, j, :], start=True, stop=True).then_inc(gn_summed, 1)
                eng.wait_ge(bonus_ready, 8)
                for j in range(QT):
                    matmul(ps[:, j, 0:T], heads, E_SQ[:, j, :], start=True, stop=True).then_inc(gn_summed, 1)
                for j in range(QT):
                    matmul(ps[:, 4 + j, 0:T], m_("g2")[:, j * P:(j + 1) * P], XG, start=True, stop=True).then_inc(gn_summed, 1)
                for n in range(KD):
                    pair, odd = n // 2, n % 2
                    w = landed(C_MERGE + 3 * pair + 2 * odd)
                    for b in range(3):
                        if n:
                            eng.wait_ge(g_ready, 3 * (n - 1) + b + 1)
                        elif b == 0:
                            eng.wait_ge(orwkv_ready, QT)
                        for k in range(KD):
                            mm = matmul(ps[:, b, 0:T], w[:, k, b * P:(b + 1) * P], H[:, k, :], start=(k == 0), stop=(k == KD - 1))
                        mm.then_inc(g_filled, 1)
                    release(C_MERGE + 3 * pair + 2 * odd)
                    landed(C_MERGE + 3 * pair + 1)
                    w = slot[(C_MERGE + 3 * pair + 1) % SLOTS][:, :].rearrange("p (b k n) -> p b k n", b=3, k=QT)
                    if n:
                        eng.wait_ge(mg_ready, n)
                    for b, o in enumerate((o_attn, o_sgu, o_rwkv)):
                        for k in range(QT):
                            mm = matmul(ps[:, 3 + b, 0:T], w[:, b, k, odd * P:(odd + 1) * P], o[:, k, :],
                                            start=(k == 0), stop=(k == QT - 1))
                        mm.then_inc(pr_filled, 1)
                    if odd:
                        release(C_MERGE + 3 * pair + 1)
                eng.wait_ge(mg_ready, KD)
                for n in range(KD):
                    w = landed(C_OUT + n // 2)
                    if n >= 2:
                        eng.wait_ge(wo_drained, 2 * (n - 1))
                    for k in range(KD):
                        mm = matmul(ps[:, 6 + n % 2, 0:T], w[:, k, (n % 2) * P:(n % 2 + 1) * P], MG[:, k, :],
                                        start=(k == 0), stop=(k == KD - 1))
                    mm.then_inc(wo_filled, 1)
                    if n % 2:
                        release(C_OUT + n // 2)
                eng.wait_ge(sq2_ready, 1)
                for k in range(KD):
                    mm = matmul(ps[:, 1, 0:T], ones, R_SQ8[:, k, :], start=(k == 0), stop=(k == KD - 1))
                mm.then_inc(sq2_summed, 1)
                eng.wait_ge(h2_ready, 2)
                for t in range(NT):
                    for k in range(KD):
                        mm = matmul(ps[:, 0, t * N_EXP:(t + 1) * N_EXP], H[:, k, t * P:(t + 1) * P],
                                        m_("router")[:, k * N_EXP:(k + 1) * N_EXP], start=(k == 0), stop=(k == KD - 1))
                mm.then_inc(lg_filled, 1)
                eng.wait_ge(comb_ready, NT)
                for t in range(NT):
                    mm = eng.transpose(ps[0:N_EXP, 1, t * P:(t + 1) * P], CB[:, t, :], ident)
                mm.then_inc(ct_filled, 1)
                eng.wait_ge(ct_ready, 1)

                def half_of(s, bank, part, signal):
                    for k in range(KD):
                        o = part * KD * P + k * P
                        mm = eng.matmul(ps[:, bank, 0:T], slot[s][:, o:o + P], H[:, k, :], start=(k == 0), stop=(k == KD - 1))
                    mm.then_inc(signal, 1)

                def down(s, start, stop):
                    for t in range(NT):
                        for h in range(2):
                            o = 2 * KD * P + h * 512
                            mm = eng.matmul(ps[:, 2 * t + h, :], HID[:, s, t * P:(t + 1) * P], slot[s][:, o:o + 512],
                                            start=start, stop=stop, skip_group_check=True)
                    return mm

                def expert(i, s, first=False, start=False):
                    e = i * SLOTS + s
                    eng.wait_ge(slot_filled[s], 16 * (C_EXP // SLOTS + 1) + 16 * i)
                    if not first:
                        eng.wait_ge(e_silu, e)
                    half_of(s, 6, 0, e_gate)
                    if not first:
                        eng.wait_ge(e_hid, e)
                    half_of(s, 7, 1, e_up)
                    if not first:
                        down((s - 1) % SLOTS, start, False).then_inc(slot_free[(s - 1) % SLOTS], 1)

                for s in range(SLOTS):
                    expert(0, s, first=(s == 0), start=(s == 1))
                with eng.Fori(1, ROUNDS) as i:
                    for s in range(SLOTS):
                        expert(i, s)
                eng.wait_ge(e_hid, N_EXP + SHARED)
                down(SLOTS - 1, False, True).then_inc(acc_filled, 1)
                eng.wait_ge(ro_ready, NT)
                for n in range(KD):
                    if n >= 2:
                        eng.wait_ge(x_ready, 2 * (n - 1))
                    for t in range(NT):
                        mm = eng.transpose(ps[:, 6 + n % 2, t * P:(t + 1) * P], RO[:, t, n * P:(n + 1) * P], ident)
                    mm.then_inc(back_filled, 1)
                layer_end(eng, "pe", layer)


def constants():
    out = np.zeros((P, N_CON), np.float32)

    def put(name, a, off=0):
        out[:, CON[name] + off:CON[name] + off + a.shape[1]] = a

    i = np.arange(P)
    put("ident", np.eye(P))
    put("heads", (i[:, None] // HD == i[None] // HD))
    put("ones", np.ones((P, P)))
    f = HD // 4
    part, low = (i // f) % 2, i % f
    rot = np.zeros((P, P))
    for m in range(P):
        rot[m + f if part[m] == 0 else m - f, m] = -1.0 if part[m] == 0 else 1.0
    put("rot", rot)
    t = np.arange(LAT)
    inv = (10000.0 ** (-np.arange(f, dtype=np.float32) / f)).astype(np.float32)
    pos = np.stack([(t // 64), (t % 64)]).astype(np.float32)
    axis = (i // (2 * f)) % 2
    ang = (pos[axis] * inv[low][:, None]).astype(np.float32)
    put("cos", np.cos(ang))
    put("sin", np.sin(ang))
    s_, t_ = i[:, None], i[None]
    for d in range(2):
        strict = (s_ < t_) if d == 0 else (s_ > t_)
        put("causal", strict, d * 2 * P)
        put("causal", strict | (s_ == t_), d * 2 * P + P)
        for lv in range(LEVELS):
            b = 1 << lv
            put("level", strict & (s_ // (2 * b) == t_ // (2 * b)) & (s_ // b != t_ // b), (d * LEVELS + lv) * P)
    put("iota", np.broadcast_to(np.arange(N_EXP), (P, N_EXP)))
    return out


def lay_out(a):
    L = a["w_in"].shape[0]
    a = {k: np.asarray(v) for k, v in a.items()}
    xT = np.concatenate([a["x_prompt"].reshape(CTX, D), a["x_sample"].reshape(LAT, D)]).T
    W = np.zeros((L, N_CHUNKS, P, SLOT_W), np.float32)

    def by_k(w, tiles):
        return w.reshape(-1, P, w.shape[-1]).transpose(1, 0, 2)

    for l in range(L):
        for n in range(16):
            W[l, C_MOD + n] = by_k(a["mod_w"][l][:, n * 384:(n + 1) * 384], 3).reshape(P, -1)
        w = a["w_in"][l]
        q, k, v, su, sv, rkv, xw, xa, xg, gates = np.split(
            w, np.cumsum([512, 128, 128, 512, 512, 1536, 128, 128, 128]), axis=1)
        q = q.reshape(D, 2, 4, HD).transpose(0, 2, 1, 3).reshape(D, 512)
        seq = np.concatenate([q, k, v, su, sv, xg, rkv, xw, xa, np.zeros((D, P), np.float32)], axis=1)
        for n in range(10):
            W[l, C_IN + n] = by_k(seq[:, n * 384:(n + 1) * 384], 3).reshape(P, -1)
        gates = gates.reshape(D, 3, D)
        pa = a["proj_attn"][l].reshape(2, 4, HD, D).transpose(1, 0, 2, 3).reshape(512, D)
        pr = np.stack([pa, a["proj_sgu"][l], a["proj_rwkv"][l]])
        for pair in range(4):
            for odd in range(2):
                n = 2 * pair + odd
                W[l, C_MERGE + 3 * pair + 2 * odd] = by_k(gates[:, :, n * P:(n + 1) * P].reshape(D, 384), 3).reshape(P, -1)
            cols = pr[:, :, 2 * pair * P:2 * (pair + 1) * P].reshape(3, 4, P, 2 * P).transpose(2, 0, 1, 3)
            W[l, C_MERGE + 3 * pair + 1] = cols.reshape(P, -1)
            W[l, C_OUT + pair].reshape(P, KD, 3 * P)[:, :, 0:2 * P] = by_k(
                a["w_out"][l][:, 2 * pair * P:2 * (pair + 1) * P], 2)
        E = W[l, C_EXP:].reshape(N_EXP + SHARED, P, 3, KD * P)
        for part, name, sh in ((0, "exp_gate", "sh_gate"), (1, "exp_up", "sh_up")):
            E[:N_EXP, :, part] = a[name][l].reshape(N_EXP, KD, P, P).transpose(0, 2, 1, 3).reshape(N_EXP, P, KD * P)
            E[N_EXP:, :, part] = a[sh][l].reshape(KD, P, SHARED, P).transpose(2, 1, 0, 3).reshape(SHARED, P, KD * P)
        E[:N_EXP, :, 2] = a["exp_down"][l]
        E[N_EXP:, :, 2] = a["sh_down"][l].reshape(SHARED, P, D)

    par = np.zeros((L, P, N_MAT + N_VEC), np.float32)

    def mat(name, x):
        par[:, :, MAT[name]:MAT[name] + x.shape[-1]] = x

    def vec(name, x):
        n = x.shape[1]
        par[:, :, N_MAT + VEC[name]:N_MAT + VEC[name] + n] = x.transpose(0, 2, 1)

    mat("sgu_ws", a["sgu_ws"].transpose(0, 3, 1, 2).reshape(L, P, 512))
    mat("w2", a["rwkv_w2"].reshape(L, P, 512))
    mat("a2", a["rwkv_a2"].reshape(L, P, 512))
    mat("g2", a["rwkv_g2"])
    mat("router", a["router_w"].reshape(L, KD, P, N_EXP).transpose(0, 2, 1, 3).reshape(L, P, KD * N_EXP))
    mat("ctx_kT", a["cache_k"][0].reshape(L, CTX, P).transpose(0, 2, 1))
    mat("ctx_v", a["cache_v"][0].reshape(L, CTX, P))
    s = a["state_wkv"][0].reshape(L, 2, 4, 2, HD, HD)
    mat("state0", s.transpose(0, 3, 5, 1, 2, 4).reshape(L, P, 512))
    vec("g1", a["norm1_g"].reshape(L, KD, P))
    vec("g2n", a["norm2_g"].reshape(L, KD, P))
    vec("mod_b", a["mod_b"].reshape(L, 48, P))
    vec("qn", np.concatenate([a["q_norm"]] * 2, axis=1).reshape(L, 1, P))
    vec("kn", np.concatenate([a["k_norm"]] * 2, axis=1).reshape(L, 1, P))
    vec("sgu_g", a["sgu_norm_g"].reshape(L, 4, P))
    vec("conv", a["rwkv_conv"].reshape(L, 36, P))
    vec("w0", a["rwkv_w0"].reshape(L, 8, P))
    vec("a0", a["rwkv_a0"].reshape(L, 8, P))
    for name, src in (("k_k", "rwkv_k_k"), ("k_a", "rwkv_k_a"), ("r_k", "rwkv_r_k"), ("ln_g", "rwkv_ln_g"), ("ln_b", "rwkv_ln_b")):
        vec(name, a[src].reshape(L, 4, P))
    rows = np.concatenate([a["sgu_bs"].reshape(L, 512), a["router_bias"]], axis=1)
    con = constants()
    cv = np.stack([a["c_ctx"].reshape(KD, P), a["c"].reshape(KD, P)], axis=-1)
    con[:, CON["cvec"]:CON["cvec"] + 2 * KD] = cv.transpose(1, 0, 2).reshape(P, 2 * KD)
    return {"xT": np.ascontiguousarray(xT), "weights": W.reshape(L * N_CHUNKS, P, SLOT_W), "params": par,
            "rows": np.ascontiguousarray(rows), "consts": con}


def kernel(**inputs):
    from concourse import bacc
    from concourse.bass_utils import run_bass_kernel_spmd

    arrays = lay_out(inputs)
    nc = bacc.Bacc("TRN2", target_bir_lowering=False, num_devices=1)
    args = [nc.dram_tensor(n, v.shape, F32, kind="ExternalInput").ap() for n, v in arrays.items()]
    outs = {"yT": (D, T), "new_k": (DEPTH, CTX, P), "new_v": (DEPTH, CTX, P), "new_s": (DEPTH, P, 512)}
    args += [nc.dram_tensor(n, s, F32, kind="ExternalOutput").ap() for n, s in outs.items()]
    program(nc, *args)
    r = run_bass_kernel_spmd(nc, [arrays], core_ids=[0]).results[0]
    y = r["yT"].T
    kv = (1, DEPTH, CTX, 2, HD)
    s = r["new_s"].reshape(DEPTH, 2, HD, 2, 4, HD).transpose(0, 3, 4, 1, 5, 2)
    return (np.ascontiguousarray(y[:CTX]).reshape(1, CTX, D), np.ascontiguousarray(y[CTX:]).reshape(1, LAT, D),
            r["new_k"].reshape(kv), r["new_v"].reshape(kv),
            np.ascontiguousarray(s).reshape(1, DEPTH, 2, 8, HD, HD))
```

```python
from contextlib import ExitStack

import numpy as np

import concourse.bass as bass
from concourse import mybir

F32 = mybir.dt.float32
F32R = mybir.dt.float32r
U32 = mybir.dt.uint32
ALU = mybir.AluOpType
ACT = mybir.ActivationFunctionType
AX = mybir.AxisListType.X

P = 128
D = 1024
KD = D // P
DEPTH = 2
CTX, LAT = 128, 256
T = CTX + LAT
NT = T // P
GROUPS = [(0, CTX), (CTX, T)]
HD = 64
QT = 4
DECAY = 0.606531
GN_EPS = 64e-5
EPS = 1e-6
N_EXP, TOP_K, SHARED = 64, 6, 2
ROUTED_SCALE = 2.5
SLOTS = 2
SLOT_W = KD * 3 * P

C_MOD = 0
MOD_A, MOD_B = 6, 10
C_IN = C_MOD + MOD_A
C_MODB = C_IN + 10
C_MERGE = C_MODB + MOD_B
C_OUT = C_MERGE + 12
C_EXP = C_OUT + 4
S_IN, S_MERGE, S_OUT, S_EXP = 0, 10, 18, 22
N_CHUNKS = C_EXP + N_EXP + SHARED
ROUNDS = (N_EXP + SHARED) // SLOTS
assert C_EXP % SLOTS == 0 and N_CHUNKS % SLOTS == 0


def offsets(sizes):
    at, out = 0, {}
    for name, n in sizes:
        out[name] = at
        at += n
    return out, at


MAT, N_MAT = offsets([("sgu_ws", 512), ("w2", 512), ("a2", 512), ("g2", 512), ("router", KD * N_EXP),
                      ("ctx_kT", P), ("ctx_v", P), ("state0", 512)])
VEC, N_VEC = offsets([("g1", KD), ("g2n", KD), ("mod_b", 48), ("qn", 1), ("kn", 1), ("sgu_g", 4),
                      ("conv", 36), ("w0", 8), ("a0", 8), ("k_k", 4), ("k_a", 4), ("r_k", 4),
                      ("ln_g", 4), ("ln_b", 4)])
ROW, N_ROW = offsets([("sgu_b", 512), ("router_b", N_EXP)])
CON, N_CON = offsets([("ident", P), ("heads", P), ("ones", P), ("rot", P), ("cos", LAT), ("sin", LAT),
                      ("causal", 4 * P), ("level", 14 * P), ("iota", N_EXP), ("cvec", KD * 2)])

PAD = 388
CVW = 386
CV_AT = [0, 129, 257]
LEVELS = 7
Z_ACT = (16, 29, 30)
Z_OF = [(0, 1, 2), (3, 4, 5), (6, 7, 8), (9, 10, 11, 12), (13, 14, 15, 16)] + [
    (17 + 3 * i, 18 + 3 * i, 19 + 3 * i) for i in range(4)] + [(29, 30)]
SCANS = [(0, 0), (1, 0), (0, 1), (1, 2), (0, 2), (1, 1)]


def program(nc, xT, weights, params, rows, consts, yT, new_k, new_v, new_s, depth=DEPTH):
    combine_dram = nc.dram_tensor("combine", (N_EXP + SHARED, T), F32).ap()
    with ExitStack() as ctx:
        def sb(name, shape, dt=F32):
            return ctx.enter_context(nc.sbuf_tensor(name, shape, dt))

        def sem(name):
            return ctx.enter_context(nc.semaphore(name))

        X = sb("X", [P, KD, T])
        H_hi = sb("H_hi", [P, KD, T], F32R)
        H_lo = sb("H_lo", [P, KD, T], F32R)
        branches = sb("branches", [P, 3 * QT * T])
        o_attn, o_sgu, o_rwkv = (branches[:, i * QT * T:(i + 1) * QT * T].rearrange("p (j t) -> p j t", j=QT)
                                 for i in range(3))
        slot = [sb(f"slot{s}", [P, SLOT_W]) for s in range(SLOTS)]
        con = sb("con", [P, N_CON])
        mat = sb("mat", [P, N_MAT])
        vec = sb("vec", [P, N_VEC])
        row = sb("row", [P, N_ROW])
        mod = sb("mod", [P, 48, 2])
        amp = sb("amp", [P, 2, KD, 2])
        csil = sb("csil", [P, KD, 2])
        mod_row = sb("mod_row", [2, 2, 3 * P])
        small = sb("small", [P, 64])
        epscol = sb("epscol", [P, 4])
        ps = ctx.enter_context(nc.psum_tensor("ps", [P, 8, 512], F32))

        def c_(name, n=P):
            return con[:, CON[name]:CON[name] + n]

        ident, heads, ones, rot = (c_(n) for n in ("ident", "heads", "ones", "rot"))
        cos, sin = c_("cos", LAT), c_("sin", LAT)

        def v_(name, i=0, n=1):
            return vec[:, VEC[name] + i:VEC[name] + i + n]

        def m_(name, n=512):
            return mat[:, MAT[name]:MAT[name] + n]

        ARENA = 24512
        arena_at = -(-nc.sbuf_base // 32) * 32
        arena = sb("arena", [P, ARENA])

        def at(off, *shape):
            n = int(np.prod(shape))
            assert off + n <= ARENA, (off, shape)
            a = arena[:, off:off + n]
            if len(shape) == 2:
                a = a.rearrange("p (a b) -> p a b", a=shape[0])
            if len(shape) == 3:
                a = a.rearrange("p (a b c) -> p a b c", a=shape[0], b=shape[1])
            return a

        def rounded(name, off, *shape):
            return nc.alloc_sbuf_tensor_at(name, [P, *shape], F32R, offset=arena_at + 4 * off)

        PARTS = ARENA - 4 * SLOT_W
        W_hi = [rounded(f"W_hi{i}", PARTS + i * SLOT_W, SLOT_W) for i in range(2)]
        W_lo = [rounded(f"W_lo{i}", PARTS + (2 + i) * SLOT_W, SLOT_W) for i in range(2)]

        XW, XA, XG = (at(i * T, T) for i in range(3))
        A0 = 3 * T
        QK = at(A0, 5, T)
        VT = at(A0 + 5 * T, NT, P)
        SU = at(A0 + 6 * T, QT, T)
        SV = at(A0 + 10 * T, NT, 512)
        RAW = at(A0 + 14 * T, 12, PAD)
        A1 = A0 + 14 * T + 12 * PAD
        SQ5 = branches[:, QT * T:QT * T + 5 * T].rearrange("p (j t) -> p j t", j=5)
        RS5 = SQ5
        ROT5 = branches[:, 0:5 * LAT].rearrange("p (j t) -> p j t", j=5)
        PM = at(A1, 3, T)
        PTS = at(A1 + 3 * T, 2, T)
        KOUT = at(A1 + 10 * T, P)
        att_small = at(A1 + 10 * T + P, 4, 24)
        SGT = at(A1, NT, P)
        SSQ = at(A1 + T, 512)
        SQ8 = at(A0, KD, T)
        RS1 = at(A0 + 8 * T, T)
        H1 = at(A0 + 9 * T, KD, T)
        CV = at(ARENA - 12 * CVW, 12, CVW)
        B1 = A0
        KK = at(B1, QT, CVW); B1 += QT * CVW
        VTM = at(B1, NT, 512); B1 += NT * 512
        KS = at(B1, QT, CVW); B1 += QT * CVW
        SG = at(B1, QT, P); B1 += 512
        SA = at(B1, QT, P); B1 += 512
        CUM = at(B1, QT, P); B1 += 512
        CX = at(B1, QT, P); B1 += 512
        EP = at(B1, QT, P); B1 += 512
        BE = at(B1, QT, P); B1 += 512
        AR = at(B1, QT, 2 * P); B1 += 1024
        KTM = at(B1, 512); B1 += 512
        KA, BTM = SG, EP.rearrange("p j t -> p (j t)")
        G = at(B1, 8, 512); B1 += 4096
        XX = at(B1, 8, 2, P); B1 += 2048
        BL = at(B1, 2, 512); B1 += 1024
        YS = at(B1, 2, 512); B1 += 1024
        SH = at(B1, QT, HD); B1 += 256
        SL = at(B1, 2, QT * HD); B1 += 512
        SOUT = at(B1, 2, QT * HD); B1 += 512
        HALF = at(B1, QT); B1 += 4
        EH = at(B1, QT); B1 += 4
        assert B1 <= ARENA - 12 * CVW, (B1, ARENA - 12 * CVW)
        RSB, USB = YS[:, 0, :], YS[:, 1, :]
        E0 = A0 + 2 * QT * CVW + NT * 512
        E_SQ = at(E0, QT, T)
        E_RS = at(E0 + 4 * T, QT, T)
        E_B = at(E0 + 8 * T, QT, T)
        MG_hi = rounded("MG_hi", 0, KD, T)
        MG_lo = rounded("MG_lo", 8 * T, KD, T)
        GT = at(16 * T, 2, 3, T)
        MT = at(22 * T, 3, T)
        SC = at(0, NT, N_EXP)
        BI = at(192, NT, N_EXP)
        CB = at(384, NT, N_EXP)
        TOPV = at(576, NT, 8)
        TOPF = at(600, NT, 8)
        EQ = at(640, TOP_K, N_EXP)
        topi = sb("topi", [P, NT, 8], U32)
        CT = at(1024, T)
        R_SQ8 = at(2048, KD, T)
        R_RS1 = at(2048 + 8 * T, T)
        H2 = at(2048 + 9 * T, KD, T)
        SGS = at(2048, SLOTS, T)
        TS = at(2048 + 2 * T, SLOTS, T)
        CBC = at(2048 + 4 * T, SLOTS, T)
        HID_hi = rounded("HID_hi", 2048 + 6 * T, SLOTS, T)
        HID_lo = rounded("HID_lo", 2048 + 8 * T, SLOTS, T)
        RO = at(2048 + 10 * T, NT, D)

        const_landed = sem("const_landed")
        pool_ready = sem("pool_ready")
        eps_ready = sem("eps_ready")
        csil_ready = sem("csil_ready")
        line_written = sem("line_written")
        y_written = sem("y_written")
        row_landed = [sem(f"row{s}_landed") for s in range(SLOTS)]
        arrived = sem("arrived")
        released = sem("released")
        seen = {n: sem(f"seen_{n}") for n in ("pe", "act", "dve", "pool", "sp")}

        layer_sems = []

        def lsem(name):
            s = sem(name)
            layer_sems.append(s)
            return s

        slot_filled = [lsem(f"slot{s}_filled") for s in range(SLOTS)]
        slot_taken = [lsem(f"slot{s}_taken") for s in range(SLOTS)]
        hi_ready, parts_used = lsem("hi_ready"), lsem("parts_used")
        e_hi, e_lo, e_down, e_prod, e_hid_hi = (lsem(n) for n in ("e_hi", "e_lo", "e_down", "e_prod", "e_hid_hi"))
        mod_row_filled, mod_row_ready, modb_filled, modb_ready = (
            lsem(n) for n in ("mod_row_filled", "mod_row_ready", "modb_filled", "modb_ready"))
        par_landed = lsem("par_landed")
        act_step, dve_step, pool_step = lsem("act_step"), lsem("dve_step"), lsem("pool_step")
        mod_filled, mod_ready, amp_ready = lsem("mod_filled"), lsem("mod_ready"), lsem("amp_ready")
        sq_ready, sq_summed, root_ready, h_ready = (lsem(n) for n in ("sq_ready", "sq_summed", "root_ready", "h_ready"))
        z_filled, z_dve, z_act = lsem("z_filled"), lsem("z_dve"), lsem("z_act")
        raw_zeroed = lsem("raw_zeroed")
        qsq_ready, qsq_summed, qroot_ready, qk_normed = (lsem(n) for n in ("qsq_ready", "qsq_summed", "qroot_ready", "qk_normed"))
        rot_filled, qk_ready = lsem("rot_filled"), lsem("qk_ready")
        kout_filled, kout_ready, kv_written = lsem("kout_filled"), lsem("kout_ready"), lsem("kv_written")
        s_filled, s_max, p_exp, p_ready = (lsem(n) for n in ("s_filled", "s_max", "p_exp", "p_ready"))
        pt_filled, pt_ready, pv_filled, oattn_ready = (lsem(n) for n in ("pt_filled", "pt_ready", "pv_filled", "oattn_ready"))
        sv_summed, sv_root, sv_normed, sgu_filled, sgu_drained = (lsem(n) for n in ("sv_summed", "sv_root", "sv_normed", "sgu_filled", "sgu_drained"))
        cv_ready, kksq_ready, kk_summed, kk_root, kk_ready = (lsem(n) for n in ("cv_ready", "kksq_ready", "kk_summed", "kk_root", "kk_ready"))
        vtm_filled, vtm_ready = lsem("vtm_filled"), lsem("vtm_ready")
        wa_filled, gate_ready, cum_ready, exp_ready, px_ready = (lsem(n) for n in ("wa_filled", "gate_ready", "cum_ready", "exp_ready", "px_ready"))
        keys_ready = lsem("keys_ready")
        tm_filled, tm_ready = lsem("tm_filled"), lsem("tm_ready")
        gram_filled, gram_ready = lsem("gram_filled"), lsem("gram_ready")
        block_ready = lsem("block_ready")
        y_filled, y_ready, xy_filled, inv_ready = (lsem(n) for n in ("y_filled", "y_ready", "xy_filled", "inv_ready"))
        sh_ready, r_filled, r_ready, u_filled, u_ready = (lsem(n) for n in ("sh_ready", "r_filled", "r_ready", "u_filled", "u_ready"))
        os_filled, os_ready = lsem("os_filled"), lsem("os_ready")
        state_written = lsem("state_written")
        state_ready = lsem("state_ready")
        gn_ready, gn_summed, gn_root = lsem("gn_ready"), lsem("gn_summed"), lsem("gn_root")
        gn_done = lsem("gn_done")
        bonus_ready = lsem("bonus_ready")
        orwkv_ready = lsem("orwkv_ready")
        g_filled, g_ready, pr_filled, mg_ready = (lsem(n) for n in ("g_filled", "g_ready", "pr_filled", "mg_ready"))
        wo_filled, wo_drained = lsem("wo_filled"), lsem("wo_drained")
        sq2_ready, sq2_summed, root2_ready, h2_ready = (lsem(n) for n in ("sq2_ready", "sq2_summed", "root2_ready", "h2_ready"))
        lg_filled, score_ready, comb_ready, ct_filled, ct_ready, ct_written = (
            lsem(n) for n in ("lg_filled", "score_ready", "comb_ready", "ct_filled", "ct_ready", "ct_written"))
        e_gate, e_silu, e_up, e_scaled, e_hid = (lsem(n) for n in ("e_gate", "e_silu", "e_up", "e_scaled", "e_hid"))
        acc_filled, ro_ready = lsem("acc_filled"), lsem("ro_ready")
        back_filled, x_ready = lsem("back_filled"), lsem("x_ready")

        block = ctx.enter_context(nc.Block())

        class InOrder:

            def __init__(self, eng, step):
                self.eng, self.step, self.count = eng, step, {}

            def __call__(self, instruction, s=None, value=None):
                s = self.step if s is None else s
                n = self.count[id(s)] = value or self.count.get(id(s), 0) + 1
                instruction.then_inc(s, 1)
                self.eng.wait_ge(s, n)

        def layer_end(eng, name, layer):
            eng.drain().then_inc(arrived, 1)
            eng.wait_ge(released, layer + 1)
            eng.sem_inc(seen[name], 1)

        def landed(eng, n):
            eng.wait_ge(slot_filled[n % SLOTS], 16 * (n // SLOTS + 1))
            return slot[n % SLOTS][:, :]

        def raw_of(m):
            if m < S_MERGE:
                return C_IN + m
            if m < S_OUT:
                return C_MERGE + 3 * ((m - S_MERGE) // 2) + m % 2
            return C_OUT + m - S_OUT

        def round_hi(eng, do, m):
            w = landed(eng, raw_of(m))
            if m >= 2:
                eng.wait_ge(parts_used, m - 1)
            do(eng.activation(W_hi[m % 2][:, :], w, ACT.Copy), hi_ready)

        def take_lo(eng, do, m):
            eng.wait_ge(hi_ready, m + 1)
            n = raw_of(m)
            do(eng.tensor_tensor(W_lo[m % 2][:, :], slot[n % SLOTS][:, :], W_hi[m % 2][:, :].bitcast(F32), ALU.subtract),
               slot_taken[n % SLOTS], n // SLOTS + 1)

        @block.sync
        def _(eng):
            eng.dma_start(con[:, :], consts).then_inc(const_landed, 16)
            eng.dma_start(X[:, :, :], xT.rearrange("(k p) t -> p k t", p=P)).then_inc(const_landed, 16)
            with eng.Fori(0, depth) as layer:
                def fill(s, n):
                    eng.dma_start(slot[s][:, :], weights[bass.ds(layer * N_CHUNKS + n, 1), :, :]
                                  .rearrange("l p n -> (l p) n")).then_inc(slot_filled[s], 16)

                for s in range(SLOTS):
                    fill(s, s)
                eng.dma_start(mat[:, :], params[bass.ds(layer, 1), :, 0:N_MAT]
                              .rearrange("l p n -> (l p) n")).then_inc(par_landed, 16)
                eng.dma_start(vec[:, :], params[bass.ds(layer, 1), :, N_MAT:N_MAT + N_VEC]
                              .rearrange("l p n -> (l p) n")).then_inc(par_landed, 16)
                eng.dma_start(row[:, :], rows[bass.ds(layer, 1), :].to_broadcast([P, N_ROW])).then_inc(par_landed, 16)
                with eng.Fori(1, N_CHUNKS // SLOTS) as i:
                    for s in range(SLOTS):
                        eng.wait_ge(slot_taken[s], i)
                        fill(s, i * SLOTS + s)
                eng.wait_ge(arrived, 4 * layer + 4)
                eng.sem_inc(seen["sp"], 1)
                for s in layer_sems:
                    eng.sem_clear(s)
                eng.sem_inc(released, 1)
            eng.dma_start(yT.rearrange("(k p) t -> p k t", p=P), X[:, :, :]).then_inc(y_written, 16)
            eng.wait_ge(y_written, 16)

        @block.gpsimd
        def _(eng):
            do0 = InOrder(eng, pool_ready)
            for i, v in enumerate((EPS, 1e-12, GN_EPS, 0.0)):
                do0(eng.memset(epscol[:, i:i + 1], v))
            eng.wait_ge(const_landed, 32)
            for t in range(NT):
                eng.dma_start(combine_dram[N_EXP:N_EXP + SHARED, t * P:(t + 1) * P],
                              ones[0:SHARED, :]).then_inc(line_written, 16)
            eng.wait_ge(line_written, 16 * NT)
            with eng.Fori(0, depth) as layer:
                do = InOrder(eng, pool_step)
                eng.wait_ge(h_ready, 2)
                for col in (0, 1 + CTX, 2 + T):
                    do(eng.memset(RAW[:, :, col:col + 1], 0.0), raw_zeroed)
                for n, (d, c) in enumerate(SCANS):
                    for lv in range(LEVELS):
                        for g in range(2):
                            eng.wait_ge(gram_ready, 8 * n + 4 * g + 4)
                            if n or lv:
                                eng.wait_ge(y_filled, 2 * LEVELS * n + 2 * lv + g - 1)
                            if lv == 1:
                                eng.wait_ge(inv_ready, 2 * LEVELS * n + g + 1)
                            m = CON["level"] + (d * LEVELS + lv) * P
                            do(eng.tensor_tensor(BL[:, g, :].rearrange("p (u t) -> p u t", u=4),
                                                 G[:, 4 * g:4 * g + 4, 0:P],
                                                 con[:, None, m:m + P].to_broadcast([P, 4, P]), ALU.mult), block_ready)
                eng.wait_ge(ct_written, 16)
                def weight_rows(i):
                    for s in range(SLOTS):
                        eng.dma_start(CBC[:, s, :], combine_dram[bass.ds(i * SLOTS + s, 1), :]
                                      .to_broadcast([P, T])).then_inc(row_landed[s], 16)

                weight_rows(0)
                with eng.Fori(1, ROUNDS) as i:
                    eng.wait_ge(e_scaled, i * SLOTS)
                    eng.sem_inc(seen["pool"], 1)
                    weight_rows(i)
                layer_end(eng, "pool", layer)

        @block.scalar
        def _(eng):
            eng.wait_ge(const_landed, 32)
            eng.wait_ge(pool_ready, 4)
            eng.activation(csil[:, :, :], c_("cvec", 2 * KD).rearrange("p (k g) -> p k g", g=2),
                           ACT.Silu).then_inc(csil_ready, 1)
            with eng.Fori(0, depth) as layer:
                do = InOrder(eng, act_step)

                def norm_input(squares, SQ, summed, root, RS):
                    do(eng.activation(SQ[:, :, :], X[:, :, :], ACT.Square), squares)
                    eng.wait_ge(summed, 1)
                    do(eng.activation(RS, ps[:, 1, 0:T], ACT.Sqrt, bias=epscol[:, 0:1], scale=1.0 / D), root)

                def mod_rows(c, bank):
                    eng.wait_ge(mod_row_filled, c + 1)
                    do(eng.activation(mod_row[:, c % 2, :], ps[0:2, bank, 0:3 * P], ACT.Copy), mod_row_ready)

                for c in range(MOD_A):
                    mod_rows(c, 2 + c % 2)
                norm_input(sq_ready, SQ8, sq_summed, root_ready, RS1)
                round_hi(eng, do, 0)
                round_hi(eng, do, 1)
                for c in range(10):
                    if c == 4:
                        for j in range(5):
                            eng.wait_ge(qsq_summed, j + 1)
                            do(eng.activation(RS5[:, j, :], ps[:, 4 + j % 4, 0:T], ACT.Sqrt, bias=epscol[:, 0:1],
                                              scale=1.0 / HD), qroot_ready)
                    for n, dst, func in zip(Z_ACT, (XG, XW, XA), (ACT.Sigmoid, ACT.Tanh, ACT.Copy)):
                        if n in Z_OF[c]:
                            eng.wait_ge(z_filled, n + 1)
                            do(eng.activation(dst, ps[:, n % 4, 0:T], func), z_act)
                    if c == 2:
                        eng.wait_ge(z_dve, 5)
                        do(eng.activation(SQ5, QK, ACT.Square), qsq_ready)
                    if c + 2 < 10:
                        round_hi(eng, do, c + 2)
                eng.wait_ge(kout_filled, 1)
                do(eng.activation(KOUT, ps[:, 7, 0:P], ACT.Copy), kout_ready)
                eng.dma_start(new_k[bass.ds(layer, 1), :, :].rearrange("l t n -> (l t) n"), KOUT).then_inc(kv_written, 16)
                eng.dma_start(new_v[bass.ds(layer, 1), :, :].rearrange("l t n -> (l t) n"), VT[:, 0, :]).then_inc(kv_written, 16)
                for u in range(24 + 2):
                    if u < 24:
                        n = P if u % NT == 0 else T
                        eng.wait_ge(s_max, u + 1)
                        if u >= 3:
                            eng.wait_ge(pt_filled, u - 2)
                        do(eng.activation(PM[:, u % 3, 0:n], ps[:, 4 + u % 3, 0:n], ACT.Exp,
                                          bias=att_small[:, 1, u:u + 1], scale=HD ** -0.5,
                                          accum_out=att_small[:, 2, u:u + 1]), p_exp)
                    if u >= 2:
                        w = u - 2
                        n = P if w % NT == 0 else T
                        eng.wait_ge(pt_filled, w + 1)
                        if w >= 2:
                            eng.wait_ge(pv_filled, w - 1)
                        do(eng.activation(PTS[:, w % 2, 0:n], ps[:, (7, 3)[w % 2], 0:n], ACT.Copy), pt_ready)
                eng.wait_ge(kv_written, 32)
                eng.wait_ge(pv_filled, 24)
                eng.wait_ge(oattn_ready, 4)
                for t in range(NT):
                    do(eng.activation(SSQ, SV[:, t, :], ACT.Square, accum_out=small[:, t:t + 1]))
                do(eng.activation(small[:, 4:7], small[:, 0:3], ACT.Sqrt, bias=epscol[:, 0:1], scale=1.0 / 512), sv_root)
                eng.wait_ge(kksq_ready, 1)
                for j in range(QT):
                    eng.wait_ge(kk_summed, j + 1)
                    do(eng.activation(G[:, 4 + j, 0:CVW - 1], ps[:, 4 + j, 0:CVW - 1], ACT.Sqrt, bias=epscol[:, 1:2]), kk_root)
                for c in range(NT):
                    eng.wait_ge(vtm_filled, c + 1)
                    do(eng.activation(VTM[:, c, :], ps[:, c, :], ACT.Copy), vtm_ready)
                for n, (d, c) in enumerate(SCANS):
                    eng.wait_ge(wa_filled, n + 1)
                    if n:
                        eng.wait_ge(os_filled, n)
                    for j in range(QT):
                        do(eng.activation(SG[:, j, :], ps[:, 0, j * P:(j + 1) * P], ACT.Sigmoid,
                                          bias=v_("w0", d * 4 + j)))
                    for j in range(QT):
                        do(eng.activation(SA[:, j, :], ps[:, 1, j * P:(j + 1) * P], ACT.Sigmoid,
                                          bias=v_("a0", d * 4 + j)), gate_ready)
                    eng.wait_ge(cum_ready, n + 1)
                    do(eng.activation(EP, CUM, ACT.Exp, scale=-DECAY))
                    do(eng.activation(CUM, CUM, ACT.Exp, scale=DECAY))
                    do(eng.activation(CX, CX, ACT.Exp, scale=-DECAY))
                    do(eng.activation(EH, HALF, ACT.Exp, scale=-DECAY), exp_ready)
                    for c2 in range(2 * n, min(2 * n + 2, MOD_B)):
                        mod_rows(MOD_A + c2, 6 + c2 % 2)
                    eng.wait_ge(tm_filled, n + 1)
                    do(eng.activation(BTM, ps[:, 2, :], ACT.Copy), tm_ready)
                    do(eng.activation(KTM, ps[:, 3, :], ACT.Copy), tm_ready)
                    for lv in range(1, LEVELS):
                        for g in range(2):
                            eng.wait_ge(y_filled, 2 * LEVELS * n + 2 * lv + g + 1)
                            do(eng.activation(YS[:, g, :], ps[:, g, :], ACT.Copy), y_ready)
                    eng.wait_ge(r_filled, n + 1)
                    for hh, b in enumerate((2, 0)):
                        do(eng.activation(RSB.rearrange("p (j h i) -> p j h i", j=QT, h=2)[:, :, hh, :],
                                          ps[:, b, 0:QT * HD].rearrange("p (j i) -> p j i", j=QT), ACT.Copy), r_ready)
                    eng.wait_ge(u_filled, n + 1)
                    do(eng.activation(USB, ps[:, 3, :], ACT.Copy, scale=-1.0), u_ready)
                eng.dma_start(new_s[bass.ds(layer, 1), :, :].rearrange("l p n -> (l p) n"),
                              SOUT.rearrange("p d n -> p (d n)")).then_inc(state_written, 16)
                for j in range(QT):
                    eng.wait_ge(gn_summed, QT + j + 1)
                    do(eng.activation(E_RS[:, j, :], ps[:, 4 + j, 0:T], ACT.Sqrt, bias=epscol[:, 2:3], scale=1.0 / HD), gn_root)
                eng.wait_ge(orwkv_ready, QT)
                eng.wait_ge(state_written, 16)
                round_hi(eng, do, S_MERGE)
                round_hi(eng, do, S_MERGE + 1)
                for n in range(KD):
                    for b in range(3):
                        eng.wait_ge(g_filled, 3 * n + b + 1)
                        if n >= 2:
                            eng.wait_ge(mg_ready, n - 1)
                        do(eng.activation(GT[:, n % 2, b, :], ps[:, b, 0:T], ACT.Sigmoid), g_ready)
                    round_hi(eng, do, S_MERGE + n + 2)
                round_hi(eng, do, S_OUT + 2)
                round_hi(eng, do, S_OUT + 3)
                eng.wait_ge(wo_drained, 2 * KD)
                norm_input(sq2_ready, R_SQ8, sq2_summed, root2_ready, R_RS1)
                eng.wait_ge(lg_filled, 1)
                do(eng.activation(SC, ps[:, 0, 0:NT * N_EXP].rearrange("p (t e) -> p t e", t=NT), ACT.Sigmoid), score_ready)
                eng.wait_ge(ct_ready, 1)
                eng.wait_ge(line_written, 16 * NT)
                eng.dma_start(combine_dram[0:N_EXP, :], CT[0:N_EXP, :]).then_inc(ct_written, 16)
                def hi_part(i, s, part, used, count):
                    e = i * SLOTS + s
                    if part == 0:
                        eng.wait_ge(slot_filled[s], i * 16 + 16 * (C_EXP // SLOTS + 1))
                    if not (isinstance(e, int) and e < 2):
                        eng.wait_ge(used, e + (count - 2))
                    o = slice(part * D, (part + 1) * D)
                    eng.activation(W_hi[s][:, o], slot[s][:, o], ACT.Copy).then_inc(e_hi, 1)

                def act_expert(i, s, split=True):
                    e, (j, q) = i * SLOTS + s, ((i, 1) if s == 0 else (i + 1, 0))
                    if split:
                        hi_part(j, q, 0, e_gate, 1)
                    if not (isinstance(e, int) and e < 2):
                        eng.wait_ge(e_scaled, e - 1)
                    eng.wait_ge(e_gate, e + 1)
                    eng.activation(SGS[:, s, :], ps[:, 6, 0:T], ACT.Silu).then_inc(e_silu, 1)
                    if split:
                        hi_part(j, q, 1, e_up, 1)
                        hi_part(j, q, 2, e_down, 1)

                eng.wait_ge(parts_used, S_EXP)
                for part in range(3):
                    hi_part(0, 0, part, None, 0)
                for s in range(SLOTS):
                    act_expert(0, s)
                with eng.Fori(1, ROUNDS - 1) as i:
                    for s in range(SLOTS):
                        act_expert(i, s)
                for s in range(SLOTS):
                    act_expert(ROUNDS - 1, s, split=(s == 0))
                layer_end(eng, "act", layer)

        @block.vector
        def _(eng):
            eng.wait_ge(const_landed, 32)
            with eng.Fori(0, depth) as layer:
                do = InOrder(eng, dve_step)

                def sum2(out, a, b, op=ALU.add, s=None):
                    do(eng.tensor_tensor(out, a, b, op), s)

                eng.wait_ge(par_landed, 48)
                eng.wait_ge(mod_filled, 1)
                def add_mod_b(a, b, bank, col, s=None):
                    do(eng.tensor_tensor(mod[:, a:b, :], ps[:, bank, col:col + 2 * (b - a)].rearrange("p (m g) -> p m g", g=2),
                                         v_("mod_b", a, b - a)[:, :, None].to_broadcast([P, b - a, 2]), ALU.add), s)

                def amplitude(i, g, m):
                    do(eng.tensor_scalar(amp[:, i, :, :], mod[:, m * KD:(m + 1) * KD, :], 1.0, None, ALU.add))
                    do(eng.tensor_tensor(amp[:, i, :, :], amp[:, i, :, :],
                                         v_(g, 0, KD)[:, :, None].to_broadcast([P, KD, 2]), ALU.mult))

                add_mod_b(0, 3 * MOD_A, 0, 0)
                amplitude(0, "g1", 1)

                def modulated(i, shift, root, RS, H, ready):
                    eng.wait_ge(root, 1)
                    do(eng.reciprocal(RS, RS))
                    do(eng.tensor_tensor(H, X[:, :, :], RS[:, None, :].to_broadcast([P, KD, T]), ALU.mult))
                    for g, (a, b) in enumerate(GROUPS):
                        for k in range(KD):
                            do(eng.tensor_scalar(H[:, k, a:b], H[:, k, a:b], amp[:, i, k, g:g + 1],
                                                 mod[:, shift * KD + k, g:g + 1], ALU.mult, ALU.add))
                    do(eng.tensor_copy(H_hi[:, :, :], H), ready)
                    do(eng.tensor_tensor(H_lo[:, :, :], H, H_hi[:, :, :].bitcast(F32), ALU.subtract), ready)

                modulated(0, 0, root_ready, RS1, H1, h_ready)
                take_lo(eng, do, 0)
                take_lo(eng, do, 1)
                def out_of(n, dst, src):
                    eng.wait_ge(z_filled, n + 1)
                    do(eng.tensor_copy(dst, src), z_dve)

                for c in range(10):
                    for n in Z_OF[c]:
                        bank = ps[:, n % 4, :]
                        if n < 5:
                            out_of(n, QK[:, n, :], bank[:, 0:T])
                        elif n == 5:
                            out_of(n, VT, bank[:, 0:T].rearrange("p (t n) -> p t n", t=NT))
                        elif n < 10:
                            out_of(n, SU[:, n - 6, :], bank[:, 0:T])
                        elif n < 13:
                            out_of(n, SV[:, n - 10, 0:256], bank[:, 0:256])
                        elif n < 16:
                            out_of(n, SV[:, n - 13, 256:512], bank[:, 0:256])
                        elif n not in Z_ACT:
                            if n == 17:
                                eng.wait_ge(raw_zeroed, 3)
                            eng.wait_ge(z_filled, n + 1)
                            do(eng.tensor_copy(RAW[:, n - 17, 1:1 + CTX], bank[:, 0:CTX]))
                            do(eng.tensor_copy(RAW[:, n - 17, 2 + CTX:2 + T], bank[:, CTX:T]), z_dve)
                    if c + 2 < 10:
                        take_lo(eng, do, c + 2)
                    if 5 <= c:
                        eng.wait_ge(qroot_ready, 5)
                        do(eng.reciprocal(RS5[:, c - 5, :], RS5[:, c - 5, :]))
                do(eng.scalar_tensor_tensor(QK[:, 0:4, :], QK[:, 0:4, :], v_("qn"), RS5[:, 0:4, :], ALU.mult, ALU.mult))
                do(eng.scalar_tensor_tensor(QK[:, 4, :], QK[:, 4, :], v_("kn"), RS5[:, 4, :], ALU.mult, ALU.mult), qk_normed)
                eng.wait_ge(rot_filled, 5)
                for j in range(5):
                    b, o = 4 + j // 2, (j % 2) * LAT
                    do(eng.tensor_tensor(SQ5[:, j, CTX:T], QK[:, j, CTX:T], cos, ALU.mult))
                    do(eng.tensor_tensor(ROT5[:, j, :], ps[:, b, o:o + LAT], sin, ALU.mult))
                do(eng.tensor_tensor(QK[:, :, CTX:T], SQ5[:, :, CTX:T], ROT5, ALU.add), qk_ready)
                for u in range(24 + 9):
                    if u < 24:
                        n = P if u % NT == 0 else T
                        eng.wait_ge(s_filled, u + 1)
                        do(eng.tensor_reduce(att_small[:, 0, u:u + 1], ps[:, 4 + u % 3, 0:n], AX, ALU.max))
                        do(eng.tensor_scalar(att_small[:, 1, u:u + 1], att_small[:, 0, u:u + 1], -HD ** -0.5, None,
                                             ALU.mult), s_max)
                    if 1 <= u <= 24:
                        w = u - 1
                        n = P if w % NT == 0 else T
                        eng.wait_ge(p_exp, w + 1)
                        do(eng.reciprocal(att_small[:, 3, w:w + 1], att_small[:, 2, w:w + 1]))
                        do(eng.tensor_scalar(PM[:, w % 3, 0:n], PM[:, w % 3, 0:n], att_small[:, 3, w:w + 1], None,
                                             ALU.mult), p_ready)
                    if u >= 9 and (u - 9) % 6 == 0 and (u - 9) // 6 < 4:
                        j = (u - 9) // 6
                        eng.wait_ge(pv_filled, 6 * j + 6)
                        do(eng.tensor_copy(o_attn[:, j, :], ps[:, j % 2, 0:T]), oattn_ready)
                eng.wait_ge(sv_root, 1)
                do(eng.reciprocal(small[:, 8:11], small[:, 4:7]))
                for t in range(NT):
                    do(eng.tensor_scalar(SV[:, t, :], SV[:, t, :], small[:, 8 + t:9 + t], None, ALU.mult), sv_normed)
                for g in range(4):
                    eng.wait_ge(sgu_filled, g + 1)
                    do(eng.scalar_tensor_tensor(SGT, ps[:, g % 2, 0:T].rearrange("p (t i) -> p t i", t=NT),
                                                v_("sgu_g", g),
                                                row[:, None, ROW["sgu_b"] + g * P:ROW["sgu_b"] + (g + 1) * P]
                                                .to_broadcast([P, NT, P]), ALU.mult, ALU.add), sgu_drained)
                    do(eng.tensor_tensor(o_sgu[:, g, :], SGT.rearrange("p t i -> p (t i)"), SU[:, g, :], ALU.mult))
                for j in range(12):
                    w = [v_("conv", i * 12 + j) for i in range(3)]
                    o = CV[:, j, 0:CVW - 1]
                    do(eng.tensor_scalar(o, RAW[:, j, 0:385], w[0], None, ALU.mult))
                    do(eng.scalar_tensor_tensor(o, RAW[:, j, 1:386], w[1], o, ALU.mult, ALU.add))
                    do(eng.scalar_tensor_tensor(o, RAW[:, j, 2:387], w[2], o, ALU.mult, ALU.add), cv_ready)
                R_, K_, V_ = CV[:, 0:4, :], CV[:, 4:8, :], CV[:, 8:12, :]
                W1 = CVW - 1
                for j in range(QT):
                    do(eng.tensor_scalar(KK[:, j, 0:W1], K_[:, j, 0:W1], v_("k_k", j), None, ALU.mult))
                do(eng.tensor_tensor(G[:, 0:4, 0:W1], KK[:, :, 0:W1], KK[:, :, 0:W1], ALU.mult), kksq_ready)
                eng.wait_ge(kk_root, 4)
                do(eng.reciprocal(G[:, 4:8, 0:W1], G[:, 4:8, 0:W1]))
                do(eng.tensor_tensor(KK[:, :, 0:W1], KK[:, :, 0:W1], G[:, 4:8, 0:W1], ALU.mult), kk_ready)
                do(eng.tensor_copy(SL, m_("state0").rearrange("p (d n) -> p d n", d=2)))
                do(eng.tensor_scalar(small[:, 16:20], v_("k_a", 0, 4), -1.0, 1.0, ALU.mult, ALU.add))
                for n, (d, c) in enumerate(SCANS):
                    a, b = CV_AT[c], CV_AT[c] + P
                    first = c not in [x[1] for x in SCANS[:n]]
                    eng.wait_ge(gate_ready, 4 * n + 4)
                    for j in range(QT):
                        src, dst, one = SG[:, j, :], CUM[:, j, :], ones
                        if d:
                            src, dst, one = src[:, ::-1], dst[:, ::-1], one[:, ::-1]
                        do(eng.tensor_tensor_scan(dst, one, src, 0.0, ALU.mult, ALU.add))
                    last = CUM[:, :, 0:1] if d else CUM[:, :, P - 1:P]
                    do(eng.tensor_scalar(HALF[:, :, None], last, 0.5, None, ALU.mult))
                    do(eng.tensor_tensor(CUM, CUM, HALF[:, :, None].to_broadcast([P, QT, P]), ALU.subtract))
                    do(eng.tensor_tensor(CX, CUM, SG, ALU.subtract), cum_ready)
                    eng.wait_ge(exp_ready, n + 1)
                    do(eng.tensor_tensor(AR[:, :, 0:P], KK[:, :, a:b], CX, ALU.mult))
                    do(eng.tensor_tensor(AR[:, :, P:2 * P], R_[:, :, a:b], EP, ALU.mult))
                    do(eng.tensor_tensor(BE, SA, CUM, ALU.mult))
                    do(eng.tensor_tensor(BE, BE, KK[:, :, a:b], ALU.mult))
                    for j in range(QT):
                        do(eng.tensor_scalar(SA[:, j, :], SA[:, j, :], v_("k_a", j), small[:, 16 + j:17 + j],
                                             ALU.mult, ALU.add))
                    do(eng.tensor_tensor(SA, SA, K_[:, :, a:b], ALU.mult))
                    if first:
                        do(eng.tensor_copy(KS[:, :, a:b], SA))
                    else:
                        do(eng.tensor_tensor(KS[:, :, a:b], KS[:, :, a:b], SA, ALU.add))
                    do(eng.tensor_tensor(KA, SA, CUM, ALU.mult), keys_ready)
                    if 2 * n < MOD_B:
                        eng.wait_ge(modb_filled, n + 1)
                        add_mod_b(3 * (MOD_A + 2 * n), 3 * (MOD_A + 2 * n + 2), 5, 0, modb_ready)
                    if c:
                        do(eng.tensor_tensor(SH, SL[:, d, :].rearrange("p (j i) -> p j i", j=QT),
                                             EH[:, :, None].to_broadcast([P, QT, HD]), ALU.mult), sh_ready)
                    mask = con[:, None, CON["causal"] + d * 2 * P:CON["causal"] + (d + 1) * 2 * P].to_broadcast([P, 2, 2 * P])
                    for u in range(8):
                        eng.wait_ge(gram_filled, 8 * n + u + 1)
                        do(eng.tensor_tensor(G[:, u, :].rearrange("p (a t) -> p a t", a=2),
                                             ps[:, 4 + u % 4, :].rearrange("p (a t) -> p a t", a=2), mask, ALU.mult), gram_ready)
                    for lv in range(LEVELS):
                        for g in range(2):
                            XG4 = XX[:, 4 * g:4 * g + 4, :, :]
                            k = 2 * LEVELS * n + 2 * lv + g + 1
                            if lv == 0:
                                eng.wait_ge(y_filled, k)
                                eye = ident[:, None, :].to_broadcast([P, 4, P])
                                do(eng.tensor_tensor(XG4[:, :, 0, :], eye, ps[:, g, :].rearrange("p (u t) -> p u t", u=4), ALU.subtract))
                                do(eng.tensor_tensor(XG4[:, :, 1, :], eye, BL[:, g, :].rearrange("p (u t) -> p u t", u=4),
                                                     ALU.subtract), inv_ready)
                            elif lv < LEVELS - 1:
                                eng.wait_ge(xy_filled, 2 * (LEVELS - 1) * n + 2 * (lv - 1) + g + 1)
                                do(eng.tensor_tensor(XG4, XG4, ps[:, 4 + 2 * g:6 + 2 * g, :].rearrange(
                                    "p a (u x t) -> p (a u) x t", u=2, x=2), ALU.subtract), inv_ready)
                            else:
                                eng.wait_ge(xy_filled, 2 * (LEVELS - 1) * n + 2 * (lv - 1) + g + 1)
                                do(eng.tensor_tensor(XG4[:, :, 1, :], XG4[:, :, 1, :], ps[:, 4 + 2 * g, :].rearrange(
                                    "p (u t) -> p u t", u=4), ALU.subtract), inv_ready)
                    eng.wait_ge(os_filled, n + 1)
                    O_ = o_rwkv[:, :, c * P:(c + 1) * P]
                    src = ps[:, 4, :].rearrange("p (j t) -> p j t", j=QT)
                    do(eng.tensor_copy(O_, src)) if first else do(eng.tensor_tensor(O_, O_, src, ALU.add))
                    to = (SOUT if c == 0 else SL)[:, d, :].rearrange("p (j i) -> p j i", j=QT)
                    src = ps[:, 5, 0:QT * HD].rearrange("p (j i) -> p j i", j=QT)
                    if c:
                        do(eng.tensor_tensor(SH, SH, src, ALU.add))
                        src = SH
                    do(eng.tensor_tensor(to, src, EH[:, :, None].to_broadcast([P, QT, HD]), ALU.mult), state_ready)
                do(eng.tensor_copy(E_B, o_rwkv[:, :, :]), gn_ready)
                for j in range(QT):
                    eng.wait_ge(gn_summed, j + 1)
                    do(eng.scalar_tensor_tensor(E_B[:, j, :], ps[:, j, 0:T], -1.0 / HD, E_B[:, j, :], ALU.mult, ALU.add))
                do(eng.tensor_tensor(E_SQ, E_B, E_B, ALU.mult), gn_ready)
                eng.wait_ge(gn_root, QT)
                do(eng.reciprocal(E_RS, E_RS))
                do(eng.tensor_tensor(E_B, E_B, E_RS, ALU.mult))
                for j in range(QT):
                    do(eng.tensor_scalar(E_B[:, j, :], E_B[:, j, :], v_("ln_g", j), v_("ln_b", j), ALU.mult, ALU.add), gn_done)
                for j in range(QT):
                    for (a, b), o in zip(GROUPS, (0, 129)):
                        do(eng.scalar_tensor_tensor(E_SQ[:, j, a:b], R_[:, j, o:o + b - a], v_("r_k", j),
                                                    KS[:, j, o:o + b - a], ALU.mult, ALU.mult), bonus_ready)
                for j in range(QT):
                    eng.wait_ge(gn_summed, 2 * QT + j + 1)
                    for (a, b), o in zip(GROUPS, (0, 129)):
                        do(eng.tensor_tensor(E_RS[:, j, a:b], ps[:, j, a:b], V_[:, j, o:o + b - a], ALU.mult))
                    do(eng.tensor_tensor(E_B[:, j, :], E_B[:, j, :], E_RS[:, j, :], ALU.add))
                for j in range(QT):
                    eng.wait_ge(gn_summed, 3 * QT + j + 1)
                    do(eng.tensor_tensor(o_rwkv[:, j, :], E_B[:, j, :], ps[:, 4 + j, 0:T], ALU.mult), orwkv_ready)
                take_lo(eng, do, S_MERGE)
                take_lo(eng, do, S_MERGE + 1)
                for n in range(KD):
                    eng.wait_ge(g_ready, 3 * n + 3)
                    for b in range(3):
                        eng.wait_ge(pr_filled, 3 * n + b + 1)
                        do(eng.tensor_tensor(MT[:, b, :], ps[:, 3 + b, 0:T], GT[:, n % 2, b, :], ALU.mult))
                    do(eng.tensor_tensor(MT[:, 0, :], MT[:, 0, :], MT[:, 1, :], ALU.add))
                    do(eng.tensor_tensor(MT[:, 0, :], MT[:, 0, :], MT[:, 2, :], ALU.add))
                    do(eng.tensor_copy(MG_hi[:, n, :], MT[:, 0, :]))
                    do(eng.tensor_tensor(MG_lo[:, n, :], MT[:, 0, :], MG_hi[:, n, :].bitcast(F32), ALU.subtract), mg_ready)
                    take_lo(eng, do, S_MERGE + n + 2)
                amplitude(1, "g2n", 4)

                def residual(n, gate, src, s):
                    for g, (a, b) in enumerate(GROUPS):
                        do(eng.scalar_tensor_tensor(X[:, n, a:b], src[:, a:b], mod[:, gate * KD + n, g:g + 1],
                                                    X[:, n, a:b], ALU.mult, ALU.add), s)

                for n in range(KD):
                    eng.wait_ge(wo_filled, n + 1)
                    residual(n, 2, ps[:, 6 + n % 2, :], wo_drained)
                    if n % 2 and n < 4:
                        take_lo(eng, do, S_OUT + 2 + n // 2)
                modulated(1, 3, root2_ready, R_RS1, H2, h2_ready)
                eng.wait_ge(score_ready, 1)
                do(eng.tensor_tensor(BI, SC, row[:, None, ROW["router_b"]:ROW["router_b"] + N_EXP]
                                     .to_broadcast([P, NT, N_EXP]), ALU.add))
                for t in range(NT):
                    do(eng.max(TOPV[:, t, :], BI[:, t, :]))
                    do(eng.max_index(topi[:, t, :], TOPV[:, t, :], BI[:, t, :]))
                do(eng.tensor_copy(TOPF, topi[:, :, :]))
                for t in range(NT):
                    do(eng.tensor_tensor(EQ, c_("iota", N_EXP)[:, None, :].to_broadcast([P, TOP_K, N_EXP]),
                                         TOPF[:, t, 0:TOP_K, None].to_broadcast([P, TOP_K, N_EXP]), ALU.is_equal))
                    do(eng.tensor_reduce(CB[:, t, :], EQ.rearrange("p k e -> p e k"), AX, ALU.add))
                do(eng.tensor_tensor(CB, CB, SC, ALU.mult))
                do(eng.tensor_reduce(small[:, 24:27], CB, AX, ALU.add))
                do(eng.reciprocal(small[:, 28:31], small[:, 24:27]))
                for t in range(NT):
                    do(eng.tensor_scalar(CB[:, t, :], CB[:, t, :], small[:, 28 + t:29 + t], ROUTED_SCALE,
                                         ALU.mult, ALU.mult), comb_ready)
                eng.wait_ge(ct_filled, 1)
                do(eng.tensor_copy(CT[0:N_EXP, :], ps[0:N_EXP, 1, 0:T]), ct_ready)
                def lo_part(i, s, part):
                    o = slice(part * D, (part + 1) * D)
                    eng.wait_ge(e_hi, (i * SLOTS + s) * 3 + part + 1)
                    eng.tensor_tensor(W_lo[s][:, o], slot[s][:, o], W_hi[s][:, o].bitcast(F32), ALU.subtract)\
                       .then_inc(slot_taken[s] if part == 2 else e_lo, 1)

                def dve_expert(i, s, split=True):
                    e, (j, q) = i * SLOTS + s, ((i, 1) if s == 0 else (i + 1, 0))
                    if split:
                        lo_part(j, q, 0)
                    eng.wait_ge(row_landed[s], layer * (16 * ROUNDS) + i * 16 + 16)
                    eng.wait_ge(e_silu, e + 1)
                    eng.tensor_tensor(TS[:, s, :], SGS[:, s, :], CBC[:, s, :], ALU.mult).then_inc(e_scaled, 1)
                    if split:
                        lo_part(j, q, 1)
                    eng.wait_ge(e_scaled, e + 1)
                    eng.wait_ge(e_up, e + 1)
                    eng.tensor_tensor(TS[:, s, :], TS[:, s, :], ps[:, 7, 0:T], ALU.mult).then_inc(e_prod, 1)
                    if not (isinstance(e, int) and e < 2):
                        eng.wait_ge(e_down, e - 1)
                    eng.wait_ge(e_prod, e + 1)
                    eng.tensor_copy(HID_hi[:, s, :], TS[:, s, :]).then_inc(e_hid_hi, 1)
                    eng.wait_ge(e_hid_hi, e + 1)
                    eng.tensor_tensor(HID_lo[:, s, :], TS[:, s, :], HID_hi[:, s, :].bitcast(F32), ALU.subtract)\
                       .then_inc(e_hid, 1)
                    if split:
                        lo_part(j, q, 2)

                for part in range(3):
                    lo_part(0, 0, part)
                for s in range(SLOTS):
                    dve_expert(0, s)
                with eng.Fori(1, ROUNDS - 1) as i:
                    for s in range(SLOTS):
                        dve_expert(i, s)
                for s in range(SLOTS):
                    dve_expert(ROUNDS - 1, s, split=(s == 0))
                eng.wait_ge(acc_filled, 1)
                for t in range(NT):
                    do(eng.tensor_copy(RO[:, t, :], ps[:, 2 * t:2 * t + 2, :].rearrange("p a b -> p (a b)")), ro_ready)
                for n in range(KD):
                    eng.wait_ge(back_filled, n + 1)
                    residual(n, 5, ps[:, 6 + n % 2, :], x_ready)
                layer_end(eng, "dve", layer)

        @block.tensor
        def _(eng):
            eng.wait_ge(const_landed, 32)
            eng.wait_ge(csil_ready, 1)
            with eng.Fori(0, depth) as layer:
                owed = []

                def release(n):
                    owed.append(parts_used)

                def matmul(*args, **kw):
                    mm = eng.matmul(*args, **kw)
                    if owed:
                        mm.then_inc(owed.pop(0), 1)
                    return mm

                def parts(m):
                    n = raw_of(m)
                    eng.wait_ge(slot_taken[n % SLOTS], n // SLOTS + 1)
                    return tuple(w[m % 2][:, :].rearrange("p (k n) -> p k n", k=KD) for w in (W_hi, W_lo))

                def product(out, w, act, k_n=KD, swap=False):
                    n = 0
                    for k in range(k_n):
                        for a_, b_ in ((1, 0), (0, 1), (0, 0)):
                            x, y = w[a_](k), act[b_](k)
                            mm = matmul(out, *((y, x) if swap else (x, y)), start=(n == 0), stop=(n == 3 * k_n - 1))
                            n += 1
                    return mm

                def mod_chunk(c, bank):
                    n = C_MOD + c if c < MOD_A else C_MODB + c - MOD_A
                    w = landed(eng, n).rearrange("p (k n) -> p k n", k=KD)
                    for k in range(KD):
                        mm = matmul(ps[0:2, bank, 0:3 * P], csil[:, k, :], w[:, k, :], start=(k == 0), stop=(k == KD - 1))
                    mm.then_inc(mod_row_filled, 1)
                    owed.append(slot_taken[n % SLOTS])

                def mod_turn(c, bank, col):
                    eng.wait_ge(mod_row_ready, c + 1)
                    for m in range(3):
                        mm = matmul(ps[:, bank, col + 2 * m:col + 2 * m + 2], mod_row[:, c % 2, m * P:(m + 1) * P],
                                    ident[0:2, 0:2], start=True, stop=True)
                    return mm

                for c in range(MOD_A):
                    mod_chunk(c, 2 + c % 2)
                    if c:
                        mod_turn(c - 1, 0, 6 * (c - 1))
                mod_turn(MOD_A - 1, 0, 6 * (MOD_A - 1)).then_inc(mod_filled, 1)
                eng.wait_ge(sq_ready, 1)
                for k in range(KD):
                    mm = matmul(ps[:, 1, 0:T], ones, SQ8[:, k, :], start=(k == 0), stop=(k == KD - 1))
                mm.then_inc(sq_summed, 1)
                eng.wait_ge(h_ready, 2)
                Z = {}

                def z_bank(n):
                    m = n - 4
                    if m in Z_ACT:
                        eng.wait_ge(z_act, Z_ACT.index(m) + 1)
                    elif m >= 0:
                        eng.wait_ge(z_dve, len([x for x in range(m + 1) if x not in Z_ACT]))
                    return n % 4

                def columns(w, col, width=P):
                    return tuple(lambda k, x=x: x[:, k, col:col + width] for x in w)

                def tokens(a_, b_):
                    return tuple(lambda k, x=x: x[:, k, a_:b_] for x in (H_hi, H_lo))

                def z_tile(n, w, col):
                    product(ps[:, z_bank(n), 0:T], columns(w, col), tokens(0, T)).then_inc(z_filled, 1)

                def z_tokens(b, at_, t, w, col, width):
                    return product(ps[:, b, at_:at_ + width], columns(w, col, width), tokens(t * P, (t + 1) * P), swap=True)

                for c in range(10):
                    w = parts(S_IN + c)
                    if c == 1:
                        z_tile(3, w, 0)
                        z_tile(4, w, P)
                        b = z_bank(5)
                        for t in range(NT):
                            mm = z_tokens(b, t * P, t, w, 2 * P, P)
                        mm.then_inc(z_filled, 1)
                    elif c == 3:
                        z_tile(9, w, 0)
                        for t in range(NT):
                            z_tokens(z_bank(10 + t), 0, t, w, P, 2 * P).then_inc(z_filled, 1)
                    elif c == 4:
                        for t in range(NT):
                            z_tokens(z_bank(13 + t), 0, t, w, 0, 2 * P).then_inc(z_filled, 1)
                        z_tile(16, w, 2 * P)
                    else:
                        for m, n in enumerate(Z_OF[c]):
                            z_tile(n, w, m * P)
                    release(S_IN + c)
                    if c == 3:
                        eng.drain().then_inc(owed.pop(0), 1)
                        eng.wait_ge(qsq_ready, 1)
                        for j in range(5):
                            if j == 4:
                                eng.wait_ge(qroot_ready, 1)
                            matmul(ps[:, 4 + j % 4, 0:T], heads, SQ5[:, j, :], start=True, stop=True).then_inc(qsq_summed, 1)
                eng.drain().then_inc(owed.pop(0), 1)
                eng.wait_ge(qk_normed, 1)
                eng.transpose(ps[:, 7, 0:P], QK[:, 4, 0:CTX], ident).then_inc(kout_filled, 1)
                for j in range(5):
                    matmul(ps[:, 4 + j // 2, (j % 2) * LAT:(j % 2 + 1) * LAT], rot, QK[:, j, CTX:T],
                               start=True, stop=True).then_inc(rot_filled, 1)
                eng.wait_ge(qk_ready, 1)
                eng.wait_ge(kout_ready, 1)
                eng.wait_ge(z_act, 3)
                eng.wait_ge(z_dve, 28)
                units = [(j, hh, t) for j in range(QT) for hh in range(2) for t in range(NT)]

                def scores(u):
                    j, hh, t = units[u]
                    r = slice(hh * HD, (hh + 1) * HD)
                    if u >= 3:
                        eng.wait_ge(p_exp, u - 2)
                    q = QK[r, j, t * P:(t + 1) * P]
                    b = 4 + u % 3
                    if t == 0:
                        mm = matmul(ps[:, b, 0:P], q, QK[r, 4, 0:CTX], start=True, stop=True)
                    else:
                        matmul(ps[:, b, 0:P], q, m_("ctx_kT", P)[r, :], start=True, stop=True)
                        mm = matmul(ps[:, b, P:T], q, QK[r, 4, CTX:T], start=True, stop=True)
                    mm.then_inc(s_filled, 1)

                def turn(u):
                    t = units[u][2]
                    eng.wait_ge(p_ready, u + 1)
                    if u >= 2:
                        eng.wait_ge(pt_ready, u - 1)
                    for kb in range(1 if t == 0 else NT):
                        mm = eng.transpose(ps[:, (7, 3)[u % 2], kb * P:(kb + 1) * P], PM[:, u % 3, kb * P:(kb + 1) * P], ident)
                    mm.then_inc(pt_filled, 1)

                def values(u):
                    j, hh, t = units[u]
                    r = slice(hh * HD, (hh + 1) * HD)
                    eng.wait_ge(pt_ready, u + 1)
                    if j >= 2 and hh == 0 and t == 0:
                        eng.wait_ge(oattn_ready, j - 1)
                    v = [VT[:, 0, r]] if t == 0 else [m_("ctx_v", P)[:, r], VT[:, 1, r], VT[:, 2, r]]
                    for kb, vb in enumerate(v):
                        mm = matmul(ps[r, j % 2, t * P:(t + 1) * P], vb, PTS[:, u % 2, kb * P:(kb + 1) * P],
                                        start=(kb == 0), stop=(kb == len(v) - 1))
                    mm.then_inc(pv_filled, 1)

                for u in range(24 + 3):
                    if u < 24:
                        scores(u)
                    if 2 <= u < 26:
                        turn(u - 2)
                    if u >= 3:
                        values(u - 3)
                eng.wait_ge(sv_normed, NT)
                eng.wait_ge(oattn_ready, 4)
                for g in range(4):
                    if g >= 2:
                        eng.wait_ge(sgu_drained, g - 1)
                    for t in range(NT):
                        mm = matmul(ps[:, g % 2, t * P:(t + 1) * P], SV[:, t, g * P:(g + 1) * P],
                                        m_("sgu_ws")[:, g * P:(g + 1) * P], start=True, stop=True)
                    mm.then_inc(sgu_filled, 1)
                eng.wait_ge(sgu_drained, 4)
                eng.wait_ge(kksq_ready, 1)
                for j in range(QT):
                    matmul(ps[:, 4 + j, 0:CVW - 1], heads, G[:, j, 0:CVW - 1], start=True, stop=True).then_inc(kk_summed, 1)
                for c in range(NT):
                    for j in range(QT):
                        mm = eng.transpose(ps[:, c, j * P:(j + 1) * P], CV[:, 8 + j, CV_AT[c]:CV_AT[c] + P], ident)
                    mm.then_inc(vtm_filled, 1)
                eng.wait_ge(vtm_ready, NT)
                for n, (d, c) in enumerate(SCANS):
                    r = slice(d * HD, (d + 1) * HD)
                    half = [slice(0, HD), slice(HD, P)]
                    if n:
                        eng.wait_ge(state_ready, n)
                        eng.wait_ge(u_ready, n)
                    for x, b, name in ((XW, 0, "w2"), (XA, 1, "a2")):
                        for j in range(QT):
                            mm = matmul(ps[:, b, j * P:(j + 1) * P], m_(name)[r, j * P:(j + 1) * P],
                                            x[r, c * P:(c + 1) * P], start=True, stop=True)
                    mm.then_inc(wa_filled, 1)
                    if 2 * n < MOD_B:
                        for c2 in (2 * n, 2 * n + 1):
                            mod_chunk(MOD_A + c2, 6 + c2 % 2)
                        for c2 in (2 * n, 2 * n + 1):
                            mm = mod_turn(MOD_A + c2, 5, 6 * (c2 % 2))
                        mm.then_inc(modb_filled, 1)
                        eng.wait_ge(modb_ready, n + 1)
                    eng.wait_ge(keys_ready, n + 1)
                    for b, src in ((2, BE), (3, KA)):
                        for j in range(QT):
                            mm = eng.transpose(ps[:, b, j * P:(j + 1) * P], src[:, j, :], ident)
                    mm.then_inc(tm_filled, 1)
                    for u in range(8):
                        j, hh = u // 2, half[u % 2]
                        if u == 0:
                            eng.wait_ge(kk_ready, 1)
                        if u >= 4:
                            eng.wait_ge(gram_ready, 8 * n + u - 3)
                        matmul(ps[:, 4 + u % 4, 0:2 * P], BE[hh, j, :], AR[hh, j, :], start=True, stop=True)
                        matmul(ps[:, 4 + u % 4, 2 * P:4 * P], KA[hh, j, :], AR[hh, j, :], start=True,
                                   stop=True).then_inc(gram_filled, 1)
                    for lv in range(LEVELS):
                        for g in range(2):
                            k = 2 * LEVELS * n + 2 * lv + g
                            eng.wait_ge(block_ready, k + 1)
                            if lv >= 1:
                                eng.wait_ge(inv_ready, k - 1)
                            if lv >= 2:
                                eng.wait_ge(y_ready, 2 * (LEVELS - 1) * n + 2 * (lv - 2) + g + 1)
                            for q in range(4):
                                mm = matmul(ps[:, g, q * P:(q + 1) * P], BL[:, g, q * P:(q + 1) * P],
                                                ident if lv == 0 else XX[:, 4 * g + q, 0, :], start=True, stop=True)
                            mm.then_inc(y_filled, 1)
                        for g in range(2):
                            if lv == 0:
                                continue
                            k = 2 * (LEVELS - 1) * n + 2 * (lv - 1) + g
                            eng.wait_ge(y_ready, k + 1)
                            if lv == 1:
                                eng.wait_ge(gram_ready, 8 * n + 8)
                            for q in range(4):
                                u, y = 4 * g + q, YS[:, g, q * P:(q + 1) * P]
                                if lv < LEVELS - 1:
                                    b, o = 4 + 2 * g + q // 2, (q % 2) * 2 * P
                                    matmul(ps[:, b, o:o + P], XX[:, u, 1, :], y, start=True, stop=True)
                                    mm = matmul(ps[:, b, o + P:o + 2 * P], y, XX[:, u, 1, :], start=True, stop=True)
                                else:
                                    mm = matmul(ps[:, 4 + 2 * g, q * P:(q + 1) * P], y, XX[:, u, 1, :], start=True, stop=True)
                            mm.then_inc(xy_filled, 1)
                    eng.wait_ge(tm_ready, 2 * n + 2)
                    eng.wait_ge(y_ready, 2 * (LEVELS - 1) * (n + 1))
                    if c:
                        eng.wait_ge(sh_ready, len([x for x in SCANS[:n + 1] if x[1]]))
                    for u in range(8):
                        j, hh = u // 2, half[u % 2]
                        out = ps[:, (2, 0)[u % 2], j * HD:(j + 1) * HD]
                        vt = VTM[:, c, u * HD:(u + 1) * HD]
                        if c:
                            matmul(out, AR[hh, j, 0:P], SH[hh, j, :], start=True, stop=False)
                        mm = matmul(out, G[:, u, 2 * P:3 * P], vt, start=(c == 0), stop=True)
                    mm.then_inc(r_filled, 1)
                    eng.wait_ge(r_ready, 2 * n + 2)
                    eng.wait_ge(inv_ready, 2 * LEVELS * (n + 1))
                    for u in range(8):
                        o = slice(u * HD, (u + 1) * HD)
                        mm = matmul(ps[:, 3, o], XX[:, u, 1, :], RSB[:, o], start=True, stop=True)
                    mm.then_inc(u_filled, 1)
                    eng.wait_ge(u_ready, n + 1)
                    for u in range(8):
                        j, hh = u // 2, half[u % 2]
                        o = slice(u * HD, (u + 1) * HD)
                        out = ps[hh, 4, j * P:(j + 1) * P]
                        if c:
                            matmul(out, SH[hh, j, :], AR[hh, j, P:2 * P], start=True, stop=False)
                        matmul(out, USB[:, o], G[:, u, P:2 * P], start=(c == 0), stop=False)
                        matmul(out, VTM[:, c, o], G[:, u, 3 * P:4 * P], start=False, stop=True)
                    for u in range(8):
                        j, hh = u // 2, half[u % 2]
                        o = slice(u * HD, (u + 1) * HD)
                        out = ps[hh, 5, j * HD:(j + 1) * HD]
                        matmul(out, BTM[:, o], USB[:, o], start=True, stop=False)
                        mm = matmul(out, KTM[:, o], VTM[:, c, o], start=False, stop=True)
                    mm.then_inc(os_filled, 1)
                eng.wait_ge(gn_ready, 1)
                for j in range(QT):
                    matmul(ps[:, j, 0:T], heads, o_rwkv[:, j, :], start=True, stop=True).then_inc(gn_summed, 1)
                eng.wait_ge(gn_ready, 2)
                for j in range(QT):
                    matmul(ps[:, 4 + j, 0:T], heads, E_SQ[:, j, :], start=True, stop=True).then_inc(gn_summed, 1)
                eng.wait_ge(bonus_ready, 8)
                for j in range(QT):
                    matmul(ps[:, j, 0:T], heads, E_SQ[:, j, :], start=True, stop=True).then_inc(gn_summed, 1)
                for j in range(QT):
                    matmul(ps[:, 4 + j, 0:T], m_("g2")[:, j * P:(j + 1) * P], XG, start=True, stop=True).then_inc(gn_summed, 1)
                for n in range(KD):
                    pair, odd = n // 2, n % 2
                    w = parts(S_MERGE + n)
                    for b in range(3):
                        if n:
                            eng.wait_ge(g_ready, 3 * (n - 1) + b + 1)
                        elif b == 0:
                            eng.wait_ge(orwkv_ready, QT)
                        product(ps[:, b, 0:T], columns(w, b * P), tokens(0, T)).then_inc(g_filled, 1)
                    release(S_MERGE + n)
                    raw = C_MERGE + 3 * pair + 2
                    w = landed(eng, raw).rearrange("p (b k n) -> p b k n", b=3, k=QT)
                    if n:
                        eng.wait_ge(mg_ready, n)
                    for b, o in enumerate((o_attn, o_sgu, o_rwkv)):
                        for k in range(QT):
                            mm = matmul(ps[:, 3 + b, 0:T], w[:, b, k, odd * P:(odd + 1) * P], o[:, k, :],
                                            start=(k == 0), stop=(k == QT - 1))
                        mm.then_inc(pr_filled, 1)
                    if odd:
                        owed.append(slot_taken[raw % SLOTS])
                eng.wait_ge(mg_ready, KD)
                for n in range(KD):
                    w = parts(S_OUT + n // 2)
                    if n >= 2:
                        eng.wait_ge(wo_drained, 2 * (n - 1))
                    product(ps[:, 6 + n % 2, 0:T], columns(w, (n % 2) * P),
                            tuple(lambda k, x=x: x[:, k, :] for x in (MG_hi, MG_lo))).then_inc(wo_filled, 1)
                    if n % 2:
                        release(S_OUT + n // 2)
                eng.wait_ge(sq2_ready, 1)
                for k in range(KD):
                    mm = matmul(ps[:, 1, 0:T], ones, R_SQ8[:, k, :], start=(k == 0), stop=(k == KD - 1))
                mm.then_inc(sq2_summed, 1)
                eng.wait_ge(h2_ready, 2)
                for t in range(NT):
                    for k in range(KD):
                        mm = matmul(ps[:, 0, t * N_EXP:(t + 1) * N_EXP], H2[:, k, t * P:(t + 1) * P],
                                        m_("router")[:, k * N_EXP:(k + 1) * N_EXP], start=(k == 0), stop=(k == KD - 1))
                mm.then_inc(lg_filled, 1)
                eng.wait_ge(comb_ready, NT)
                for t in range(NT):
                    mm = eng.transpose(ps[0:N_EXP, 1, t * P:(t + 1) * P], CB[:, t, :], ident)
                mm.then_inc(ct_filled, 1)
                eng.wait_ge(ct_ready, 1)

                def half_of(s, bank, part):
                    w = tuple(lambda k, x=x: x[s][:, part * D + k * P:part * D + (k + 1) * P] for x in (W_hi, W_lo))
                    return product(ps[:, bank, 0:T], w, tokens(0, T))

                def down(s, start, stop):
                    for t in range(NT):
                        for h in range(2):
                            o = slice(2 * D + h * 512, 2 * D + (h + 1) * 512)
                            for n, (x, w) in enumerate(((HID_lo, W_hi), (HID_hi, W_lo), (HID_hi, W_hi))):
                                mm = eng.matmul(ps[:, 2 * t + h, :], x[:, s, t * P:(t + 1) * P], w[s][:, o],
                                                start=(start and n == 0), stop=(stop and n == 2), skip_group_check=True)
                    return mm

                def pe_expert(i, s, start=False):
                    e, (j, q) = i * SLOTS + s, ((i, 0) if s == 1 else (i - 1, 1))
                    first = isinstance(e, int) and e == 0
                    eng.wait_ge(e_lo, e * 2 + 1)
                    if not first:
                        eng.wait_ge(e_silu, e)
                    half_of(s, 6, 0).then_inc(e_gate, 1)
                    eng.wait_ge(e_lo, e * 2 + 2)
                    if not first:
                        eng.wait_ge(e_prod, e)
                    half_of(s, 7, 1).then_inc(e_up, 1)
                    if not first:
                        eng.wait_ge(e_hid, e)
                        eng.wait_ge(slot_taken[q], j + (C_EXP // SLOTS + 1))
                        down(q, start, False).then_inc(e_down, 1)

                for s in range(SLOTS):
                    pe_expert(0, s, start=(s == 1))
                with eng.Fori(1, ROUNDS) as i:
                    for s in range(SLOTS):
                        pe_expert(i, s)
                eng.wait_ge(e_hid, N_EXP + SHARED)
                eng.wait_ge(slot_taken[1], C_EXP // SLOTS + ROUNDS)
                down(1, False, True).then_inc(acc_filled, 1)
                eng.wait_ge(ro_ready, NT)
                for n in range(KD):
                    if n >= 2:
                        eng.wait_ge(x_ready, 2 * (n - 1))
                    for t in range(NT):
                        mm = eng.transpose(ps[:, 6 + n % 2, t * P:(t + 1) * P], RO[:, t, n * P:(n + 1) * P], ident)
                    mm.then_inc(back_filled, 1)
                layer_end(eng, "pe", layer)


def constants():
    out = np.zeros((P, N_CON), np.float32)

    def put(name, a, off=0):
        out[:, CON[name] + off:CON[name] + off + a.shape[1]] = a

    i = np.arange(P)
    put("ident", np.eye(P))
    put("heads", (i[:, None] // HD == i[None] // HD))
    put("ones", np.ones((P, P)))
    f = HD // 4
    part, low = (i // f) % 2, i % f
    rot = np.zeros((P, P))
    for m in range(P):
        rot[m + f if part[m] == 0 else m - f, m] = -1.0 if part[m] == 0 else 1.0
    put("rot", rot)
    t = np.arange(LAT)
    inv = (10000.0 ** (-np.arange(f, dtype=np.float32) / f)).astype(np.float32)
    pos = np.stack([(t // 64), (t % 64)]).astype(np.float32)
    axis = (i // (2 * f)) % 2
    ang = (pos[axis] * inv[low][:, None]).astype(np.float32)
    put("cos", np.cos(ang))
    put("sin", np.sin(ang))
    s_, t_ = i[:, None], i[None]
    for d in range(2):
        strict = (s_ < t_) if d == 0 else (s_ > t_)
        put("causal", strict, d * 2 * P)
        put("causal", strict | (s_ == t_), d * 2 * P + P)
        for lv in range(LEVELS):
            b = 1 << lv
            put("level", strict & (s_ // (2 * b) == t_ // (2 * b)) & (s_ // b != t_ // b), (d * LEVELS + lv) * P)
    put("iota", np.broadcast_to(np.arange(N_EXP), (P, N_EXP)))
    return out


def lay_out(a):
    L = a["w_in"].shape[0]
    a = {k: np.asarray(v) for k, v in a.items()}
    xT = np.concatenate([a["x_prompt"].reshape(CTX, D), a["x_sample"].reshape(LAT, D)]).T
    W = np.zeros((L, N_CHUNKS, P, SLOT_W), np.float32)

    def by_k(w, tiles):
        return w.reshape(-1, P, w.shape[-1]).transpose(1, 0, 2)

    for l in range(L):
        for n in range(16):
            W[l, C_MOD + n if n < MOD_A else C_MODB + n - MOD_A] = by_k(a["mod_w"][l][:, n * 384:(n + 1) * 384], 3).reshape(P, -1)
        w = a["w_in"][l]
        q, k, v, su, sv, rkv, xw, xa, xg, gates = np.split(
            w, np.cumsum([512, 128, 128, 512, 512, 1536, 128, 128, 128]), axis=1)
        q = q.reshape(D, 2, 4, HD).transpose(0, 2, 1, 3).reshape(D, 512)
        seq = np.concatenate([q, k, v, su, sv, xg, rkv, xw, xa, np.zeros((D, P), np.float32)], axis=1)
        for n in range(10):
            W[l, C_IN + n] = by_k(seq[:, n * 384:(n + 1) * 384], 3).reshape(P, -1)
        gates = gates.reshape(D, 3, D)
        pa = a["proj_attn"][l].reshape(2, 4, HD, D).transpose(1, 0, 2, 3).reshape(512, D)
        pr = np.stack([pa, a["proj_sgu"][l], a["proj_rwkv"][l]])
        for pair in range(4):
            for odd in range(2):
                n = 2 * pair + odd
                W[l, C_MERGE + 3 * pair + odd] = by_k(gates[:, :, n * P:(n + 1) * P].reshape(D, 384), 3).reshape(P, -1)
            cols = pr[:, :, 2 * pair * P:2 * (pair + 1) * P].reshape(3, 4, P, 2 * P).transpose(2, 0, 1, 3)
            W[l, C_MERGE + 3 * pair + 2] = cols.reshape(P, -1)
            W[l, C_OUT + pair].reshape(P, KD, 3 * P)[:, :, 0:2 * P] = by_k(
                a["w_out"][l][:, 2 * pair * P:2 * (pair + 1) * P], 2)
        E = W[l, C_EXP:].reshape(N_EXP + SHARED, P, 3, KD * P)
        for part, name, sh in ((0, "exp_gate", "sh_gate"), (1, "exp_up", "sh_up")):
            E[:N_EXP, :, part] = a[name][l].reshape(N_EXP, KD, P, P).transpose(0, 2, 1, 3).reshape(N_EXP, P, KD * P)
            E[N_EXP:, :, part] = a[sh][l].reshape(KD, P, SHARED, P).transpose(2, 1, 0, 3).reshape(SHARED, P, KD * P)
        E[:N_EXP, :, 2] = a["exp_down"][l]
        E[N_EXP:, :, 2] = a["sh_down"][l].reshape(SHARED, P, D)

    par = np.zeros((L, P, N_MAT + N_VEC), np.float32)

    def mat(name, x):
        par[:, :, MAT[name]:MAT[name] + x.shape[-1]] = x

    def vec(name, x):
        n = x.shape[1]
        par[:, :, N_MAT + VEC[name]:N_MAT + VEC[name] + n] = x.transpose(0, 2, 1)

    mat("sgu_ws", a["sgu_ws"].transpose(0, 3, 1, 2).reshape(L, P, 512))
    mat("w2", a["rwkv_w2"].reshape(L, P, 512))
    mat("a2", a["rwkv_a2"].reshape(L, P, 512))
    mat("g2", a["rwkv_g2"])
    mat("router", a["router_w"].reshape(L, KD, P, N_EXP).transpose(0, 2, 1, 3).reshape(L, P, KD * N_EXP))
    mat("ctx_kT", a["cache_k"][0].reshape(L, CTX, P).transpose(0, 2, 1))
    mat("ctx_v", a["cache_v"][0].reshape(L, CTX, P))
    s = a["state_wkv"][0].reshape(L, 2, 4, 2, HD, HD)
    mat("state0", s.transpose(0, 3, 5, 1, 2, 4).reshape(L, P, 512))
    vec("g1", a["norm1_g"].reshape(L, KD, P))
    vec("g2n", a["norm2_g"].reshape(L, KD, P))
    vec("mod_b", a["mod_b"].reshape(L, 48, P))
    vec("qn", np.concatenate([a["q_norm"]] * 2, axis=1).reshape(L, 1, P))
    vec("kn", np.concatenate([a["k_norm"]] * 2, axis=1).reshape(L, 1, P))
    vec("sgu_g", a["sgu_norm_g"].reshape(L, 4, P))
    vec("conv", a["rwkv_conv"].reshape(L, 36, P))
    vec("w0", a["rwkv_w0"].reshape(L, 8, P))
    vec("a0", a["rwkv_a0"].reshape(L, 8, P))
    for name, src in (("k_k", "rwkv_k_k"), ("k_a", "rwkv_k_a"), ("r_k", "rwkv_r_k"), ("ln_g", "rwkv_ln_g"), ("ln_b", "rwkv_ln_b")):
        vec(name, a[src].reshape(L, 4, P))
    rows = np.concatenate([a["sgu_bs"].reshape(L, 512), a["router_bias"]], axis=1)
    con = constants()
    cv = np.stack([a["c_ctx"].reshape(KD, P), a["c"].reshape(KD, P)], axis=-1)
    con[:, CON["cvec"]:CON["cvec"] + 2 * KD] = cv.transpose(1, 0, 2).reshape(P, 2 * KD)
    return {"xT": np.ascontiguousarray(xT), "weights": W.reshape(L * N_CHUNKS, P, SLOT_W), "params": par,
            "rows": np.ascontiguousarray(rows), "consts": con}


def kernel(**inputs):
    from concourse import bacc
    from concourse.bass_utils import run_bass_kernel_spmd

    arrays = lay_out(inputs)
    nc = bacc.Bacc("TRN2", target_bir_lowering=False, num_devices=1)
    args = [nc.dram_tensor(n, v.shape, F32, kind="ExternalInput").ap() for n, v in arrays.items()]
    outs = {"yT": (D, T), "new_k": (DEPTH, CTX, P), "new_v": (DEPTH, CTX, P), "new_s": (DEPTH, P, 512)}
    args += [nc.dram_tensor(n, s, F32, kind="ExternalOutput").ap() for n, s in outs.items()]
    program(nc, *args)
    r = run_bass_kernel_spmd(nc, [arrays], core_ids=[0]).results[0]
    y = r["yT"].T
    kv = (1, DEPTH, CTX, 2, HD)
    s = r["new_s"].reshape(DEPTH, 2, HD, 2, 4, HD).transpose(0, 3, 4, 1, 5, 2)
    return (np.ascontiguousarray(y[:CTX]).reshape(1, CTX, D), np.ascontiguousarray(y[CTX:]).reshape(1, LAT, D),
            r["new_k"].reshape(kv), r["new_v"].reshape(kv),
            np.ascontiguousarray(s).reshape(1, DEPTH, 2, 8, HD, HD))
```

```python
from contextlib import ExitStack

import numpy as np

import concourse.bass as bass
from concourse import mybir

F32 = mybir.dt.float32
F32R = mybir.dt.float32r
U32 = mybir.dt.uint32
ALU = mybir.AluOpType
ACT = mybir.ActivationFunctionType
AX = mybir.AxisListType.X

P = 128
D = 1024
KD = D // P
DEPTH = 2
CTX, LAT = 128, 256
T = CTX + LAT
NT = T // P
GROUPS = [(0, CTX), (CTX, T)]
HD = 64
QT = 4
DECAY = 0.606531
GN_EPS = 64e-5
EPS = 1e-6
N_EXP, TOP_K, SHARED = 64, 6, 2
ROUTED_SCALE = 2.5
SLOTS = 2
SLOT_W = KD * 3 * P

C_MOD = 0
MOD_A, MOD_B = 6, 10
C_IN = C_MOD + MOD_A
C_MODB = C_IN + 10
C_MERGE = C_MODB + MOD_B
C_OUT = C_MERGE + 12
C_EXP = C_OUT + 4
S_IN, S_MERGE, S_OUT, S_EXP = 0, 10, 18, 22
N_CHUNKS = C_EXP + N_EXP + SHARED
ROUNDS = (N_EXP + SHARED) // SLOTS
assert C_EXP % SLOTS == 0 and N_CHUNKS % SLOTS == 0


def offsets(sizes):
    at, out = 0, {}
    for name, n in sizes:
        out[name] = at
        at += n
    return out, at


MAT, N_MAT = offsets([("sgu_ws", 512), ("w2", 512), ("a2", 512), ("g2", 512), ("router", KD * N_EXP),
                      ("ctx_kT", P), ("ctx_v", P), ("state0", 512)])
VEC, N_VEC = offsets([("g1", KD), ("g2n", KD), ("mod_b", 48), ("qn", 1), ("kn", 1), ("sgu_g", 4),
                      ("conv", 36), ("w0", 8), ("a0", 8), ("k_k", 4), ("k_a", 4), ("r_k", 4),
                      ("ln_g", 4), ("ln_b", 4)])
ROW, N_ROW = offsets([("sgu_b", 512), ("router_b", N_EXP)])
CON, N_CON = offsets([("ident", P), ("heads", P), ("ones", P), ("rot", P), ("cos", LAT), ("sin", LAT),
                      ("causal", 4 * P), ("level", 14 * P), ("iota", N_EXP), ("cvec", KD * 2)])

PAD = 388
CVW = 386
CV_AT = [0, 129, 257]
LEVELS = 7
Z_ACT = (16, 29, 30)
Z_OF = [(0, 1, 2), (3, 4, 5), (6, 7, 8), (9, 10, 11, 12), (13, 14, 15, 16)] + [
    (17 + 3 * i, 18 + 3 * i, 19 + 3 * i) for i in range(4)] + [(29, 30)]
SCANS = [(0, 0), (1, 0), (0, 1), (1, 2), (0, 2), (1, 1)]


def program(nc, xT, weights, params, rows, consts, yT, new_k, new_v, new_s, depth=DEPTH):
    combine_dram = nc.dram_tensor("combine", (N_EXP + SHARED, T), F32).ap()
    with ExitStack() as ctx:
        def sb(name, shape, dt=F32):
            return ctx.enter_context(nc.sbuf_tensor(name, shape, dt))

        def sem(name):
            return ctx.enter_context(nc.semaphore(name))

        X = sb("X", [P, KD, T])
        H_hi = sb("H_hi", [P, KD, T], F32R)
        H_lo = sb("H_lo", [P, KD, T], F32R)
        branches = sb("branches", [P, 3 * QT * T])
        o_attn, o_sgu, o_rwkv = (branches[:, i * QT * T:(i + 1) * QT * T].rearrange("p (j t) -> p j t", j=QT)
                                 for i in range(3))
        slot = [sb(f"slot{s}", [P, SLOT_W]) for s in range(SLOTS)]
        con = sb("con", [P, N_CON])
        mat = sb("mat", [P, N_MAT])
        vec = sb("vec", [P, N_VEC])
        row = sb("row", [P, N_ROW])
        mod = sb("mod", [P, 48, 2])
        amp = sb("amp", [P, 2, KD, 2])
        csil = sb("csil", [P, KD, 2])
        mod_row = sb("mod_row", [2, 2, 3 * P])
        small = sb("small", [P, 64])
        epscol = sb("epscol", [P, 4])
        ps = ctx.enter_context(nc.psum_tensor("ps", [P, 8, 512], F32))

        def c_(name, n=P):
            return con[:, CON[name]:CON[name] + n]

        ident, heads, ones, rot = (c_(n) for n in ("ident", "heads", "ones", "rot"))
        cos, sin = c_("cos", LAT), c_("sin", LAT)

        def v_(name, i=0, n=1):
            return vec[:, VEC[name] + i:VEC[name] + i + n]

        def m_(name, n=512):
            return mat[:, MAT[name]:MAT[name] + n]

        ARENA = 24512
        arena_at = -(-nc.sbuf_base // 32) * 32
        arena = sb("arena", [P, ARENA])

        def at(off, *shape):
            n = int(np.prod(shape))
            assert off + n <= ARENA, (off, shape)
            a = arena[:, off:off + n]
            if len(shape) == 2:
                a = a.rearrange("p (a b) -> p a b", a=shape[0])
            if len(shape) == 3:
                a = a.rearrange("p (a b c) -> p a b c", a=shape[0], b=shape[1])
            return a

        def rounded(name, off, *shape):
            return nc.alloc_sbuf_tensor_at(name, [P, *shape], F32R, offset=arena_at + 4 * off)

        PARTS = ARENA - 4 * SLOT_W
        W_hi = [rounded(f"W_hi{i}", PARTS + 2 * i * SLOT_W, SLOT_W) for i in range(2)]
        W_lo = [rounded(f"W_lo{i}", PARTS + (2 * i + 1) * SLOT_W, SLOT_W) for i in range(2)]

        XW, XA, XG = (at(i * T, T) for i in range(3))
        A0 = 3 * T
        QK = at(A0, 5, T)
        VT = at(A0 + 5 * T, NT, P)
        SU = at(A0 + 6 * T, QT, T)
        SV = at(A0 + 10 * T, NT, 512)
        RAW = at(A0 + 14 * T, 12, PAD)
        A1 = A0 + 14 * T + 12 * PAD
        SQ5 = branches[:, QT * T:QT * T + 5 * T].rearrange("p (j t) -> p j t", j=5)
        RS5 = SQ5
        ROT5 = branches[:, 0:5 * LAT].rearrange("p (j t) -> p j t", j=5)
        PM = at(A1, 3, T)
        PTS = at(A1 + 3 * T, 2, T)
        KOUT = at(A1 + 10 * T, P)
        att_small = at(A1 + 10 * T + P, 4, 24)
        SGT = at(A1 + 12 * T, NT, P)
        SSQ = at(A1 + 13 * T, 512)
        SQ8 = at(A0, KD, T)
        RS1 = at(A0 + 8 * T, T)
        H1 = at(A0 + 9 * T, KD, T)
        CV = at(ARENA - 12 * CVW, 12, CVW)
        B1 = A0
        KK = at(B1, QT, CVW); B1 += QT * CVW
        VTM = at(B1, NT, 512); B1 += NT * 512
        KS = at(B1, QT, CVW); B1 += QT * CVW
        SG = at(B1, QT, P); B1 += 512
        SA = at(B1, QT, P); B1 += 512
        CUM = at(B1, QT, P); B1 += 512
        BE = at(B1, QT, P); B1 += 512
        ARS = at(B1, 2, QT * 2 * P); B1 += 2048
        AR2 = [ARS[:, i, :].rearrange("p (j t) -> p j t", j=QT) for i in range(2)]
        BTM = at(B1, 512); B1 += 512
        KTM = at(B1, 512); B1 += 512
        KA = SG
        G = at(B1, 8, 512); B1 += 4096
        XX = at(B1, 8, 2, P); B1 += 2048
        BL = at(B1, 2, 512); B1 += 1024
        YS = at(B1, 2, 512); B1 += 1024
        SH = at(B1, QT, HD); B1 += 256
        SL = m_("state0").rearrange("p (d n) -> p d n", d=2)
        SOUT = at(B1, 2, QT * HD); B1 += 512
        HALF, EH2 = small[:, 32:36], (small[:, 36:40], small[:, 40:44])
        assert B1 <= ARENA - 12 * CVW, (B1, ARENA - 12 * CVW)
        RSB, USB = YS[:, 0, :], YS[:, 1, :]
        E0 = A0 + 2 * QT * CVW + NT * 512
        E_SQ = at(E0, QT, T)
        E_RS = at(E0 + 4 * T, QT, T)
        E_B = at(E0 + 8 * T, QT, T)
        MG_hi = rounded("MG_hi", 0, KD, T)
        MG_lo = rounded("MG_lo", 8 * T, KD, T)
        GT = at(16 * T, 2, 3, T)
        MT = at(22 * T, 3, T)
        SC = at(0, NT, N_EXP)
        BI = at(192, NT, N_EXP)
        CB = at(384, NT, N_EXP)
        TOPV = at(576, NT, 8)
        TOPF = at(600, NT, 8)
        EQ = at(640, TOP_K, N_EXP)
        topi = sb("topi", [P, NT, 8], U32)
        CT = at(1024, T)
        R_SQ8 = at(2048 + 6928, KD, T)
        R_RS1 = at(2048 + 8 * T, T)
        H2 = at(2048 + 9 * T, KD, T)
        SGS = at(2048, SLOTS, T)
        TS = at(2048 + 2 * T, SLOTS, T)
        CBC = at(2048 + 4 * T, SLOTS, T)
        HID_hi = rounded("HID_hi", 2048 + 6 * T, SLOTS, T)
        HID_lo = rounded("HID_lo", 2048 + 8 * T, SLOTS, T)
        RO = at(2048 + 10 * T, NT, D)

        const_landed = sem("const_landed")
        pool_ready = sem("pool_ready")
        eps_ready = sem("eps_ready")
        csil_ready = sem("csil_ready")
        line_written = sem("line_written")
        y_written = sem("y_written")
        row_landed = [sem(f"row{s}_landed") for s in range(SLOTS)]
        arrived = sem("arrived")
        released = sem("released")
        seen = {n: sem(f"seen_{n}") for n in ("pe", "act", "dve", "pool", "sp")}

        layer_sems = []

        def lsem(name):
            s = sem(name)
            layer_sems.append(s)
            return s

        slot_filled = [lsem(f"slot{s}_filled") for s in range(SLOTS)]
        slot_taken = [lsem(f"slot{s}_taken") for s in range(SLOTS)]
        hi_ready, parts_used = lsem("hi_ready"), lsem("parts_used")
        e_hi, e_lo, e_down, e_prod, e_hid_hi = (lsem(n) for n in ("e_hi", "e_lo", "e_down", "e_prod", "e_hid_hi"))
        mod_row_filled, mod_row_ready, modb_filled, modb_ready = (
            lsem(n) for n in ("mod_row_filled", "mod_row_ready", "modb_filled", "modb_ready"))
        par_landed = lsem("par_landed")
        act_step, dve_step, pool_step = lsem("act_step"), lsem("dve_step"), lsem("pool_step")
        mod_filled, mod_ready, amp_ready = lsem("mod_filled"), lsem("mod_ready"), lsem("amp_ready")
        sq_ready, sq_summed, root_ready, h_ready = (lsem(n) for n in ("sq_ready", "sq_summed", "root_ready", "h_ready"))
        h_scaled, h_hi, h2_scaled, h2_hi = (lsem(n) for n in ("h_scaled", "h_hi", "h2_scaled", "h2_hi"))
        z_filled, z_dve, z_act = lsem("z_filled"), lsem("z_dve"), lsem("z_act")
        raw_zeroed = lsem("raw_zeroed")
        qsq_ready, qsq_summed, qroot_ready, qk_normed = (lsem(n) for n in ("qsq_ready", "qsq_summed", "qroot_ready", "qk_normed"))
        rot_filled, qk_ready = lsem("rot_filled"), lsem("qk_ready")
        kout_filled, kout_ready, kv_written = lsem("kout_filled"), lsem("kout_ready"), lsem("kv_written")
        s_filled, s_max, p_exp, p_ready = (lsem(n) for n in ("s_filled", "s_max", "p_exp", "p_ready"))
        pt_filled, pt_ready, pv_filled, oattn_ready = (lsem(n) for n in ("pt_filled", "pt_ready", "pv_filled", "oattn_ready"))
        sv_root, sv_normed, sgu_filled, sgu_drained = (lsem(n) for n in ("sv_root", "sv_normed", "sgu_filled", "sgu_drained"))
        cv_ready, kksq_ready, kk_summed, kk_root, kk_ready = (lsem(n) for n in ("cv_ready", "kksq_ready", "kk_summed", "kk_root", "kk_ready"))
        vtm_filled, vtm_ready = lsem("vtm_filled"), lsem("vtm_ready")
        wa_filled, decay_ready, rate_ready, cum_ready, exp_ready = (
            lsem(n) for n in ("wa_filled", "decay_ready", "rate_ready", "cum_ready", "exp_ready"))
        keys_ready = lsem("keys_ready")
        tm_filled, tm_ready = lsem("tm_filled"), lsem("tm_ready")
        gram_filled, gram_ready = lsem("gram_filled"), lsem("gram_ready")
        block_ready = lsem("block_ready")
        y_filled, y_ready, xy_filled, inv_ready = (lsem(n) for n in ("y_filled", "y_ready", "xy_filled", "inv_ready"))
        sh_ready, r_filled, r_ready, u_filled, u_ready = (lsem(n) for n in ("sh_ready", "r_filled", "r_ready", "u_filled", "u_ready"))
        os_filled, os_ready = lsem("os_filled"), lsem("os_ready")
        state_written = lsem("state_written")
        state_ready = lsem("state_ready")
        gn_ready, gn_squared, gn_summed, gn_root = (lsem(n) for n in ("gn_ready", "gn_squared", "gn_summed", "gn_root"))
        bonus_ready, bonus_summed, bonus_done, outgate_ready = (
            lsem(n) for n in ("bonus_ready", "bonus_summed", "bonus_done", "outgate_ready"))
        orwkv_ready = lsem("orwkv_ready")
        g_filled, g_ready, pr_filled, mg_ready = (lsem(n) for n in ("g_filled", "g_ready", "pr_filled", "mg_ready"))
        wo_filled, wo_drained = lsem("wo_filled"), lsem("wo_drained")
        sq2_ready, sq2_summed, root2_ready, h2_ready = (lsem(n) for n in ("sq2_ready", "sq2_summed", "root2_ready", "h2_ready"))
        lg_filled, score_ready, comb_ready, ct_filled, ct_ready, ct_written = (
            lsem(n) for n in ("lg_filled", "score_ready", "comb_ready", "ct_filled", "ct_ready", "ct_written"))
        e_gate, e_silu, e_up, e_scaled, e_hid = (lsem(n) for n in ("e_gate", "e_silu", "e_up", "e_scaled", "e_hid"))
        acc_filled, ro_ready = lsem("acc_filled"), lsem("ro_ready")
        back_filled, x_ready = lsem("back_filled"), lsem("x_ready")

        block = ctx.enter_context(nc.Block())

        class InOrder:

            def __init__(self, eng, step):
                self.eng, self.step, self.count = eng, step, {}

            def __call__(self, instruction, s=None, value=None):
                s = self.step if s is None else s
                n = self.count[id(s)] = value or self.count.get(id(s), 0) + 1
                instruction.then_inc(s, 1)
                self.eng.wait_ge(s, n)

        def layer_end(eng, name, layer):
            eng.drain().then_inc(arrived, 1)
            eng.wait_ge(released, layer + 1)
            eng.sem_inc(seen[name], 1)

        def landed(eng, n):
            eng.wait_ge(slot_filled[n % SLOTS], 16 * (n // SLOTS + 1))
            return slot[n % SLOTS][:, :]

        def raw_of(m):
            if m < S_MERGE:
                return C_IN + m
            if m < S_OUT:
                return C_MERGE + 3 * ((m - S_MERGE) // 2) + m % 2
            return C_OUT + m - S_OUT

        def round_hi(eng, do, m):
            w = landed(eng, raw_of(m))
            if m >= 2:
                eng.wait_ge(parts_used, m - 1)
            do(eng.activation(W_hi[m % 2][:, :], w, ACT.Copy), hi_ready)

        def take_lo(eng, do, m):
            eng.wait_ge(hi_ready, m + 1)
            n = raw_of(m)
            do(eng.tensor_tensor(W_lo[m % 2][:, :], slot[n % SLOTS][:, :], W_hi[m % 2][:, :].bitcast(F32), ALU.subtract),
               slot_taken[n % SLOTS], n // SLOTS + 1)

        @block.sync
        def _(eng):
            eng.dma_start(con[:, :], consts).then_inc(const_landed, 16)
            eng.dma_start(X[:, :, :], xT.rearrange("(k p) t -> p k t", p=P)).then_inc(const_landed, 16)
            with eng.Fori(0, depth) as layer:
                def fill(s, n):
                    eng.dma_start(slot[s][:, :], weights[bass.ds(layer * N_CHUNKS + n, 1), :, :]
                                  .rearrange("l p n -> (l p) n")).then_inc(slot_filled[s], 16)

                for s in range(SLOTS):
                    fill(s, s)
                eng.dma_start(mat[:, :], params[bass.ds(layer, 1), :, 0:N_MAT]
                              .rearrange("l p n -> (l p) n")).then_inc(par_landed, 16)
                eng.dma_start(vec[:, :], params[bass.ds(layer, 1), :, N_MAT:N_MAT + N_VEC]
                              .rearrange("l p n -> (l p) n")).then_inc(par_landed, 16)
                eng.dma_start(row[:, :], rows[bass.ds(layer, 1), :].to_broadcast([P, N_ROW])).then_inc(par_landed, 16)
                with eng.Fori(1, N_CHUNKS // SLOTS) as i:
                    for s in range(SLOTS):
                        eng.wait_ge(slot_taken[s], i)
                        fill(s, i * SLOTS + s)
                eng.wait_ge(arrived, 4 * layer + 4)
                eng.sem_inc(seen["sp"], 1)
                for s in layer_sems:
                    eng.sem_clear(s)
                eng.sem_inc(released, 1)
            eng.dma_start(yT.rearrange("(k p) t -> p k t", p=P), X[:, :, :]).then_inc(y_written, 16)
            eng.wait_ge(y_written, 16)

        @block.gpsimd
        def _(eng):
            do0 = InOrder(eng, pool_ready)
            for i, v in enumerate((EPS, 1e-12, GN_EPS, 0.0)):
                do0(eng.memset(epscol[:, i:i + 1], v))
            eng.wait_ge(const_landed, 32)
            for t in range(NT):
                eng.dma_start(combine_dram[0:SHARED, t * P:(t + 1) * P],
                              ones[0:SHARED, :]).then_inc(line_written, 16)
            eng.wait_ge(line_written, 16 * NT)
            with eng.Fori(0, depth) as layer:
                do = InOrder(eng, pool_step)
                eng.wait_ge(h_ready, KD)
                for col in (0, 1 + CTX, 2 + T):
                    do(eng.memset(RAW[:, :, col:col + 1], 0.0), raw_zeroed)
                for n, (d, c) in enumerate(SCANS):
                    for lv in range(LEVELS):
                        for g in range(2):
                            eng.wait_ge(gram_ready, 8 * n + 4 * g + 4)
                            if n or lv:
                                eng.wait_ge(y_filled, 2 * LEVELS * n + 2 * lv + g - 1)
                            if lv == 1:
                                eng.wait_ge(inv_ready, 2 * LEVELS * n + g + 1)
                            m = CON["level"] + (d * LEVELS + lv) * P
                            do(eng.tensor_tensor(BL[:, g, :].rearrange("p (u t) -> p u t", u=4),
                                                 G[:, 4 * g:4 * g + 4, 0:P],
                                                 con[:, None, m:m + P].to_broadcast([P, 4, P]), ALU.mult), block_ready)
                def weight_rows(i):
                    for s in range(SLOTS):
                        eng.dma_start(CBC[:, s, :], combine_dram[bass.ds(i * SLOTS + s, 1), :]
                                      .to_broadcast([P, T])).then_inc(row_landed[s], 16)

                eng.wait_ge(wo_drained, 2 * KD)
                weight_rows(0)
                eng.wait_ge(ct_written, 16)
                with eng.Fori(1, ROUNDS) as i:
                    eng.wait_ge(e_scaled, i * SLOTS)
                    eng.sem_inc(seen["pool"], 1)
                    weight_rows(i)
                layer_end(eng, "pool", layer)

        @block.scalar
        def _(eng):
            eng.wait_ge(const_landed, 32)
            eng.wait_ge(pool_ready, 4)
            eng.activation(csil[:, :, :], c_("cvec", 2 * KD).rearrange("p (k g) -> p k g", g=2),
                           ACT.Silu).then_inc(csil_ready, 1)
            with eng.Fori(0, depth) as layer:
                do = InOrder(eng, act_step)

                def root_of(summed, root, RS):
                    eng.wait_ge(summed, 1)
                    do(eng.activation(RS, ps[:, 1, 0:T], ACT.Sqrt, bias=epscol[:, 0:1], scale=1.0 / D), root)

                def hi_of(H, scaled, h_hi):
                    for k in range(KD):
                        eng.wait_ge(scaled, k + 1)
                        do(eng.activation(H_hi[:, k, :], H[:, k, :], ACT.Copy), h_hi)

                def mod_rows(c, bank):
                    eng.wait_ge(mod_row_filled, c + 1)
                    do(eng.activation(mod_row[:, c % 2, :], ps[0:2, bank, 0:3 * P], ACT.Copy), mod_row_ready)

                do(eng.activation(SQ8[:, :, :], X[:, :, :], ACT.Square), sq_ready)
                root_of(sq_summed, root_ready, RS1)
                for c in range(MOD_A):
                    mod_rows(c, 2 + c % 2)
                round_hi(eng, do, 0)
                hi_of(H1, h_scaled, h_hi)
                round_hi(eng, do, 1)
                for c in range(10):
                    if c == 4:
                        for j in range(5):
                            eng.wait_ge(qsq_summed, j + 1)
                            do(eng.activation(RS5[:, j, :], ps[:, 4 + j % 4, 0:T], ACT.Sqrt, bias=epscol[:, 0:1],
                                              scale=1.0 / HD), qroot_ready)
                    for n, dst, func in zip(Z_ACT, (XG, XW, XA), (ACT.Sigmoid, ACT.Tanh, ACT.Copy)):
                        if n in Z_OF[c]:
                            eng.wait_ge(z_filled, n + 1)
                            do(eng.activation(dst, ps[:, n % 4, 0:T], func), z_act)
                    if c == 2:
                        eng.wait_ge(z_dve, 5)
                        do(eng.activation(SQ5, QK, ACT.Square), qsq_ready)
                    if c + 2 < 10:
                        round_hi(eng, do, c + 2)
                mod_rows(MOD_A, 2)
                eng.wait_ge(kout_filled, 1)
                do(eng.activation(KOUT, ps[:, 7, 0:P], ACT.Copy), kout_ready)
                eng.dma_start(new_k[bass.ds(layer, 1), :, :].rearrange("l t n -> (l t) n"), KOUT).then_inc(kv_written, 16)
                eng.dma_start(new_v[bass.ds(layer, 1), :, :].rearrange("l t n -> (l t) n"), VT[:, 0, :]).then_inc(kv_written, 16)
                mod_rows(MOD_A + 1, 2)
                eng.wait_ge(z_dve, 28)
                for t in range(NT):
                    do(eng.activation(SSQ, SV[:, t, :], ACT.Square, accum_out=small[:, t:t + 1]))
                do(eng.activation(small[:, 4:7], small[:, 0:3], ACT.Sqrt, bias=epscol[:, 0:1], scale=1.0 / 512), sv_root)
                for u in range(24 + 2):
                    if u and u % 3 == 0:
                        mod_rows(MOD_A + u // 3 + 1, 2)
                    if u < 24:
                        n = P if u % NT == 0 else T
                        eng.wait_ge(s_max, u + 1)
                        if u >= 3:
                            eng.wait_ge(pt_filled, u - 2)
                        do(eng.activation(PM[:, u % 3, 0:n], ps[:, 4 + u % 3, 0:n], ACT.Exp,
                                          bias=att_small[:, 1, u:u + 1], scale=HD ** -0.5,
                                          accum_out=att_small[:, 2, u:u + 1]), p_exp)
                    if u >= 2:
                        w = u - 2
                        n = P if w % NT == 0 else T
                        eng.wait_ge(pt_filled, w + 1)
                        if w >= 2:
                            eng.wait_ge(pv_filled, w - 1)
                        do(eng.activation(PTS[:, w % 2, 0:n], ps[:, (7, 3)[w % 2], 0:n], ACT.Copy), pt_ready)
                eng.wait_ge(kv_written, 32)
                eng.wait_ge(kksq_ready, 1)
                for j in range(QT):
                    eng.wait_ge(kk_summed, j + 1)
                    do(eng.activation(G[:, 4 + j, 0:CVW - 1], ps[:, 4 + j, 0:CVW - 1], ACT.Sqrt, bias=epscol[:, 1:2]), kk_root)
                def decays(n):
                    d = SCANS[n][0]
                    eng.wait_ge(wa_filled, n + 1)
                    for j in range(QT):
                        do(eng.activation(SG[:, j, :], ps[:, 2, j * P:(j + 1) * P], ACT.Sigmoid,
                                          bias=v_("w0", d * 4 + j)), decay_ready)

                def rates(n):
                    d = SCANS[n][0]
                    for j in range(QT):
                        do(eng.activation(SA[:, j, :], ps[:, 3, j * P:(j + 1) * P], ACT.Sigmoid,
                                          bias=v_("a0", d * 4 + j)), rate_ready)

                def exponentials(n):
                    AR = AR2[n % 2]
                    eng.wait_ge(cum_ready, n + 1)
                    do(eng.activation(AR[:, :, 0:P], AR[:, :, 0:P], ACT.Exp, scale=-DECAY))
                    do(eng.activation(AR[:, :, P:2 * P], CUM, ACT.Exp, scale=-DECAY))
                    do(eng.activation(CUM, CUM, ACT.Exp, scale=DECAY))
                    do(eng.activation(EH2[n % 2], HALF, ACT.Exp, scale=-DECAY), exp_ready)

                def group_root(j):
                    eng.wait_ge(gn_summed, QT + j + 1)
                    do(eng.activation(E_RS[:, j, :], ps[:, 4 + j, 0:T], ACT.Sqrt, bias=epscol[:, 2:3], scale=1.0 / HD), gn_root)

                decays(0)
                rates(0)
                exponentials(0)
                for c in range(NT):
                    eng.wait_ge(vtm_filled, c + 1)
                    do(eng.activation(VTM[:, c, :], ps[:, (0, 1, 4)[c], :], ACT.Copy), vtm_ready)
                for n, (d, c) in enumerate(SCANS):
                    eng.wait_ge(tm_filled, n + 1)
                    if n == 2:
                        eng.wait_ge(state_ready, 2)
                        eng.dma_start(new_s[bass.ds(layer, 1), :, :].rearrange("l p n -> (l p) n"),
                                      SOUT.rearrange("p d n -> p (d n)")).then_inc(state_written, 16)
                    do(eng.activation(BTM, ps[:, 2, :], ACT.Copy), tm_ready)
                    do(eng.activation(KTM, ps[:, 3, :], ACT.Copy), tm_ready)
                    more = n + 1 < len(SCANS)
                    if more:
                        decays(n + 1)
                    for lv in range(1, LEVELS):
                        for g in range(2):
                            eng.wait_ge(y_filled, 2 * LEVELS * n + 2 * lv + g + 1)
                            do(eng.activation(YS[:, g, :], ps[:, g, :], ACT.Copy), y_ready)
                        if more and lv == 1:
                            rates(n + 1)
                        if more and lv == 2:
                            exponentials(n + 1)
                        if not more and 2 <= lv < 2 + QT:
                            eng.wait_ge(bonus_summed, lv - 1)
                            do(eng.activation(CV[:, 4 + lv - 2, 0:T], ps[:, 3, 0:T], ACT.Copy), outgate_ready)
                    eng.wait_ge(r_filled, n + 1)
                    for hh, b in enumerate((2, 0)):
                        do(eng.activation(RSB.rearrange("p (j h i) -> p j h i", j=QT, h=2)[:, :, hh, :],
                                          ps[:, b, 0:QT * HD].rearrange("p (j i) -> p j i", j=QT), ACT.Copy), r_ready)
                    eng.wait_ge(u_filled, n + 1)
                    do(eng.activation(USB, ps[:, 3, :], ACT.Copy, scale=-1.0), u_ready)
                eng.wait_ge(state_written, 16)
                eng.wait_ge(state_ready, len(SCANS))
                round_hi(eng, do, S_MERGE)
                for j in range(QT):
                    eng.wait_ge(gn_ready, 1 + j)
                    do(eng.activation(E_SQ[:, j, :], E_B[:, j, :], ACT.Square), gn_squared)
                    if j:
                        group_root(j - 1)
                group_root(QT - 1)
                eng.wait_ge(orwkv_ready, QT)
                round_hi(eng, do, S_MERGE + 1)
                for n in range(KD):
                    for b in range(3):
                        eng.wait_ge(g_filled, 3 * n + b + 1)
                        if n >= 2:
                            eng.wait_ge(mg_ready, n - 1)
                        do(eng.activation(GT[:, n % 2, b, :], ps[:, b, 0:T], ACT.Sigmoid), g_ready)
                    round_hi(eng, do, S_MERGE + n + 2)
                for n in range(KD):
                    if n in (0, 2):
                        round_hi(eng, do, S_OUT + 2 + n // 2)
                    eng.wait_ge(wo_drained, 2 * n + 2)
                    do(eng.activation(R_SQ8[:, n, :], X[:, n, :], ACT.Square), sq2_ready)
                root_of(sq2_summed, root2_ready, R_RS1)
                hi_of(H2, h2_scaled, h2_hi)
                def hi_part(i, s, part, used, count):
                    e = i * SLOTS + s
                    if part == 0:
                        eng.wait_ge(slot_filled[s], i * 16 + 16 * (C_EXP // SLOTS + 1))
                    if not (isinstance(e, int) and e < 2):
                        eng.wait_ge(used, e + (count - 2))
                    o = slice(part * D, (part + 1) * D)
                    eng.activation(W_hi[s][:, o], slot[s][:, o], ACT.Copy).then_inc(e_hi, 1)

                def act_expert(i, s, split=True):
                    e, (j, q) = i * SLOTS + s, ((i, 1) if s == 0 else (i + 1, 0))
                    if split:
                        hi_part(j, q, 0, e_gate, 1)
                    if not (isinstance(e, int) and e < 2):
                        eng.wait_ge(e_scaled, e - 1)
                    eng.wait_ge(e_gate, e + 1)
                    eng.activation(SGS[:, s, :], ps[:, 6, 0:T], ACT.Silu).then_inc(e_silu, 1)
                    if split:
                        hi_part(j, q, 1, e_up, 1)
                        hi_part(j, q, 2, e_down, 1)

                eng.wait_ge(parts_used, S_EXP)
                for part in range(3):
                    hi_part(0, 0, part, None, 0)
                eng.wait_ge(lg_filled, 1)
                do(eng.activation(SC, ps[:, 0, 0:NT * N_EXP].rearrange("p (t e) -> p t e", t=NT), ACT.Sigmoid), score_ready)
                act_expert(0, 0)
                eng.wait_ge(ct_ready, 1)
                eng.wait_ge(line_written, 16 * NT)
                eng.dma_start(combine_dram[SHARED:, :], CT[0:N_EXP, :]).then_inc(ct_written, 16)
                act_expert(0, 1)
                with eng.Fori(1, ROUNDS - 1) as i:
                    for s in range(SLOTS):
                        act_expert(i, s)
                for s in range(SLOTS):
                    act_expert(ROUNDS - 1, s, split=(s == 0))
                layer_end(eng, "act", layer)

        @block.vector
        def _(eng):
            eng.wait_ge(const_landed, 32)
            with eng.Fori(0, depth) as layer:
                do = InOrder(eng, dve_step)

                def over_rms(root, RS):
                    eng.wait_ge(root, 1)
                    do(eng.reciprocal(RS, RS))

                over_rms(root_ready, RS1)
                do(eng.tensor_tensor(H1, X[:, :, :], RS1[:, None, :].to_broadcast([P, KD, T]), ALU.mult))
                eng.wait_ge(par_landed, 48)
                eng.wait_ge(mod_filled, 1)
                def add_mod_b(a, b, bank, col, s=None):
                    do(eng.tensor_tensor(mod[:, a:b, :], ps[:, bank, col:col + 2 * (b - a)].rearrange("p (m g) -> p m g", g=2),
                                         v_("mod_b", a, b - a)[:, :, None].to_broadcast([P, b - a, 2]), ALU.add), s)

                def more_mod(q):
                    eng.wait_ge(modb_filled, q + 1)
                    add_mod_b(3 * (MOD_A + q), 3 * (MOD_A + q + 1), 2, 3 * P, modb_ready)

                def amplitude(i, g, m):
                    do(eng.tensor_scalar(amp[:, i, :, :], mod[:, m * KD:(m + 1) * KD, :], 1.0, None, ALU.add))
                    do(eng.tensor_tensor(amp[:, i, :, :], amp[:, i, :, :],
                                         v_(g, 0, KD)[:, :, None].to_broadcast([P, KD, 2]), ALU.mult))

                add_mod_b(0, 3 * MOD_A, 0, 0)
                amplitude(0, "g1", 1)

                def modulated(i, shift, H, scaled, k):
                    for g, (a, b) in enumerate(GROUPS):
                        do(eng.tensor_scalar(H[:, k, a:b], H[:, k, a:b], amp[:, i, k, g:g + 1],
                                             mod[:, shift * KD + k, g:g + 1], ALU.mult, ALU.add), scaled if g else None)

                def lo_of(H, h_hi, ready, k):
                    eng.wait_ge(h_hi, k + 1)
                    do(eng.tensor_tensor(H_lo[:, k, :], H[:, k, :], H_hi[:, k, :].bitcast(F32), ALU.subtract), ready)

                take_lo(eng, do, 0)
                for k in range(KD + 1):
                    if k < KD:
                        modulated(0, 0, H1, h_scaled, k)
                    if k:
                        lo_of(H1, h_hi, h_ready, k - 1)
                take_lo(eng, do, 1)
                def out_of(n, dst, src):
                    eng.wait_ge(z_filled, n + 1)
                    do(eng.tensor_copy(dst, src), z_dve)

                for c in range(10):
                    for n in Z_OF[c]:
                        bank = ps[:, n % 4, :]
                        if n < 5:
                            out_of(n, QK[:, n, :], bank[:, 0:T])
                        elif n == 5:
                            out_of(n, VT, bank[:, 0:T].rearrange("p (t n) -> p t n", t=NT))
                        elif n < 10:
                            out_of(n, SU[:, n - 6, :], bank[:, 0:T])
                        elif n < 13:
                            out_of(n, SV[:, n - 10, 0:256], bank[:, 0:256])
                        elif n < 16:
                            out_of(n, SV[:, n - 13, 256:512], bank[:, 0:256])
                        elif n not in Z_ACT:
                            if n == 17:
                                eng.wait_ge(raw_zeroed, 3)
                            eng.wait_ge(z_filled, n + 1)
                            do(eng.tensor_copy(RAW[:, n - 17, 1:1 + CTX], bank[:, 0:CTX]))
                            do(eng.tensor_copy(RAW[:, n - 17, 2 + CTX:2 + T], bank[:, CTX:T]), z_dve)
                    if c + 2 < 10:
                        take_lo(eng, do, c + 2)
                    if 5 <= c:
                        eng.wait_ge(qroot_ready, 5)
                        do(eng.reciprocal(RS5[:, c - 5, :], RS5[:, c - 5, :]))
                do(eng.scalar_tensor_tensor(QK[:, 0:4, :], QK[:, 0:4, :], v_("qn"), RS5[:, 0:4, :], ALU.mult, ALU.mult))
                do(eng.scalar_tensor_tensor(QK[:, 4, :], QK[:, 4, :], v_("kn"), RS5[:, 4, :], ALU.mult, ALU.mult), qk_normed)
                more_mod(0)
                eng.wait_ge(rot_filled, 5)
                for j in range(5):
                    b, o = 4 + j // 2, (j % 2) * LAT
                    do(eng.tensor_tensor(SQ5[:, j, CTX:T], QK[:, j, CTX:T], cos, ALU.mult))
                    do(eng.tensor_tensor(ROT5[:, j, :], ps[:, b, o:o + LAT], sin, ALU.mult))
                do(eng.tensor_tensor(QK[:, :, CTX:T], SQ5[:, :, CTX:T], ROT5, ALU.add), qk_ready)
                def convolve(j):
                    w = [v_("conv", i * 12 + j) for i in range(3)]
                    o = CV[:, j, 0:CVW - 1]
                    do(eng.tensor_scalar(o, RAW[:, j, 0:385], w[0], None, ALU.mult))
                    do(eng.scalar_tensor_tensor(o, RAW[:, j, 1:386], w[1], o, ALU.mult, ALU.add))
                    do(eng.scalar_tensor_tensor(o, RAW[:, j, 2:387], w[2], o, ALU.mult, ALU.add), cv_ready)

                for u in range(24 + 9):
                    if u % 3 == 1 and u // 3 + 1 < MOD_B:
                        more_mod(u // 3 + 1)
                    if u % 2 == 0 and u < 24:
                        convolve(u // 2)
                    if u in (3, 5, 9):
                        t = (3, 5, 9).index(u)
                        if t == 0:
                            eng.wait_ge(sv_root, 1)
                            do(eng.reciprocal(small[:, 8:11], small[:, 4:7]))
                        do(eng.tensor_scalar(SV[:, t, :], SV[:, t, :], small[:, 8 + t:9 + t], None, ALU.mult), sv_normed)
                    if u < 24:
                        n = P if u % NT == 0 else T
                        eng.wait_ge(s_filled, u + 1)
                        do(eng.tensor_reduce(att_small[:, 0, u:u + 1], ps[:, 4 + u % 3, 0:n], AX, ALU.max))
                        do(eng.tensor_scalar(att_small[:, 1, u:u + 1], att_small[:, 0, u:u + 1], -HD ** -0.5, None,
                                             ALU.mult), s_max)
                    if 1 <= u <= 24:
                        w = u - 1
                        n = P if w % NT == 0 else T
                        eng.wait_ge(p_exp, w + 1)
                        do(eng.reciprocal(att_small[:, 3, w:w + 1], att_small[:, 2, w:w + 1]))
                        do(eng.tensor_scalar(PM[:, w % 3, 0:n], PM[:, w % 3, 0:n], att_small[:, 3, w:w + 1], None,
                                             ALU.mult), p_ready)
                    if u >= 9 and (u - 9) % 6 == 0 and (u - 9) // 6 < 4:
                        j = (u - 9) // 6
                        eng.wait_ge(pv_filled, 6 * j + 6)
                        do(eng.tensor_copy(o_attn[:, j, :], ps[:, j % 2, 0:T]), oattn_ready)
                for g in range(4):
                    eng.wait_ge(sgu_filled, g + 1)
                    do(eng.scalar_tensor_tensor(SGT, ps[:, g % 2, 0:T].rearrange("p (t i) -> p t i", t=NT),
                                                v_("sgu_g", g),
                                                row[:, None, ROW["sgu_b"] + g * P:ROW["sgu_b"] + (g + 1) * P]
                                                .to_broadcast([P, NT, P]), ALU.mult, ALU.add), sgu_drained)
                    do(eng.tensor_tensor(o_sgu[:, g, :], SGT.rearrange("p t i -> p (t i)"), SU[:, g, :], ALU.mult))
                def sum_decays(n):
                    d, AR = SCANS[n][0], AR2[n % 2]
                    for j in range(QT):
                        eng.wait_ge(decay_ready, 4 * n + j + 1)
                        src, dst, one = SG[:, j, :], CUM[:, j, :], ones
                        if d:
                            src, dst, one = src[:, ::-1], dst[:, ::-1], one[:, ::-1]
                        do(eng.tensor_tensor_scan(dst, one, src, 0.0, ALU.mult, ALU.add))
                    last = CUM[:, :, 0:1] if d else CUM[:, :, P - 1:P]
                    do(eng.tensor_scalar(HALF[:, :, None], last, 0.5, None, ALU.mult))
                    do(eng.tensor_tensor(CUM, CUM, HALF[:, :, None].to_broadcast([P, QT, P]), ALU.subtract))
                    do(eng.tensor_tensor(AR[:, :, 0:P], CUM, SG, ALU.subtract), cum_ready)

                def scale_queries(n):
                    a, AR = CV_AT[SCANS[n][1]], AR2[n % 2]
                    eng.wait_ge(rate_ready, 4 * n + 4)
                    eng.wait_ge(exp_ready, n + 1)
                    do(eng.tensor_tensor(AR[:, :, 0:P], KK[:, :, a:a + P], AR[:, :, 0:P], ALU.mult))
                    do(eng.tensor_tensor(AR[:, :, P:2 * P], R_[:, :, a:a + P], AR[:, :, P:2 * P], ALU.mult))
                    do(eng.tensor_tensor(BE, SA, CUM, ALU.mult))
                    do(eng.tensor_tensor(BE, BE, KK[:, :, a:a + P], ALU.mult))

                def scale_keys(n):
                    a = CV_AT[SCANS[n][1]]
                    for j in range(QT):
                        do(eng.tensor_scalar(SA[:, j, :], SA[:, j, :], v_("k_a", j), small[:, 16 + j:17 + j],
                                             ALU.mult, ALU.add))
                    do(eng.tensor_tensor(SA, SA, K_[:, :, a:a + P], ALU.mult))
                    if SCANS[n][1] in [x[1] for x in SCANS[:n]]:
                        do(eng.tensor_tensor(KS[:, :, a:a + P], KS[:, :, a:a + P], SA, ALU.add))
                    else:
                        do(eng.tensor_copy(KS[:, :, a:a + P], SA))
                    do(eng.tensor_tensor(KA, SA, CUM, ALU.mult), keys_ready)

                def centre_state(n):
                    do(eng.tensor_tensor(SH, SL[:, SCANS[n][0], :].rearrange("p (j i) -> p j i", j=QT),
                                         EH2[n % 2][:, :, None].to_broadcast([P, QT, HD]), ALU.mult), sh_ready)

                do(eng.tensor_scalar(small[:, 16:20], v_("k_a", 0, 4), -1.0, 1.0, ALU.mult, ALU.add))
                R_, K_, V_ = CV[:, 0:4, :], CV[:, 4:8, :], CV[:, 8:12, :]
                W1 = CVW - 1
                for j in range(QT):
                    do(eng.tensor_scalar(KK[:, j, 0:W1], K_[:, j, 0:W1], v_("k_k", j), None, ALU.mult))
                do(eng.tensor_tensor(G[:, 0:4, 0:W1], KK[:, :, 0:W1], KK[:, :, 0:W1], ALU.mult), kksq_ready)
                sum_decays(0)
                eng.wait_ge(kk_root, 4)
                do(eng.reciprocal(G[:, 4:8, 0:W1], G[:, 4:8, 0:W1]))
                do(eng.tensor_tensor(KK[:, :, 0:W1], KK[:, :, 0:W1], G[:, 4:8, 0:W1], ALU.mult), kk_ready)
                scale_queries(0)
                scale_keys(0)
                for n, (d, c) in enumerate(SCANS):
                    first = c not in [x[1] for x in SCANS[:n]]
                    more = n + 1 < len(SCANS)
                    mask = con[:, None, CON["causal"] + d * 2 * P:CON["causal"] + (d + 1) * 2 * P].to_broadcast([P, 2, 2 * P])
                    for u in range(8):
                        eng.wait_ge(gram_filled, 8 * n + u + 1)
                        do(eng.tensor_tensor(G[:, u, :].rearrange("p (a t) -> p a t", a=2),
                                             ps[:, 4 + (u + 2) % 4, :].rearrange("p (a t) -> p a t", a=2), mask, ALU.mult), gram_ready)
                    for lv in range(LEVELS):
                        for g in range(2):
                            XG4 = XX[:, 4 * g:4 * g + 4, :, :]
                            k = 2 * LEVELS * n + 2 * lv + g + 1
                            if lv == 0:
                                eng.wait_ge(y_filled, k)
                                eye = ident[:, None, :].to_broadcast([P, 4, P])
                                do(eng.tensor_tensor(XG4[:, :, 0, :], eye, ps[:, g, :].rearrange("p (u t) -> p u t", u=4), ALU.subtract))
                                do(eng.tensor_tensor(XG4[:, :, 1, :], eye, BL[:, g, :].rearrange("p (u t) -> p u t", u=4),
                                                     ALU.subtract), inv_ready)
                            elif lv < LEVELS - 1:
                                eng.wait_ge(xy_filled, 2 * (LEVELS - 1) * n + 2 * (lv - 1) + g + 1)
                                do(eng.tensor_tensor(XG4, XG4, ps[:, 4 + 2 * g:6 + 2 * g, :].rearrange(
                                    "p a (u x t) -> p (a u) x t", u=2, x=2), ALU.subtract), inv_ready)
                            else:
                                eng.wait_ge(xy_filled, 2 * (LEVELS - 1) * n + 2 * (lv - 1) + g + 1)
                                do(eng.tensor_tensor(XG4[:, :, 1, :], XG4[:, :, 1, :], ps[:, 4 + 2 * g, :].rearrange(
                                    "p (u t) -> p u t", u=4), ALU.subtract), inv_ready)
                        if more and 1 <= lv <= 3:
                            (sum_decays, scale_queries, scale_keys)[lv - 1](n + 1)
                        if not more and lv == 1:
                            for j in range(QT):
                                for (a, b), o in zip(GROUPS, (0, 129)):
                                    do(eng.scalar_tensor_tensor(K_[:, j, a:b], R_[:, j, o:o + b - a], v_("r_k", j),
                                                                KS[:, j, o:o + b - a], ALU.mult, ALU.mult), bonus_ready)
                        if not more and 2 <= lv < 2 + QT:
                            j = lv - 2
                            eng.wait_ge(bonus_summed, j + 1)
                            for (a, b), o in zip(GROUPS, (0, 129)):
                                do(eng.tensor_tensor(V_[:, j, o:o + b - a], ps[:, 2, a:b], V_[:, j, o:o + b - a],
                                                     ALU.mult), bonus_done)
                    eng.wait_ge(os_filled, n + 1)
                    O_ = o_rwkv[:, :, c * P:(c + 1) * P]
                    src = ps[:, 4, :].rearrange("p (j t) -> p j t", j=QT)
                    do(eng.tensor_copy(O_, src)) if first else do(eng.tensor_tensor(O_, O_, src, ALU.add))
                    to = (SOUT if c == 0 else SL)[:, d, :].rearrange("p (j i) -> p j i", j=QT)
                    src = ps[:, 5, 0:QT * HD].rearrange("p (j i) -> p j i", j=QT)
                    if c:
                        do(eng.tensor_tensor(SH, SH, src, ALU.add))
                        src = SH
                    do(eng.tensor_tensor(to, src, EH2[n % 2][:, :, None].to_broadcast([P, QT, HD]), ALU.mult), state_ready)
                    if more and SCANS[n + 1][1]:
                        centre_state(n + 1)
                for j in range(QT):
                    eng.wait_ge(gn_summed, j + 1)
                    do(eng.scalar_tensor_tensor(E_B[:, j, :], ps[:, j, 0:T], -1.0 / HD, o_rwkv[:, j, :], ALU.mult,
                                                ALU.add), gn_ready)
                take_lo(eng, do, S_MERGE)
                for j in range(QT):
                    eng.wait_ge(gn_root, j + 1)
                    do(eng.reciprocal(E_RS[:, j, :], E_RS[:, j, :]))
                    do(eng.scalar_tensor_tensor(E_B[:, j, :], E_B[:, j, :], v_("ln_g", j), E_RS[:, j, :], ALU.mult, ALU.mult))
                    for (a, b), o in zip(GROUPS, (0, 129)):
                        do(eng.scalar_tensor_tensor(E_B[:, j, a:b], E_B[:, j, a:b], v_("ln_b", j),
                                                    V_[:, j, o:o + b - a], ALU.add, ALU.add))
                    eng.wait_ge(outgate_ready, j + 1)
                    do(eng.tensor_tensor(o_rwkv[:, j, :], E_B[:, j, :], K_[:, j, 0:T], ALU.mult), orwkv_ready)
                take_lo(eng, do, S_MERGE + 1)
                for n in range(KD):
                    eng.wait_ge(g_ready, 3 * n + 3)
                    for b in range(3):
                        eng.wait_ge(pr_filled, 3 * n + b + 1)
                        do(eng.tensor_tensor(MT[:, b, :], ps[:, 3 + b, 0:T], GT[:, n % 2, b, :], ALU.mult))
                    do(eng.tensor_tensor(MT[:, 0, :], MT[:, 0, :], MT[:, 1, :], ALU.add))
                    do(eng.tensor_tensor(MT[:, 0, :], MT[:, 0, :], MT[:, 2, :], ALU.add))
                    do(eng.tensor_copy(MG_hi[:, n, :], MT[:, 0, :]))
                    do(eng.tensor_tensor(MG_lo[:, n, :], MT[:, 0, :], MG_hi[:, n, :].bitcast(F32), ALU.subtract), mg_ready)
                    take_lo(eng, do, S_MERGE + n + 2)
                amplitude(1, "g2n", 4)

                def residual(n, gate, src, s):
                    for g, (a, b) in enumerate(GROUPS):
                        do(eng.scalar_tensor_tensor(X[:, n, a:b], src[:, a:b], mod[:, gate * KD + n, g:g + 1],
                                                    X[:, n, a:b], ALU.mult, ALU.add), s)

                for n in range(KD):
                    eng.wait_ge(wo_filled, n + 1)
                    residual(n, 2, ps[:, 6 + n % 2, :], wo_drained)
                    if n % 2 and n < 4:
                        take_lo(eng, do, S_OUT + 2 + n // 2)
                over_rms(root2_ready, R_RS1)
                for k in range(KD):
                    do(eng.tensor_tensor(H2[:, k, :], X[:, k, :], R_RS1, ALU.mult))
                    modulated(1, 3, H2, h2_scaled, k)
                for k in range(KD):
                    lo_of(H2, h2_hi, h2_ready, k)
                def lo_part(i, s, part):
                    o = slice(part * D, (part + 1) * D)
                    eng.wait_ge(e_hi, (i * SLOTS + s) * 3 + part + 1)
                    eng.tensor_tensor(W_lo[s][:, o], slot[s][:, o], W_hi[s][:, o].bitcast(F32), ALU.subtract)\
                       .then_inc(slot_taken[s] if part == 2 else e_lo, 1)

                def dve_expert(i, s, split=True):
                    e, (j, q) = i * SLOTS + s, ((i, 1) if s == 0 else (i + 1, 0))
                    if split:
                        lo_part(j, q, 0)
                    eng.wait_ge(row_landed[s], layer * (16 * ROUNDS) + i * 16 + 16)
                    eng.wait_ge(e_silu, e + 1)
                    eng.tensor_tensor(TS[:, s, :], SGS[:, s, :], CBC[:, s, :], ALU.mult).then_inc(e_scaled, 1)
                    if split:
                        lo_part(j, q, 1)
                    eng.wait_ge(e_scaled, e + 1)
                    eng.wait_ge(e_up, e + 1)
                    eng.tensor_tensor(TS[:, s, :], TS[:, s, :], ps[:, 7, 0:T], ALU.mult).then_inc(e_prod, 1)
                    if not (isinstance(e, int) and e < 2):
                        eng.wait_ge(e_down, e - 1)
                    eng.wait_ge(e_prod, e + 1)
                    eng.tensor_copy(HID_hi[:, s, :], TS[:, s, :]).then_inc(e_hid_hi, 1)
                    eng.wait_ge(e_hid_hi, e + 1)
                    eng.tensor_tensor(HID_lo[:, s, :], TS[:, s, :], HID_hi[:, s, :].bitcast(F32), ALU.subtract)\
                       .then_inc(e_hid, 1)
                    if split:
                        lo_part(j, q, 2)

                for part in range(3):
                    lo_part(0, 0, part)
                eng.wait_ge(score_ready, 1)
                do(eng.tensor_tensor(BI, SC, row[:, None, ROW["router_b"]:ROW["router_b"] + N_EXP]
                                     .to_broadcast([P, NT, N_EXP]), ALU.add))
                for t in range(NT):
                    do(eng.max(TOPV[:, t, :], BI[:, t, :]))
                    do(eng.max_index(topi[:, t, :], TOPV[:, t, :], BI[:, t, :]))
                do(eng.tensor_copy(TOPF, topi[:, :, :]))
                for t in range(NT):
                    do(eng.tensor_tensor(EQ, c_("iota", N_EXP)[:, None, :].to_broadcast([P, TOP_K, N_EXP]),
                                         TOPF[:, t, 0:TOP_K, None].to_broadcast([P, TOP_K, N_EXP]), ALU.is_equal))
                    do(eng.tensor_reduce(CB[:, t, :], EQ.rearrange("p k e -> p e k"), AX, ALU.add))
                do(eng.tensor_tensor(CB, CB, SC, ALU.mult))
                do(eng.tensor_reduce(small[:, 24:27], CB, AX, ALU.add))
                do(eng.reciprocal(small[:, 28:31], small[:, 24:27]))
                for t in range(NT):
                    do(eng.tensor_scalar(CB[:, t, :], CB[:, t, :], small[:, 28 + t:29 + t], ROUTED_SCALE,
                                         ALU.mult, ALU.mult), comb_ready)
                eng.wait_ge(ct_filled, 1)
                do(eng.tensor_copy(CT[0:N_EXP, :], ps[0:N_EXP, 1, 0:T]), ct_ready)
                for s in range(SLOTS):
                    dve_expert(0, s)
                with eng.Fori(1, ROUNDS - 1) as i:
                    for s in range(SLOTS):
                        dve_expert(i, s)
                for s in range(SLOTS):
                    dve_expert(ROUNDS - 1, s, split=(s == 0))
                eng.wait_ge(acc_filled, 1)
                for t in range(NT):
                    do(eng.tensor_copy(RO[:, t, :], ps[:, 2 * t:2 * t + 2, :].rearrange("p a b -> p (a b)")), ro_ready)
                for n in range(KD):
                    eng.wait_ge(back_filled, n + 1)
                    residual(n, 5, ps[:, 6 + n % 2, :], x_ready)
                layer_end(eng, "dve", layer)

        @block.tensor
        def _(eng):
            eng.wait_ge(const_landed, 32)
            eng.wait_ge(csil_ready, 1)
            with eng.Fori(0, depth) as layer:
                owed = []

                def release(n):
                    owed.append(parts_used)

                def matmul(*args, **kw):
                    mm = eng.matmul(*args, **kw)
                    if owed:
                        mm.then_inc(owed.pop(0), 1)
                    return mm

                def keep_clock(bank, n):
                    for _ in range(n):
                        eng.matmul(ps[:, bank, 0:P], ident, ones, start=True, stop=True)

                def parts(m):
                    n = raw_of(m)
                    eng.wait_ge(slot_taken[n % SLOTS], n // SLOTS + 1)
                    return tuple(w[m % 2][:, :].rearrange("p (k n) -> p k n", k=KD) for w in (W_hi, W_lo))

                def product(out, w, act, k_n=KD, swap=False, ready=None):
                    n = 0
                    for k in range(k_n):
                        if ready is not None:
                            eng.wait_ge(ready, k + 1)
                        for a_, b_ in ((1, 0), (0, 1), (0, 0)):
                            x, y = w[a_](k), act[b_](k)
                            mm = matmul(out, *((y, x) if swap else (x, y)), start=(n == 0), stop=(n == 3 * k_n - 1))
                            n += 1
                    return mm

                def mod_chunk(c, bank, k0=0, k1=KD):
                    n = C_MOD + c if c < MOD_A else C_MODB + c - MOD_A
                    w = landed(eng, n).rearrange("p (k n) -> p k n", k=KD)
                    for k in range(k0, k1):
                        mm = matmul(ps[0:2, bank, 0:3 * P], csil[:, k, :], w[:, k, :], start=(k == 0), stop=(k == KD - 1))
                    if k1 == KD:
                        mm.then_inc(mod_row_filled, 1)
                        if c < MOD_A:
                            owed.append(slot_taken[n % SLOTS])

                def mod_turn(c, bank, col):
                    eng.wait_ge(mod_row_ready, c + 1)
                    for m in range(3):
                        mm = matmul(ps[:, bank, col + 2 * m:col + 2 * m + 2], mod_row[:, c % 2, m * P:(m + 1) * P],
                                    ident[0:2, 0:2], start=True, stop=True)
                        if m == 0 and c >= MOD_A:
                            mm.then_inc(slot_taken[(C_MODB + c - MOD_A) % SLOTS], 1)
                    return mm

                eng.wait_ge(sq_ready, 1)
                for k in range(KD):
                    mm = matmul(ps[:, 1, 0:T], ones, SQ8[:, k, :], start=(k == 0), stop=(k == KD - 1))
                mm.then_inc(sq_summed, 1)
                for c in range(MOD_A):
                    mod_chunk(c, 2 + c % 2)
                    if c:
                        mod_turn(c - 1, 0, 6 * (c - 1))
                mod_turn(MOD_A - 1, 0, 6 * (MOD_A - 1)).then_inc(mod_filled, 1)

                def z_bank(n):
                    m = n - 4
                    if m in Z_ACT:
                        eng.wait_ge(z_act, Z_ACT.index(m) + 1)
                    elif m >= 0:
                        eng.wait_ge(z_dve, len([x for x in range(m + 1) if x not in Z_ACT]))
                    return n % 4

                def columns(w, col, width=P):
                    return tuple(lambda k, x=x: x[:, k, col:col + width] for x in w)

                def tokens(a_, b_):
                    return tuple(lambda k, x=x: x[:, k, a_:b_] for x in (H_hi, H_lo))

                def z_tile(n, w, col):
                    product(ps[:, z_bank(n), 0:T], columns(w, col), tokens(0, T), ready=None if n else h_ready)\
                        .then_inc(z_filled, 1)

                def z_tokens(b, at_, t, w, col, width):
                    return product(ps[:, b, at_:at_ + width], columns(w, col, width), tokens(t * P, (t + 1) * P), swap=True)

                for c in range(10):
                    w = parts(S_IN + c)
                    if c == 1:
                        z_tile(3, w, 0)
                        z_tile(4, w, P)
                        b = z_bank(5)
                        for t in range(NT):
                            mm = z_tokens(b, t * P, t, w, 2 * P, P)
                        mm.then_inc(z_filled, 1)
                    elif c == 3:
                        z_tile(9, w, 0)
                        for t in range(NT):
                            z_tokens(z_bank(10 + t), 0, t, w, P, 2 * P).then_inc(z_filled, 1)
                    elif c == 4:
                        for t in range(NT):
                            z_tokens(z_bank(13 + t), 0, t, w, 0, 2 * P).then_inc(z_filled, 1)
                        z_tile(16, w, 2 * P)
                    else:
                        for m, n in enumerate(Z_OF[c]):
                            z_tile(n, w, m * P)
                    release(S_IN + c)
                    if c == 3:
                        eng.drain().then_inc(owed.pop(0), 1)
                        eng.wait_ge(qsq_ready, 1)
                        for j in range(5):
                            if j == 4:
                                eng.wait_ge(qroot_ready, 1)
                            matmul(ps[:, 4 + j % 4, 0:T], heads, SQ5[:, j, :], start=True, stop=True).then_inc(qsq_summed, 1)
                eng.drain().then_inc(owed.pop(0), 1)
                eng.wait_ge(z_act, 3)
                eng.wait_ge(z_dve, 28)
                mod_chunk(MOD_A, 2)
                eng.wait_ge(qk_normed, 1)
                eng.transpose(ps[:, 7, 0:P], QK[:, 4, 0:CTX], ident).then_inc(kout_filled, 1)
                for j in range(5):
                    matmul(ps[:, 4 + j // 2, (j % 2) * LAT:(j % 2 + 1) * LAT], rot, QK[:, j, CTX:T],
                               start=True, stop=True).then_inc(rot_filled, 1)
                mod_turn(MOD_A, 2, 3 * P).then_inc(modb_filled, 1)
                eng.wait_ge(modb_ready, 1)
                mod_chunk(MOD_A + 1, 2)
                eng.wait_ge(qk_ready, 1)
                eng.wait_ge(kout_ready, 1)
                units = [(j, hh, t) for j in range(QT) for hh in range(2) for t in range(NT)]

                def scores(u):
                    j, hh, t = units[u]
                    r = slice(hh * HD, (hh + 1) * HD)
                    if u >= 3:
                        eng.wait_ge(p_exp, u - 2)
                    q = QK[r, j, t * P:(t + 1) * P]
                    b = 4 + u % 3
                    if t == 0:
                        mm = matmul(ps[:, b, 0:P], q, QK[r, 4, 0:CTX], start=True, stop=True)
                    else:
                        matmul(ps[:, b, 0:P], q, m_("ctx_kT", P)[r, :], start=True, stop=True)
                        mm = matmul(ps[:, b, P:T], q, QK[r, 4, CTX:T], start=True, stop=True)
                    mm.then_inc(s_filled, 1)

                def turn(u):
                    t = units[u][2]
                    eng.wait_ge(p_ready, u + 1)
                    if u >= 2:
                        eng.wait_ge(pt_ready, u - 1)
                    for kb in range(1 if t == 0 else NT):
                        mm = eng.transpose(ps[:, (7, 3)[u % 2], kb * P:(kb + 1) * P], PM[:, u % 3, kb * P:(kb + 1) * P], ident)
                    mm.then_inc(pt_filled, 1)

                def values(u):
                    j, hh, t = units[u]
                    r = slice(hh * HD, (hh + 1) * HD)
                    eng.wait_ge(pt_ready, u + 1)
                    if j >= 2 and hh == 0 and t == 0:
                        eng.wait_ge(oattn_ready, j - 1)
                    v = [VT[:, 0, r]] if t == 0 else [m_("ctx_v", P)[:, r], VT[:, 1, r], VT[:, 2, r]]
                    for kb, vb in enumerate(v):
                        mm = matmul(ps[r, j % 2, t * P:(t + 1) * P], vb, PTS[:, u % 2, kb * P:(kb + 1) * P],
                                        start=(kb == 0), stop=(kb == len(v) - 1))
                    mm.then_inc(pv_filled, 1)

                for u in range(24 + 3):
                    if u < 24:
                        scores(u)
                    if 2 <= u < 26:
                        turn(u - 2)
                    if u >= 3:
                        values(u - 3)
                    q = u // 3 + 2
                    if u % 3 == 0 and q <= MOD_B:
                        mod_turn(MOD_A + q - 1, 2, 3 * P).then_inc(modb_filled, 1)
                    elif u % 3 and q < MOD_B:
                        if u % 3 == 1:
                            eng.wait_ge(modb_ready, q)
                        mod_chunk(MOD_A + q, 2, (u % 3 - 1) * QT, u % 3 * QT)
                eng.wait_ge(sv_normed, NT)
                eng.wait_ge(oattn_ready, 4)
                eng.wait_ge(cv_ready, 12)
                for g in range(4):
                    if g >= 2:
                        eng.wait_ge(sgu_drained, g - 1)
                    for t in range(NT):
                        mm = matmul(ps[:, g % 2, t * P:(t + 1) * P], SV[:, t, g * P:(g + 1) * P],
                                        m_("sgu_ws")[:, g * P:(g + 1) * P], start=True, stop=True)
                    mm.then_inc(sgu_filled, 1)
                eng.wait_ge(sgu_drained, 4)
                eng.wait_ge(kksq_ready, 1)
                for j in range(QT):
                    matmul(ps[:, 4 + j, 0:CVW - 1], heads, G[:, j, 0:CVW - 1], start=True, stop=True).then_inc(kk_summed, 1)
                half = [slice(0, HD), slice(HD, P)]

                def decay_and_rate(n):
                    d, c = SCANS[n]
                    for x, b, name in ((XW, 2, "w2"), (XA, 3, "a2")):
                        for j in range(QT):
                            mm = matmul(ps[:, b, j * P:(j + 1) * P], m_(name)[half[d], j * P:(j + 1) * P],
                                        x[half[d], c * P:(c + 1) * P], start=True, stop=True)
                    mm.then_inc(wa_filled, 1)

                decay_and_rate(0)
                for c in range(NT):
                    if c == 2:
                        eng.wait_ge(kk_root, 1)
                    for j in range(QT):
                        mm = eng.transpose(ps[:, (0, 1, 4)[c], j * P:(j + 1) * P], CV[:, 8 + j, CV_AT[c]:CV_AT[c] + P], ident)
                    mm.then_inc(vtm_filled, 1)
                eng.wait_ge(kk_root, QT)
                keep_clock(7, 105)
                eng.wait_ge(vtm_ready, NT)
                for n, (d, c) in enumerate(SCANS):
                    more = n + 1 < len(SCANS)
                    AR = AR2[n % 2]
                    if n == 0:
                        eng.wait_ge(rate_ready, 4)
                    eng.wait_ge(keys_ready, n + 1)
                    for b, src in ((2, BE), (3, KA)):
                        for j in range(QT):
                            mm = eng.transpose(ps[:, b, j * P:(j + 1) * P], src[:, j, :], ident)
                    mm.then_inc(tm_filled, 1)
                    for u in range(8):
                        j, hh = u // 2, half[u % 2]
                        if u == 0:
                            eng.wait_ge(kk_ready, 1)
                        if u == 2 and n:
                            eng.wait_ge(state_ready, n)
                        if u >= 4:
                            eng.wait_ge(gram_ready, 8 * n + u - 3)
                        matmul(ps[:, 4 + (u + 2) % 4, 0:2 * P], BE[hh, j, :], AR[hh, j, :], start=True, stop=True)
                        matmul(ps[:, 4 + (u + 2) % 4, 2 * P:4 * P], KA[hh, j, :], AR[hh, j, :], start=True,
                                   stop=True).then_inc(gram_filled, 1)
                    for lv in range(LEVELS):
                        for g in range(2):
                            k = 2 * LEVELS * n + 2 * lv + g
                            eng.wait_ge(block_ready, k + 1)
                            if lv >= 1:
                                eng.wait_ge(inv_ready, k - 1)
                            if lv >= 2:
                                eng.wait_ge(y_ready, 2 * (LEVELS - 1) * n + 2 * (lv - 2) + g + 1)
                            for q in range(4):
                                mm = matmul(ps[:, g, q * P:(q + 1) * P], BL[:, g, q * P:(q + 1) * P],
                                                ident if lv == 0 else XX[:, 4 * g + q, 0, :], start=True, stop=True)
                            mm.then_inc(y_filled, 1)
                        if lv == 0 and more:
                            eng.wait_ge(tm_ready, 2 * n + 2)
                            decay_and_rate(n + 1)
                        if not more and 2 <= lv < 2 + QT:
                            j = lv - 2
                            eng.wait_ge(bonus_ready, 2 * j + 2)
                            eng.wait_ge(tm_ready, 2 * n + 2)
                            if j:
                                eng.wait_ge(bonus_done, 2 * j)
                                eng.wait_ge(outgate_ready, j)
                            matmul(ps[:, 3, 0:T], m_("g2")[:, j * P:(j + 1) * P], XG, start=True, stop=True)
                            matmul(ps[:, 2, 0:T], heads, CV[:, 4 + j, 0:T], start=True, stop=True).then_inc(bonus_summed, 1)
                        for g in range(2):
                            if lv == 0:
                                continue
                            k = 2 * (LEVELS - 1) * n + 2 * (lv - 1) + g
                            eng.wait_ge(y_ready, k + 1)
                            if lv == 1:
                                eng.wait_ge(gram_ready, 8 * n + 8)
                            for q in range(4):
                                u, y = 4 * g + q, YS[:, g, q * P:(q + 1) * P]
                                if lv < LEVELS - 1:
                                    b, o = 4 + 2 * g + q // 2, (q % 2) * 2 * P
                                    matmul(ps[:, b, o:o + P], XX[:, u, 1, :], y, start=True, stop=True)
                                    mm = matmul(ps[:, b, o + P:o + 2 * P], y, XX[:, u, 1, :], start=True, stop=True)
                                else:
                                    mm = matmul(ps[:, 4 + 2 * g, q * P:(q + 1) * P], y, XX[:, u, 1, :], start=True, stop=True)
                            mm.then_inc(xy_filled, 1)
                    eng.wait_ge(tm_ready, 2 * n + 2)
                    if not more:
                        eng.wait_ge(bonus_done, 2 * QT)
                        eng.wait_ge(outgate_ready, QT)
                    eng.wait_ge(y_ready, 2 * (LEVELS - 1) * (n + 1))
                    if c:
                        eng.wait_ge(sh_ready, len([x for x in SCANS[:n + 1] if x[1]]))
                    for u in range(8):
                        j, hh = u // 2, half[u % 2]
                        out = ps[:, (2, 0)[u % 2], j * HD:(j + 1) * HD]
                        vt = VTM[:, c, u * HD:(u + 1) * HD]
                        if c:
                            matmul(out, AR[hh, j, 0:P], SH[hh, j, :], start=True, stop=False)
                        mm = matmul(out, G[:, u, 2 * P:3 * P], vt, start=(c == 0), stop=True)
                    mm.then_inc(r_filled, 1)
                    keep_clock(7, 5)
                    eng.wait_ge(r_ready, 2 * n + 2)
                    eng.wait_ge(inv_ready, 2 * LEVELS * (n + 1))
                    for u in range(8):
                        o = slice(u * HD, (u + 1) * HD)
                        mm = matmul(ps[:, 3, o], XX[:, u, 1, :], RSB[:, o], start=True, stop=True)
                    mm.then_inc(u_filled, 1)
                    keep_clock(7, 4)
                    eng.wait_ge(u_ready, n + 1)
                    for u in range(8):
                        j, hh = u // 2, half[u % 2]
                        o = slice(u * HD, (u + 1) * HD)
                        out = ps[hh, 4, j * P:(j + 1) * P]
                        if c:
                            matmul(out, SH[hh, j, :], AR[hh, j, P:2 * P], start=True, stop=False)
                        matmul(out, USB[:, o], G[:, u, P:2 * P], start=(c == 0), stop=False)
                        matmul(out, VTM[:, c, o], G[:, u, 3 * P:4 * P], start=False, stop=True)
                    for u in range(8):
                        j, hh = u // 2, half[u % 2]
                        o = slice(u * HD, (u + 1) * HD)
                        out = ps[hh, 5, j * HD:(j + 1) * HD]
                        matmul(out, BTM[:, o], USB[:, o], start=True, stop=False)
                        mm = matmul(out, KTM[:, o], VTM[:, c, o], start=False, stop=True)
                    mm.then_inc(os_filled, 1)
                eng.wait_ge(state_ready, len(SCANS))
                for j in range(QT):
                    matmul(ps[:, j, 0:T], heads, o_rwkv[:, j, :], start=True, stop=True).then_inc(gn_summed, 1)
                for j in range(QT):
                    eng.wait_ge(gn_squared, j + 1)
                    matmul(ps[:, 4 + j, 0:T], heads, E_SQ[:, j, :], start=True, stop=True).then_inc(gn_summed, 1)
                for n in range(KD):
                    pair, odd = n // 2, n % 2
                    w = parts(S_MERGE + n)
                    for b in range(3):
                        if n:
                            eng.wait_ge(g_ready, 3 * (n - 1) + b + 1)
                        else:
                            eng.wait_ge(gn_ready, b + 1)
                        product(ps[:, b, 0:T], columns(w, b * P), tokens(0, T)).then_inc(g_filled, 1)
                    release(S_MERGE + n)
                    raw = C_MERGE + 3 * pair + 2
                    w = landed(eng, raw).rearrange("p (b k n) -> p b k n", b=3, k=QT)
                    if n:
                        eng.wait_ge(mg_ready, n)
                    for b, o in enumerate((o_attn, o_sgu, o_rwkv)):
                        if n == 0:
                            eng.wait_ge(*((gn_ready, QT), (gn_root, 1), (orwkv_ready, QT))[b])
                        for k in range(QT):
                            mm = matmul(ps[:, 3 + b, 0:T], w[:, b, k, odd * P:(odd + 1) * P], o[:, k, :],
                                            start=(k == 0), stop=(k == QT - 1))
                        mm.then_inc(pr_filled, 1)
                    if odd:
                        owed.append(slot_taken[raw % SLOTS])
                eng.wait_ge(mg_ready, KD)
                for n in range(KD):
                    w = parts(S_OUT + n // 2)
                    if n >= 2:
                        eng.wait_ge(wo_drained, 2 * (n - 1))
                    product(ps[:, 6 + n % 2, 0:T], columns(w, (n % 2) * P),
                            tuple(lambda k, x=x: x[:, k, :] for x in (MG_hi, MG_lo))).then_inc(wo_filled, 1)
                    if n % 2:
                        release(S_OUT + n // 2)
                    for k in ((n - 2,) if n < KD - 1 else (n - 2, n - 1, n)):
                        if k >= 0:
                            eng.wait_ge(sq2_ready, k + 1)
                            mm = matmul(ps[:, 1, 0:T], ones, R_SQ8[:, k, :], start=(k == 0), stop=(k == KD - 1))
                mm.then_inc(sq2_summed, 1)
                eng.wait_ge(h2_scaled, KD)
                for t in range(NT):
                    for k in range(KD):
                        mm = matmul(ps[:, 0, t * N_EXP:(t + 1) * N_EXP], H2[:, k, t * P:(t + 1) * P],
                                        m_("router")[:, k * N_EXP:(k + 1) * N_EXP], start=(k == 0), stop=(k == KD - 1))
                mm.then_inc(lg_filled, 1)
                eng.wait_ge(h2_ready, KD)

                def half_of(s, bank, part):
                    w = tuple(lambda k, x=x: x[s][:, part * D + k * P:part * D + (k + 1) * P] for x in (W_hi, W_lo))
                    return product(ps[:, bank, 0:T], w, tokens(0, T))

                def down(s, start, stop):
                    for t in range(NT):
                        for h in range(2):
                            o = slice(2 * D + h * 512, 2 * D + (h + 1) * 512)
                            for n, (x, w) in enumerate(((HID_lo, W_hi), (HID_hi, W_lo), (HID_hi, W_hi))):
                                mm = eng.matmul(ps[:, 2 * t + h, :], x[:, s, t * P:(t + 1) * P], w[s][:, o],
                                                start=(start and n == 0), stop=(stop and n == 2), skip_group_check=True)
                    return mm

                def pe_expert(i, s, start=False):
                    e, (j, q) = i * SLOTS + s, ((i, 0) if s == 1 else (i - 1, 1))
                    first = isinstance(e, int) and e == 0
                    eng.wait_ge(e_lo, e * 2 + 1)
                    if not first:
                        eng.wait_ge(e_silu, e)
                    half_of(s, 6, 0).then_inc(e_gate, 1)
                    eng.wait_ge(e_lo, e * 2 + 2)
                    if not first:
                        eng.wait_ge(e_prod, e)
                    half_of(s, 7, 1).then_inc(e_up, 1)
                    if not first:
                        eng.wait_ge(e_hid, e)
                        eng.wait_ge(slot_taken[q], j + (C_EXP // SLOTS + 1))
                        down(q, start, False).then_inc(e_down, 1)

                pe_expert(0, 0)
                eng.wait_ge(comb_ready, NT)
                for t in range(NT):
                    mm = eng.transpose(ps[0:N_EXP, 1, t * P:(t + 1) * P], CB[:, t, :], ident)
                mm.then_inc(ct_filled, 1)
                eng.wait_ge(ct_ready, 1)
                pe_expert(0, 1, start=True)
                with eng.Fori(1, ROUNDS) as i:
                    for s in range(SLOTS):
                        pe_expert(i, s)
                eng.wait_ge(e_hid, N_EXP + SHARED)
                eng.wait_ge(slot_taken[1], C_EXP // SLOTS + ROUNDS)
                down(1, False, True).then_inc(acc_filled, 1)
                eng.wait_ge(ro_ready, NT)
                for n in range(KD):
                    if n >= 2:
                        eng.wait_ge(x_ready, 2 * (n - 1))
                    for t in range(NT):
                        mm = eng.transpose(ps[:, 6 + n % 2, t * P:(t + 1) * P], RO[:, t, n * P:(n + 1) * P], ident)
                    mm.then_inc(back_filled, 1)
                layer_end(eng, "pe", layer)


def constants():
    out = np.zeros((P, N_CON), np.float32)

    def put(name, a, off=0):
        out[:, CON[name] + off:CON[name] + off + a.shape[1]] = a

    i = np.arange(P)
    put("ident", np.eye(P))
    put("heads", (i[:, None] // HD == i[None] // HD))
    put("ones", np.ones((P, P)))
    f = HD // 4
    part, low = (i // f) % 2, i % f
    rot = np.zeros((P, P))
    for m in range(P):
        rot[m + f if part[m] == 0 else m - f, m] = -1.0 if part[m] == 0 else 1.0
    put("rot", rot)
    t = np.arange(LAT)
    inv = (10000.0 ** (-np.arange(f, dtype=np.float32) / f)).astype(np.float32)
    pos = np.stack([(t // 64), (t % 64)]).astype(np.float32)
    axis = (i // (2 * f)) % 2
    ang = (pos[axis] * inv[low][:, None]).astype(np.float32)
    put("cos", np.cos(ang))
    put("sin", np.sin(ang))
    s_, t_ = i[:, None], i[None]
    for d in range(2):
        strict = (s_ < t_) if d == 0 else (s_ > t_)
        put("causal", strict, d * 2 * P)
        put("causal", strict | (s_ == t_), d * 2 * P + P)
        for lv in range(LEVELS):
            b = 1 << lv
            put("level", strict & (s_ // (2 * b) == t_ // (2 * b)) & (s_ // b != t_ // b), (d * LEVELS + lv) * P)
    put("iota", np.broadcast_to(np.arange(N_EXP), (P, N_EXP)))
    return out


def lay_out(a):
    L = a["w_in"].shape[0]
    a = {k: np.asarray(v) for k, v in a.items()}
    xT = np.concatenate([a["x_prompt"].reshape(CTX, D), a["x_sample"].reshape(LAT, D)]).T
    W = np.zeros((L, N_CHUNKS, P, SLOT_W), np.float32)

    def by_k(w, tiles):
        return w.reshape(-1, P, w.shape[-1]).transpose(1, 0, 2)

    for l in range(L):
        for n in range(16):
            W[l, C_MOD + n if n < MOD_A else C_MODB + n - MOD_A] = by_k(a["mod_w"][l][:, n * 384:(n + 1) * 384], 3).reshape(P, -1)
        w = a["w_in"][l]
        q, k, v, su, sv, rkv, xw, xa, xg, gates = np.split(
            w, np.cumsum([512, 128, 128, 512, 512, 1536, 128, 128, 128]), axis=1)
        q = q.reshape(D, 2, 4, HD).transpose(0, 2, 1, 3).reshape(D, 512)
        seq = np.concatenate([q, k, v, su, sv, xg, rkv, xw, xa, np.zeros((D, P), np.float32)], axis=1)
        for n in range(10):
            W[l, C_IN + n] = by_k(seq[:, n * 384:(n + 1) * 384], 3).reshape(P, -1)
        gates = gates.reshape(D, 3, D)
        pa = a["proj_attn"][l].reshape(2, 4, HD, D).transpose(1, 0, 2, 3).reshape(512, D)
        pr = np.stack([pa, a["proj_sgu"][l], a["proj_rwkv"][l]])
        for pair in range(4):
            for odd in range(2):
                n = 2 * pair + odd
                W[l, C_MERGE + 3 * pair + odd] = by_k(gates[:, :, n * P:(n + 1) * P].reshape(D, 384), 3).reshape(P, -1)
            cols = pr[:, :, 2 * pair * P:2 * (pair + 1) * P].reshape(3, 4, P, 2 * P).transpose(2, 0, 1, 3)
            W[l, C_MERGE + 3 * pair + 2] = cols.reshape(P, -1)
            W[l, C_OUT + pair].reshape(P, KD, 3 * P)[:, :, 0:2 * P] = by_k(
                a["w_out"][l][:, 2 * pair * P:2 * (pair + 1) * P], 2)
        E = W[l, C_EXP:].reshape(N_EXP + SHARED, P, 3, KD * P)
        for part, name, sh in ((0, "exp_gate", "sh_gate"), (1, "exp_up", "sh_up")):
            E[SHARED:, :, part] = a[name][l].reshape(N_EXP, KD, P, P).transpose(0, 2, 1, 3).reshape(N_EXP, P, KD * P)
            E[:SHARED, :, part] = a[sh][l].reshape(KD, P, SHARED, P).transpose(2, 1, 0, 3).reshape(SHARED, P, KD * P)
        E[SHARED:, :, 2] = a["exp_down"][l]
        E[:SHARED, :, 2] = a["sh_down"][l].reshape(SHARED, P, D)

    par = np.zeros((L, P, N_MAT + N_VEC), np.float32)

    def mat(name, x):
        par[:, :, MAT[name]:MAT[name] + x.shape[-1]] = x

    def vec(name, x):
        n = x.shape[1]
        par[:, :, N_MAT + VEC[name]:N_MAT + VEC[name] + n] = x.transpose(0, 2, 1)

    mat("sgu_ws", a["sgu_ws"].transpose(0, 3, 1, 2).reshape(L, P, 512))
    mat("w2", a["rwkv_w2"].reshape(L, P, 512))
    mat("a2", a["rwkv_a2"].reshape(L, P, 512))
    mat("g2", a["rwkv_g2"])
    mat("router", a["router_w"].reshape(L, KD, P, N_EXP).transpose(0, 2, 1, 3).reshape(L, P, KD * N_EXP))
    mat("ctx_kT", a["cache_k"][0].reshape(L, CTX, P).transpose(0, 2, 1))
    mat("ctx_v", a["cache_v"][0].reshape(L, CTX, P))
    s = a["state_wkv"][0].reshape(L, 2, 4, 2, HD, HD)
    mat("state0", s.transpose(0, 3, 5, 1, 2, 4).reshape(L, P, 512))
    vec("g1", a["norm1_g"].reshape(L, KD, P))
    vec("g2n", a["norm2_g"].reshape(L, KD, P))
    vec("mod_b", a["mod_b"].reshape(L, 48, P))
    vec("qn", np.concatenate([a["q_norm"]] * 2, axis=1).reshape(L, 1, P))
    vec("kn", np.concatenate([a["k_norm"]] * 2, axis=1).reshape(L, 1, P))
    vec("sgu_g", a["sgu_norm_g"].reshape(L, 4, P))
    vec("conv", a["rwkv_conv"].reshape(L, 36, P))
    vec("w0", a["rwkv_w0"].reshape(L, 8, P))
    vec("a0", a["rwkv_a0"].reshape(L, 8, P))
    for name, src in (("k_k", "rwkv_k_k"), ("k_a", "rwkv_k_a"), ("r_k", "rwkv_r_k"), ("ln_g", "rwkv_ln_g"), ("ln_b", "rwkv_ln_b")):
        vec(name, a[src].reshape(L, 4, P))
    rows = np.concatenate([a["sgu_bs"].reshape(L, 512), a["router_bias"]], axis=1)
    con = constants()
    cv = np.stack([a["c_ctx"].reshape(KD, P), a["c"].reshape(KD, P)], axis=-1)
    con[:, CON["cvec"]:CON["cvec"] + 2 * KD] = cv.transpose(1, 0, 2).reshape(P, 2 * KD)
    return {"xT": np.ascontiguousarray(xT), "weights": W.reshape(L * N_CHUNKS, P, SLOT_W), "params": par,
            "rows": np.ascontiguousarray(rows), "consts": con}


def kernel(**inputs):
    from concourse import bacc
    from concourse.bass_utils import run_bass_kernel_spmd

    arrays = lay_out(inputs)
    nc = bacc.Bacc("TRN2", target_bir_lowering=False, num_devices=1)
    args = [nc.dram_tensor(n, v.shape, F32, kind="ExternalInput").ap() for n, v in arrays.items()]
    outs = {"yT": (D, T), "new_k": (DEPTH, CTX, P), "new_v": (DEPTH, CTX, P), "new_s": (DEPTH, P, 512)}
    args += [nc.dram_tensor(n, s, F32, kind="ExternalOutput").ap() for n, s in outs.items()]
    program(nc, *args)
    r = run_bass_kernel_spmd(nc, [arrays], core_ids=[0]).results[0]
    y = r["yT"].T
    kv = (1, DEPTH, CTX, 2, HD)
    s = r["new_s"].reshape(DEPTH, 2, HD, 2, 4, HD).transpose(0, 3, 4, 1, 5, 2)
    return (np.ascontiguousarray(y[:CTX]).reshape(1, CTX, D), np.ascontiguousarray(y[CTX:]).reshape(1, LAT, D),
            r["new_k"].reshape(kv), r["new_v"].reshape(kv),
            np.ascontiguousarray(s).reshape(1, DEPTH, 2, 8, HD, HD))
```
